# Optimizing a Trainium2 kernel written in Bass

```python
import jax
import jax.numpy as jnp
from jax import lax
import numpy as np
import jax, jax.numpy as jnp

D_MODEL = 1024
BATCH = 1
SEQ = 1024
DEPTH = 1

HEAD_DIM = 64
N_HEADS = 4
BRANCH_W = N_HEADS * HEAD_DIM
N_BRANCH = 4
Q_BLOCK = 128
CMP_BLOCK = 32
SEL_BLOCK = 64
SEL_TOPK = 16
NSA_WINDOW = 512
SWA_WINDOW = 128
SWA_KV_HEADS = 2
RET_CHUNK = 128
RMS_EPS = 1e-6
LN_EPS = 1e-5
NEG_INF = -1e30
TINY = 1e-30
FORCED_SCORE = 1e4

IN_WIDTHS = (
    BRANCH_W, 6 * HEAD_DIM, 3 * N_HEADS, BRANCH_W,
    BRANCH_W, SWA_KV_HEADS * HEAD_DIM, SWA_KV_HEADS * HEAD_DIM, BRANCH_W,
    BRANCH_W, BRANCH_W, BRANCH_W, BRANCH_W,
    BRANCH_W, BRANCH_W, BRANCH_W, BRANCH_W,
)
IN_W = sum(IN_WIDTHS)
IN_OFFSETS = tuple(int(v) for v in np.cumsum(IN_WIDTHS)[:-1])


def alibi_slopes(n):
    return jnp.asarray(2.0 ** (-8.0 * (np.arange(n) + 1) / n), dtype=jnp.float32)

def rms_norm(x, g):
    xf = x.astype(jnp.float32)
    y = xf * lax.rsqrt(jnp.mean(xf * xf, axis=-1, keepdims=True) + RMS_EPS)
    return (y * g.astype(jnp.float32)).astype(x.dtype)

def masked_softmax(s, mask, sink=None):
    s = jnp.where(mask, s, NEG_INF)
    m = jnp.max(s, axis=-1, keepdims=True)
    if sink is not None:
        m = jnp.maximum(m, sink)
    e = jnp.where(mask, jnp.exp(s - m), 0.0)
    den = jnp.sum(e, axis=-1, keepdims=True)
    if sink is not None:
        den = den + jnp.exp(sink - m)
    return e / jnp.maximum(den, TINY)

def band_windows(k, n_prev):
    B, S = k.shape[:2]
    nblk = S // Q_BLOCK
    pad = [(0, 0), (n_prev * Q_BLOCK, 0)] + [(0, 0)] * (k.ndim - 2)
    kp = jnp.pad(k, pad).reshape(B, nblk + n_prev, Q_BLOCK, *k.shape[2:])
    return jnp.concatenate([kp[:, j:j + nblk] for j in range(n_prev + 1)], axis=2)

def banded_attention(q, k, v, window, slopes, sink=None):
    B, S, H, Dh = q.shape
    Hkv = k.shape[2]
    G = H // Hkv
    nblk = S // Q_BLOCK
    n_prev = -(-(window - 1) // Q_BLOCK)
    K = (n_prev + 1) * Q_BLOCK
    kw = band_windows(k, n_prev)
    vw = band_windows(v, n_prev)
    qb = q.reshape(B, nblk, Q_BLOCK, Hkv, G, Dh)
    s = jnp.einsum("bnqhgd,bnkhd->bnhgqk", qb, kw).astype(jnp.float32) * Dh ** -0.5
    rel = jnp.arange(Q_BLOCK)[:, None] + n_prev * Q_BLOCK - jnp.arange(K)[None, :]
    kpos = jnp.arange(nblk)[:, None] * Q_BLOCK - n_prev * Q_BLOCK + jnp.arange(K)[None, :]
    mask = ((rel >= 0) & (rel < window))[None] & (kpos >= 0)[:, None, :]
    s = s - slopes.reshape(Hkv, G, 1, 1) * rel.astype(jnp.float32)
    sk = None if sink is None else sink.astype(jnp.float32).reshape(1, 1, Hkv, G, 1, 1)
    p = masked_softmax(s, mask[None, :, None, None], sk)
    o = jnp.einsum("bnhgqk,bnkhd->bnqhgd", p.astype(v.dtype), vw)
    return o.reshape(B, S, H, Dh)

def nsa_attention(q, kv, gate_logits, pos_emb, w1, w2):
    B, S, H, Dh = q.shape
    k_cmp, v_cmp, k_sel, v_sel, k_win, v_win = jnp.split(kv, 6, axis=-1)
    slopes = alibi_slopes(H)
    scale = Dh ** -0.5
    t = jnp.arange(S)

    nc = S // CMP_BLOCK
    def compress(z, j):
        zb = z.reshape(B, nc, CMP_BLOCK, Dh) + pos_emb[j]
        return jax.nn.silu(zb.reshape(B, nc, CMP_BLOCK * Dh) @ w1[j]) @ w2[j]
    kc = compress(k_cmp, 0)
    vc = compress(v_cmp, 1)
    blk_end = jnp.arange(nc) * CMP_BLOCK + CMP_BLOCK - 1
    dist = t[:, None] - blk_end[None, :]
    s = jnp.einsum("bshd,bcd->bhsc", q, kc).astype(jnp.float32) * scale
    s = s - slopes[:, None, None] * dist.astype(jnp.float32)
    p_cmp = masked_softmax(s, dist >= 0)
    o_cmp = jnp.einsum("bhsc,bcd->bshd", p_cmp.astype(vc.dtype), vc)

    ns = S // SEL_BLOCK
    ratio = SEL_BLOCK // CMP_BLOCK
    imp = p_cmp.sum(axis=1).reshape(B, S, ns, ratio).sum(axis=-1)
    blk = jnp.arange(ns)[None, :]
    cur = (t // SEL_BLOCK)[:, None]
    future = blk * SEL_BLOCK > t[:, None]
    forced = (blk == 0) | (blk == cur) | (blk == cur - 1)
    imp = jnp.where(forced, FORCED_SCORE, jnp.where(future, -1.0, imp))
    topk = min(SEL_TOPK, ns)
    _, idx = lax.top_k(imp, topk)

    kb = k_sel.reshape(B, ns, SEL_BLOCK, Dh)
    vb = v_sel.reshape(B, ns, SEL_BLOCK, Dh)
    nq = S // Q_BLOCK
    qs = q.reshape(B, nq, Q_BLOCK, H, Dh).swapaxes(0, 1)
    ids = idx.reshape(B, nq, Q_BLOCK, topk).swapaxes(0, 1)
    qpos = t.reshape(nq, Q_BLOCK)
    bidx = jnp.arange(B)[:, None, None]
    n_keys = topk * SEL_BLOCK

    def sel_block(args):
        qi, ii, pi = args
        kg = kb[bidx, ii].reshape(B, Q_BLOCK, n_keys, Dh)
        vg = vb[bidx, ii].reshape(B, Q_BLOCK, n_keys, Dh)
        kpos = (ii[..., None] * SEL_BLOCK + jnp.arange(SEL_BLOCK)).reshape(B, Q_BLOCK, n_keys)
        d = pi[None, :, None] - kpos
        sc = jnp.einsum("bqhd,bqkd->bhqk", qi, kg).astype(jnp.float32) * scale
        sc = sc - slopes[:, None, None] * d[:, None].astype(jnp.float32)
        pr = masked_softmax(sc, (d >= 0)[:, None])
        return jnp.einsum("bhqk,bqkd->bqhd", pr.astype(vg.dtype), vg)

    o_sel = lax.map(sel_block, (qs, ids, qpos)).swapaxes(0, 1).reshape(B, S, H, Dh)

    o_win = banded_attention(q, k_win[:, :, None], v_win[:, :, None], NSA_WINDOW, slopes)

    g = jax.nn.sigmoid(gate_logits.astype(jnp.float32)).reshape(B, S, H, 3).astype(q.dtype)
    return g[..., 0:1] * o_cmp + g[..., 1:2] * o_sel + g[..., 2:3] * o_win

def stick_breaking_attention(q, k, v):
    B, S, H, Dh = q.shape
    nq = S // Q_BLOCK
    qs = q.reshape(B, nq, Q_BLOCK, H, Dh).swapaxes(0, 1)
    qpos = jnp.arange(S).reshape(nq, Q_BLOCK)
    kpos = jnp.arange(S)
    scale = Dh ** -0.5

    def one_block(args):
        qi, pi = args
        z = jnp.einsum("bqhd,bkhd->bhqk", qi, k).astype(jnp.float32) * scale
        mask = kpos[None, :] < pi[:, None]
        log_beta = jax.nn.log_sigmoid(z)
        log_1m = jnp.where(mask, jax.nn.log_sigmoid(-z), 0.0)
        suffix = lax.cumsum(log_1m, axis=3, reverse=True) - log_1m
        a = jnp.where(mask, jnp.exp(log_beta + suffix), 0.0)
        return jnp.einsum("bhqk,bkhd->bqhd", a.astype(v.dtype), v)

    return lax.map(one_block, (qs, qpos)).swapaxes(0, 1).reshape(B, S, H, Dh)

def retention(q, k, v):
    B, S, H, Dh = q.shape
    C = RET_CHUNK
    n = S // C
    log_g = jnp.log(1.0 - jnp.asarray(2.0 ** (-5.0 - np.arange(H)), dtype=jnp.float32))
    qc = (q.astype(jnp.float32) * Dh ** -0.5).reshape(B, n, C, H, Dh)
    kc = k.astype(jnp.float32).reshape(B, n, C, H, Dh)
    vc = v.astype(jnp.float32).reshape(B, n, C, H, Dh)
    i = jnp.arange(C)
    diff = (i[:, None] - i[None, :]).astype(jnp.float32)
    dmat = jnp.where(diff >= 0, jnp.exp(log_g[:, None, None] * jnp.maximum(diff, 0.0)), 0.0)
    s = jnp.einsum("bnihd,bnjhd->bnhij", qc, kc) * dmat
    intra = jnp.einsum("bnhij,bnjhd->bnihd", s, vc)
    zeta = jnp.exp(log_g[:, None] * (C - 1 - i)[None, :].astype(jnp.float32))
    u = jnp.einsum("bnjhd,bnjhe,hj->nbhde", kc, vc, zeta)
    g_chunk = jnp.exp(log_g * C)[None, :, None, None]

    def step(r, u_n):
        return r * g_chunk + u_n, r

    _, r_prev = lax.scan(step, jnp.zeros((B, H, Dh, Dh), jnp.float32), u)
    xi = jnp.exp(log_g[:, None] * (i + 1)[None, :].astype(jnp.float32))
    cross = jnp.einsum("bnihd,nbhde,hi->bnihe", qc, r_prev, xi)
    o = (intra + cross).reshape(B, S, H, Dh)
    mu = jnp.mean(o, axis=-1, keepdims=True)
    var = jnp.mean((o - mu) ** 2, axis=-1, keepdims=True)
    return ((o - mu) * lax.rsqrt(var + LN_EPS)).astype(q.dtype)

def hybrid_layer(x, c, w_ada, b_ada, norm_g, w_in, cmp_pos, cmp_w1, cmp_w2, sink, w_merge, w_br, w_out):
    B, S, _ = x.shape
    mod = (jax.nn.silu(c) @ w_ada + b_ada)[:, None, :]
    shift, scale, gate = jnp.split(mod, 3, axis=-1)
    h = rms_norm(x, norm_g) * (1.0 + scale) + shift
    (a_q, a_kv, a_g, a_z, b_q, b_k, b_v, b_z,
     c_q, c_k, c_v, c_z, d_q, d_k, d_v, d_z) = jnp.split(h @ w_in, IN_OFFSETS, axis=-1)

    def heads(z):
        return z.reshape(B, S, -1, HEAD_DIM)

    y_a = nsa_attention(heads(a_q), a_kv, a_g, cmp_pos, cmp_w1, cmp_w2)
    y_b = banded_attention(heads(b_q), heads(b_k), heads(b_v), SWA_WINDOW, alibi_slopes(N_HEADS), sink)
    y_c = stick_breaking_attention(heads(c_q), heads(c_k), heads(c_v))
    y_d = retention(heads(d_q), heads(d_k), heads(d_v))

    branches = ((y_a, a_z), (y_b, b_z), (y_c, c_z), (y_d, d_z))
    merged = None
    for i, (y, z) in enumerate(branches):
        yi = y.reshape(B, S, BRANCH_W) * jax.nn.silu(z)
        term = jax.nn.sigmoid(h @ w_merge[i]) * (yi @ w_br[i])
        merged = term if merged is None else merged + term
    return x + gate * (merged @ w_out)

def first_inputs(seed: int = 0) -> dict:
    key = jax.random.key(seed)
    ks = jax.random.split(key, 14)
    D = D_MODEL
    f32 = jnp.float32

    def nrm(k, shape, fan):
        return jax.random.normal(k, shape, f32) * fan ** -0.5

    return {
        "x": jax.random.normal(ks[0], (BATCH, SEQ, D), f32),
        "c": jax.random.normal(ks[1], (BATCH, D), f32),
        "w_ada": nrm(ks[2], (DEPTH, D, 3 * D), D) * 0.5,
        "b_ada": 0.02 * jax.random.normal(ks[3], (DEPTH, 3 * D), f32),
        "norm_g": 1.0 + 0.05 * jax.random.normal(ks[4], (DEPTH, D), f32),
        "w_in": nrm(ks[5], (DEPTH, D, IN_W), D),
        "cmp_pos": 0.1 * jax.random.normal(ks[6], (DEPTH, 2, CMP_BLOCK, HEAD_DIM), f32),
        "cmp_w1": nrm(ks[7], (DEPTH, 2, CMP_BLOCK * HEAD_DIM, HEAD_DIM), CMP_BLOCK * HEAD_DIM),
        "cmp_w2": nrm(ks[8], (DEPTH, 2, HEAD_DIM, HEAD_DIM), HEAD_DIM),
        "sink": 0.5 * jax.random.normal(ks[9], (DEPTH, N_HEADS), f32),
        "w_merge": nrm(ks[10], (DEPTH, N_BRANCH, D, D), D),
        "w_br": nrm(ks[11], (DEPTH, N_BRANCH, BRANCH_W, D), BRANCH_W),
        "w_out": nrm(ks[12], (DEPTH, D, D), D),
        "final_g": 1.0 + 0.05 * jax.random.normal(ks[13], (D,), f32),
    }

def first_block(x, c, w_ada, b_ada, norm_g, w_in, cmp_pos, cmp_w1, cmp_w2, sink, w_merge, w_br, w_out, final_g):
    for l in range(DEPTH):
        x = hybrid_layer(x, c, w_ada[l], b_ada[l], norm_g[l], w_in[l], cmp_pos[l], cmp_w1[l], cmp_w2[l],
                         sink[l], w_merge[l], w_br[l], w_out[l])
    return rms_norm(x, final_g)


D_MIX = D_MODEL
D_CONF = D_MIX // 4
D_ATT = D_MIX // 4
D_SC = D_MIX // 4
D_POOL = D_MIX - D_CONF - D_ATT - D_SC
N_ATT_HEADS = D_ATT // HEAD_DIM
CONF_KERNEL = 31
SC_KERNEL = 3
POOL_WINDOWS = (2, 4, 8, 16)
N_POOL_GROUPS = len(POOL_WINDOWS)
POOL_GROUP_DIM = D_POOL // N_POOL_GROUPS
D_FF = 4 * D_MODEL
D_PLE = 256
EPS = 1e-6
SPLITS = (2 * D_CONF, D_ATT, D_ATT, D_ATT, N_ATT_HEADS, D_SC, D_SC, D_SC, D_POOL)
D_IN = sum(SPLITS)
SPLIT_IDX = tuple(int(s) for s in np.cumsum(SPLITS)[:-1])


def rms_norm_2(x, g):
    x32 = x.astype(jnp.float32)
    y = x32 * lax.rsqrt(jnp.mean(x32 * x32, axis=-1, keepdims=True) + EPS)
    return (y * g.astype(jnp.float32)).astype(x.dtype)

def layer_norm(x, g, b):
    x32 = x.astype(jnp.float32)
    mu = jnp.mean(x32, axis=-1, keepdims=True)
    xc = x32 - mu
    y = xc * lax.rsqrt(jnp.mean(xc * xc, axis=-1, keepdims=True) + EPS)
    return (y * g.astype(jnp.float32) + b.astype(jnp.float32)).astype(x.dtype)

def causal_depthwise_conv(u, w):
    k = w.shape[0]
    return lax.conv_general_dilated(
        u, w[:, None, :].astype(u.dtype), window_strides=(1,), padding=((k - 1, 0),),
        dimension_numbers=("NWC", "WIO", "NWC"), feature_group_count=u.shape[-1])

def conformer_conv(ab, w_dw, ln_g, ln_b, w_pw):
    a, b = jnp.split(ab, 2, axis=-1)
    u = a * jax.nn.sigmoid(b)
    u = causal_depthwise_conv(u, w_dw)
    u = jax.nn.silu(layer_norm(u, ln_g, ln_b))
    return u @ w_pw

def forgetting_attention(q, k, v, f_logit):
    b, s, _ = q.shape
    q = q.reshape(b, s, N_ATT_HEADS, HEAD_DIM).transpose(0, 2, 1, 3)
    k = k.reshape(b, s, N_ATT_HEADS, HEAD_DIM).transpose(0, 2, 1, 3)
    v = v.reshape(b, s, N_ATT_HEADS, HEAD_DIM).transpose(0, 2, 1, 3)
    log_f = jax.nn.log_sigmoid(f_logit.astype(jnp.float32))
    c = jnp.cumsum(log_f, axis=1).transpose(0, 2, 1)
    nb = s // Q_BLOCK
    qb = q.reshape(b, N_ATT_HEADS, nb, Q_BLOCK, HEAD_DIM).transpose(2, 0, 1, 3, 4)
    cb = c.reshape(b, N_ATT_HEADS, nb, Q_BLOCK).transpose(2, 0, 1, 3)
    pos = jnp.arange(s, dtype=jnp.int32)
    posb = pos.reshape(nb, Q_BLOCK)
    k32 = k.astype(jnp.float32)
    scale = HEAD_DIM ** -0.5

    def block(args):
        qi, ci, pi = args
        logits = jnp.einsum("bhqd,bhkd->bhqk", qi.astype(jnp.float32), k32) * scale
        logits = logits + ci[..., None] - c[:, :, None, :]
        mask = pi[:, None] >= pos[None, :]
        logits = jnp.where(mask, logits, -jnp.inf)
        probs = jax.nn.softmax(logits, axis=-1)
        return jnp.einsum("bhqk,bhkd->bhqd", probs.astype(v.dtype), v)

    o = lax.map(block, (qb, cb, posb))
    return o.transpose(1, 0, 3, 2, 4).reshape(b, s, D_ATT)

def short_conv_mixer(h, bg, cg, w_sc):
    return bg * causal_depthwise_conv(cg * h, w_sc)

def multiscale_pool(v, w_pool, scale):
    b, s, _ = v.shape
    v32 = v.astype(jnp.float32)
    count = jnp.arange(1, s + 1, dtype=jnp.float32)[None, :, None]
    groups = jnp.split(v32, N_POOL_GROUPS, axis=-1)
    outs = []
    for g, w in zip(groups, POOL_WINDOWS):
        csum = jnp.cumsum(g, axis=1)
        lag = jnp.pad(csum, ((0, 0), (w, 0), (0, 0)))[:, :s]
        mean = (csum - lag) / jnp.minimum(count, w)
        outs.append(mean - g)
    d = jnp.stack(outs, axis=2).astype(v.dtype)
    d = jnp.einsum("bsgc,gcd->bsgd", d, w_pool).reshape(b, s, D_POOL)
    return d * scale

def second_inputs(seed: int = 0) -> dict:
    key = jax.random.key(seed)
    ks = jax.random.split(key, 24)
    f32 = jnp.float32
    L = DEPTH

    def nrm(k, shape, fan_in):
        return jax.random.normal(k, shape, f32) * (fan_in ** -0.5)

    def gain(k, shape):
        return 1.0 + 0.05 * jax.random.normal(k, shape, f32)

    return {
        "x": jax.random.normal(ks[0], (BATCH, SEQ, D_MODEL), f32),
        "p": jax.random.normal(ks[1], (DEPTH, BATCH, SEQ, D_PLE), f32),
        "g_mix_pre": gain(ks[2], (L, D_MODEL)),
        "w_in": nrm(ks[3], (L, D_MODEL, D_IN), D_MODEL),
        "b_forget": 0.1 * jax.random.normal(ks[4], (L, N_ATT_HEADS), f32),
        "w_conf_dw": nrm(ks[5], (L, CONF_KERNEL, D_CONF), CONF_KERNEL),
        "conf_ln_g": gain(ks[6], (L, D_CONF)),
        "conf_ln_b": 0.02 * jax.random.normal(ks[7], (L, D_CONF), f32),
        "w_conf_pw": nrm(ks[8], (L, D_CONF, D_CONF), D_CONF),
        "w_sc": nrm(ks[9], (L, SC_KERNEL, D_SC), SC_KERNEL),
        "w_pool": nrm(ks[10], (L, N_POOL_GROUPS, POOL_GROUP_DIM, POOL_GROUP_DIM), POOL_GROUP_DIM),
        "pool_scale": gain(ks[11], (L, D_POOL)),
        "w_out": nrm(ks[12], (L, D_MIX, D_MODEL), D_MIX),
        "g_mix_post": gain(ks[13], (L, D_MODEL)),
        "g_mlp_pre": gain(ks[14], (L, D_MODEL)),
        "w_up": nrm(ks[15], (L, D_MODEL, D_FF), D_MODEL),
        "w_down": nrm(ks[16], (L, D_FF, D_MODEL), D_FF),
        "g_mlp_post": gain(ks[17], (L, D_MODEL)),
        "g_ple_pre": gain(ks[18], (L, D_MODEL)),
        "w_ple_gate": nrm(ks[19], (L, D_MODEL, D_MODEL), D_MODEL),
        "w_ple_proj": nrm(ks[20], (L, D_PLE, D_MODEL), D_PLE),
        "g_ple_post": gain(ks[21], (L, D_MODEL)),
    }

def second_block(x, p, g_mix_pre, w_in, b_forget, w_conf_dw, conf_ln_g, conf_ln_b, w_conf_pw,
              w_sc, w_pool, pool_scale, w_out, g_mix_post, g_mlp_pre, w_up, w_down,
              g_mlp_post, g_ple_pre, w_ple_gate, w_ple_proj, g_ple_post):
    h = x
    for i in range(DEPTH):
        xn = rms_norm_2(h, g_mix_pre[i])
        z = xn @ w_in[i]
        conf_ab, q, k, v, f_logit, sc_h, sc_b, sc_c, pool_v = jnp.split(z, SPLIT_IDX, axis=-1)
        y_conf = conformer_conv(conf_ab, w_conf_dw[i], conf_ln_g[i], conf_ln_b[i], w_conf_pw[i])
        y_att = forgetting_attention(q, k, v, f_logit + b_forget[i])
        y_sc = short_conv_mixer(sc_h, sc_b, sc_c, w_sc[i])
        y_pool = multiscale_pool(pool_v, w_pool[i], pool_scale[i])
        mix = jnp.concatenate([y_conf, y_att, y_sc, y_pool], axis=-1) @ w_out[i]
        h = h + rms_norm_2(mix, g_mix_post[i])
        hn = rms_norm_2(h, g_mlp_pre[i])
        ff = jnp.square(jax.nn.relu(hn @ w_up[i])) @ w_down[i]
        h = h + rms_norm_2(ff, g_mlp_post[i])
        gate = jax.nn.sigmoid(rms_norm_2(h, g_ple_pre[i]) @ w_ple_gate[i])
        e = (p[i] @ w_ple_proj[i]) * gate
        h = h + rms_norm_2(e, g_ple_post[i])
    return h


def setup_inputs(seed=0):
    out = dict(first_inputs(seed))
    for name, value in second_inputs(seed + 1).items():
        if name != "x":
            out[name + "_2"] = value
    return out


def reference(
    x, c, w_ada, b_ada, norm_g, w_in, cmp_pos, cmp_w1, cmp_w2, sink, w_merge, w_br, w_out,
    final_g, p_2, g_mix_pre_2, w_in_2, b_forget_2, w_conf_dw_2, conf_ln_g_2, conf_ln_b_2,
    w_conf_pw_2, w_sc_2, w_pool_2, pool_scale_2, w_out_2, g_mix_post_2, g_mlp_pre_2, w_up_2,
    w_down_2, g_mlp_post_2, g_ple_pre_2, w_ple_gate_2, w_ple_proj_2, g_ple_post_2,
):
    x = first_block(
        x, c, w_ada, b_ada, norm_g, w_in, cmp_pos, cmp_w1, cmp_w2, sink, w_merge, w_br, w_out,
        final_g,
    )
    return second_block(
        x, p_2, g_mix_pre_2, w_in_2, b_forget_2, w_conf_dw_2, conf_ln_g_2, conf_ln_b_2,
        w_conf_pw_2, w_sc_2, w_pool_2, pool_scale_2, w_out_2, g_mix_post_2, g_mlp_pre_2, w_up_2,
        w_down_2, g_mlp_post_2, g_ple_pre_2, w_ple_gate_2, w_ple_proj_2, g_ple_post_2,
    )


_drawn_inputs = setup_inputs


def setup_inputs(seed=0):
    import zlib

    import numpy as np

    out = dict(_drawn_inputs(seed))
    spreads = {}
    factors = {'b_ada': 3.53,
     'norm_g': 3.641,
     'cmp_pos': 8.0,
     'sink': 200.0,
     'b_forget_2': 8.0,
     'conf_ln_g_2': 3.643,
     'conf_ln_b_2': 21.35,
     'pool_scale_2': 2.775,
     'g_ple_pre_2': 5.764}
    for name, (base, spread) in spreads.items():
        noise = np.random.default_rng([zlib.crc32(name.encode()), seed]).standard_normal(out[name].shape)
        drawn = base * np.exp(spread * noise) if base else spread * noise
        out[name] = jnp.asarray(drawn.astype(out[name].dtype))
    for name, factor in factors.items():
        out[name] = (out[name] * factor).astype(out[name].dtype)
    return out
```

```python
from contextlib import ExitStack

import numpy as np
import concourse.bass as bass
from concourse import mybir

ALU = mybir.AluOpType
ACT = mybir.ActivationFunctionType
F32 = mybir.dt.float32
F32R = mybir.dt.float32r
BF16 = mybir.dt.bfloat16
I32 = mybir.dt.int32
AX = mybir.AxisListType.X

P = 128
S = 1024
D = 1024
NC = D // P
NB = S // P
H = 4
DH = 64
BW = H * DH
HALF = 512
FF = 4 * D
NCMP = S // 32
TINY = 1e-30
NEG = -1e30
SLOPES = [2.0 ** (-8.0 * (h + 1) / H) for h in range(H)]
QSCALE = DH ** -0.5

BRANCHES = "DBCA"
NPROJ = {"D": ["q0", "q1", "k0", "k1", "v0", "v1", "t0", "t1"],
         "B": ["q0", "q1", "k0", "k1", "v0"],
         "C": ["q0", "q1", "k0", "k1", "v0", "v1"],
         "A": ["q0", "q1", "cmp", "k0", "k1", "v0", "gates"]}
NEIGHTH = 8
UPS = FF // P // NEIGHTH


def list_blocks():
    blocks = []

    def proj(br):
        for name in NPROJ[br]:
            kind = "T" if name[0] in "vtg" else "F"
            blocks.append(("T" if kind == "T" else "F", br + name, 12 if name == "gates" else P))

    def merge(br):
        for n in range(2):
            blocks.append(("F", br + "z%d" % n, P))
        for n in range(NC):
            blocks.append(("M", br + "m%d" % n, P))

    proj("D")
    proj("B")
    merge("D")
    proj("C")
    merge("B")
    proj("A")
    merge("C")
    merge("A")
    blocks.extend(("F", "o%d" % n, P) for n in range(NC))
    for name in ["q0", "q1", "k0", "k1", "v0", "v1", "f", "cb0", "ca0", "cb1", "ca1",
                 "sh0", "sc0", "sb0", "sh1", "sc1", "sb1", "p0", "p1"]:
        blocks.append(("T" if name[0] == "v" else "F", "E" + name, P))
    blocks.extend(("F", "x%d" % n, P) for n in range(NC))
    for e in range(NEIGHTH):
        blocks.extend(("F", "u%d_%d" % (e, n), P) for n in range(UPS))
        blocks.extend(("D", "d%d_%d" % (e, n), 2 * P) for n in range(NC // 2))
    blocks.extend(("M", "g%d" % n, P) for n in range(NC))
    return blocks


BLOCKS = list_blocks()
INDEX = {name: b for b, (_, name, _) in enumerate(BLOCKS)}
BLOCK_LEN = [{"F": 8 * P, "T": 8 * n, "M": 10 * P, "D": 8 * P}[kind] for kind, _, n in BLOCKS]
BLOCK_OFF = [P * int(v) for v in np.cumsum([0] + BLOCK_LEN)]

TIMELINE_TILES = {}


def dense_part_events(names):
    return [("dense", INDEX[n], part) for n in names for part in range(4)]


def spread(dense, steps):
    out, done = [], 0
    for n, ev in enumerate(dense):
        out.append(ev)
        want = (n + 1) * len(steps) // len(dense)
        out.extend(steps[done:want])
        done = want
    return out


NRET, NSTICK, NSWA, NSEL, NWIN, NFGT = NB, H * 12, 32, 32, 32, 32
U_SWA, U_SEL, U_WIN, U_FGT = 0, 32, 64, 96


def soft_events(first, n):
    return [("soft", first + u, first, n) for u in range(n + 2)]


def list_timeline():
    def merge_names(br):
        return [br + "m%d" % n for n in range(NC)]

    def z_events(br):
        ev = dense_part_events([br + "z0", br + "z1"])
        return ev + [("ytrans", br, 0), ("ytrans", br, 1)]

    tl = [("norm1",)]
    tl += dense_part_events("D" + n for n in NPROJ["D"])
    ret = [("ret", n) for n in range(NB + 1)] + [("retnorm",)]
    tl += spread(dense_part_events("B" + n for n in NPROJ["B"]), ret)
    tl += z_events("D")
    tl += spread(dense_part_events(merge_names("D")), soft_events(U_SWA, NSWA))
    tl += dense_part_events("C" + n for n in NPROJ["C"])
    tl += z_events("B")
    tl += spread(dense_part_events(merge_names("B")), [("stick", s) for s in range(NSTICK + 2)])
    tl += dense_part_events("A" + n for n in NPROJ["A"])
    tl += z_events("C")
    tl += spread(dense_part_events(merge_names("C")),
                 [("cmp", s) for s in range(6)] + soft_events(U_SEL, NSEL + NWIN))
    tl += z_events("A")
    tl += dense_part_events(merge_names("A"))
    tl += [("split_merged",)]
    tl += dense_part_events("o%d" % n for n in range(NC))
    tl += [("norm2",)]
    tl += dense_part_events("E" + n for n in ["q0", "q1", "k0", "k1", "v0", "v1", "f"])
    soft = [("fprep", 0)] + soft_events(U_FGT, NFGT)
    taps = [("conv", t, k) for t in range(2) for k in range(31)]
    steps, soft = soft[:17], soft[17:]
    while soft or taps:
        steps += taps[:3] + soft[:1]
        taps, soft = taps[3:], soft[1:]
    rest = ["cb0", "ca0", "cb1", "ca1", "sh0", "sc0", "sb0", "sh1", "sc1", "sb1", "p0", "p1"]
    tl += spread(dense_part_events("E" + n for n in rest), steps)
    tl += [("mix",)]
    tl += dense_part_events("x%d" % n for n in range(NC))
    tl += [("norm3",)]
    for e in range(NEIGHTH):
        tl += dense_part_events("u%d_%d" % (e, n) for n in range(UPS))
        tl += dense_part_events("d%d_%d" % (e, n) for n in range(NC // 2))
    tl += [("norm4",)]
    tl += dense_part_events("g%d" % n for n in range(NC))
    tl += [("norm5",)]
    return tl


TIMELINE = list_timeline()


def number_tiles():
    g, tiles = 0, {}
    for ev in TIMELINE:
        if ev[0] == "dense" and ev[2] == 0:
            kind, name, _ = BLOCKS[ev[1]]
            tiles[name] = g
            g += 2 if kind in "MD" else 1
        elif ev[0] == "ytrans":
            tiles["y%s%d" % (ev[1], ev[2])] = g
            g += 1
        elif ev[0] == "mix":
            tiles["yE0"] = g
            g += 2
    tiles["yE1"] = tiles["yE0"] + 1
    return tiles


TILE = number_tiles()


def last_tile(b):
    kind, name, _ = BLOCKS[b]
    return TILE[name] + (1 if kind in "MD" else 0)


def unit(u):
    ph, r = ("SWA", "SEL", "WIN", "FGT")[u // 32], u % 32
    if ph == "FGT":
        h, i = r // NB, r % NB
    else:
        i, h = r // H, r % H
    lo = {"SWA": max(0, i - 1), "SEL": 0, "WIN": max(0, i - 4), "FGT": 0}[ph]
    return ph, h, i, lo, i + 1 - lo


def batches(u):
    return -(-unit(u)[4] // 4)


BATCH_END = [int(v) for v in np.cumsum([batches(u) for u in range(128)])]


STICK = [(h, half, j) for h in range(H) for half in range(2) for j in range(4 * half + 3, -1, -1)]
STICK_DIAG = [j * P >= half * HALF for _, half, j in STICK]
DIAG_COUNT = [int(v) for v in np.cumsum(STICK_DIAG)]


def stick_q0(s):
    _, half, j = STICK[s]
    return max(0, j * P - half * HALF)


def table_layout():
    at, out = 0, {}
    for name, n in [("dist", S), ("ident", P), ("strict", P), ("tri", P), ("negones", P), ("ones", P),
                    ("up", P), ("low", P), ("cdist", NB * NCMP), ("cmask", NB * NCMP), ("gc", 2),
                    ("eps6", 1), ("eps5", 1), ("invw", 2), ("invc", 32)]:
        out[name] = (at, n)
        at += n
    return out, at


TABLES, NTABLE = table_layout()
VECS = {}
_at = 0
for _n, _w in [("c", 8), ("b_ada", 24), ("norm_g", 8), ("final_g", 8), ("g_mix_pre", 8), ("g_mix_post", 8),
               ("g_mlp_pre", 8), ("g_mlp_post", 8), ("g_ple_pre", 8), ("g_ple_post", 8),
               ("dw", 62), ("ln_g", 2), ("ln_b", 2), ("sc", 6), ("pool_scale", 2), ("sink", 4), ("bf", 1),
               ("pos", 32)]:
    VECS[_n] = (_at, _w)
    _at += _w
NVEC = _at
RET_TABLE = 4 * P + 2 * P + 2 * P
CMP_W2 = 3 * DH


def build(nc, xT, pT, wstream, wada, vecs, tables, rtables, cw1, cw2, wpw, wpool, out):
    with ExitStack() as ctx:
        base = 16512
        K = 256

        def at(name, kib, shape, dt=F32):
            return nc.alloc_sbuf_tensor_at(name, shape, dt, offset=base + int(kib * 1024))

        def psum(name, shape):
            return ctx.enter_context(nc.psum_tensor(name, shape, F32))

        def sem(name):
            return ctx.enter_context(nc.semaphore(name))

        xhi = at("xhi", 0, [P, NC, S], F32R)
        xlo = at("xlo", 32, [P, NC, S], F32R)
        ada0 = at("ada0", 0, [P, 8, D])
        ada1 = at("ada1", 32, [P, 8, D])
        mm = at("mm", 64, [P, NC, S])
        raw = at("raw", 96, [P, 10 * P])
        whi = [at("whi%d" % i, 101 + 5 * i, [P, 10, P], F32R) for i in range(2)]
        wlo = [at("wlo%d" % i, 111 + 5 * i, [P, 10, P], F32R) for i in range(2)]
        yhi = at("yhi", 121, [P, 2, S], F32R)
        ylo = at("ylo", 129, [P, 2, S], F32R)
        uhi = at("uhi", 121, [P, UPS, S], F32R)
        ulo = at("ulo", 137, [P, UPS, S], F32R)
        rtab = at("rtab", 121, [P, RET_TABLE])
        rst = at("rst", 125, [P, NB, 2, DH])
        cb = at("cb", 121, [P, S])
        ct = at("ct", 125, [P, S])
        cu = at("cu", 129, [P, 2, S])
        ytok = at("ytok", 137, [P, NB, BW])
        zs2 = [at("zs2%d" % i, 137 + 4 * i, [P, S]) for i in range(2)]
        sbuf = [at("sbuf%d" % i, 145 + 4 * i, [P, S]) for i in range(2)]
        pbuf = [at("pbuf%d" % i, 153 + 4 * i, [P, S]) for i in range(2)]
        sq8 = at("sq8", 145, [P, NB, BW])
        skt = [at("skt%d" % i, 145 + 2 * i, [P, HALF]) for i in range(2)]
        ska = [at("ska%d" % i, 153 + 2 * i, [P, HALF]) for i in range(2)]
        skl = [at("skl%d" % i, 157 + 2 * i, [P, HALF]) for i in range(2)]
        cw1s = at("cw1s", 153, [P, 32, DH])
        tbuf = [at("tbuf0", 153, [P, S]), at("tbuf1", 157, [P, S])]
        brq = at("brq", 161, [P, 2, S])
        brk = at("brk", 169, [P, 2, S])
        brv = at("brv", 177, [P, 2, NB, P])
        dq = at("dq", 64, [P, 2, S])
        dk = at("dk", 72, [P, 2, S])
        dv = at("dv", 80, [P, 2, NB, P])
        dt_ = at("dt", 88, [P, 2, NB, P])
        acmp = at("acmp", 181, [P, S])
        ada2 = at("ada2", 161, [P, 8, D])
        res = at("res", 161, [P, NC, S])
        zs = [at("zs%d" % i, 186 + 4 * i, [P, S]) for i in range(2)]
        cacc = at("cacc", 64, [P, 2, S])
        scy = at("scy", 72, [P, 2, S])
        ply = at("ply", 80, [P, 2, S])
        su = at("su", 88, [P, S])
        sx = at("sx", 92, [P, S])
        tab = at("tab", 194, [P, NTABLE])
        top = 194 + (NTABLE * 4 + 31) // 32 * 32 / 1024

        small_at = [top]

        def small(name, shape, dt=F32):
            n = int(np.prod(shape[1:])) * (2 if dt == BF16 else 4)
            t = at(name, small_at[0], shape, dt)
            small_at[0] += (n + 31) // 32 * 32 / 1024
            return t

        vec = small("vec", [P, NVEC])
        identb = small("identb", [P, P], BF16)
        upb = small("upb", [P, P], BF16)
        lowb = small("lowb", [P, P], BF16)
        csil = small("csil", [P, 8])
        mod = small("mod", [P, 24])
        gmul = small("gmul", [P, 8])
        nsink = small("nsink", [P, 4])
        nmx = small("nmx", [P, 4])
        den = small("den", [P, 4])
        esk = small("esk", [P, 4])
        fac = small("fac", [P, 4])
        gates = small("gates", [P, NB, 12])
        st32 = small("st32", [P, 4, 32])
        ci = small("ci", [P, NB, 4])
        kct = small("kct", [P, NCMP])
        vc4 = small("vc4", [P, DH])
        hsil = small("hsil", [DH, 5 * NCMP])
        assert base + small_at[0] * 1024 <= 229344, small_at[0]
        cw2s = at("cw2s", 185, [DH, CMP_W2])
        wpws = at("wpws", 186, [P, 2, BW])
        wpls = at("wpls", 188, [P, 2, P])

        def t_(name, a=0, n=None):
            o, w = TABLES[name]
            return tab[:, o + a:o + (w if n is None else a + n)]

        def v_(name, a=0, n=None):
            o, w = VECS[name]
            return vec[:, o + a:o + (w if n is None else a + n)]

        slot = [psum("slot%d" % i, [P, S]) for i in range(2)]
        ps4 = psum("ps4", [P, S])
        ps6 = psum("ps6", [P, HALF])
        ps7 = psum("ps7", [P, HALF])
        psb = [ps4[:, 0:HALF], ps4[:, HALF:S]]
        pso = [ps6, ps7]

        res_dram = nc.dram_tensor("res_dram", [P, NC, S], F32, kind="Internal").ap()

        small_in, x_in, raw_in, rtab_in = (sem(n) for n in ("small_in", "x_in", "raw_in", "rtab_in"))
        ada_in = [sem("ada_in%d" % i) for i in range(3)]
        cmp_in, xres_in, res_out, res_in, p_in, pw_in, out_done = (
            sem(n) for n in ("cmp_in", "xres_in", "res_out", "res_in", "p_in", "pw_in", "out_done"))
        w_hi, w_lo, tile_done = sem("w_hi"), sem("w_lo"), sem("tile_done")
        slot_free = [sem("slot_free0"), sem("slot_free1")]
        x_hi, x_lo, x_src = sem("x_hi"), sem("x_lo"), sem("x_src")
        y_src, y_hi, y_lo = sem("y_src"), sem("y_hi"), sem("y_lo")
        u_src, u_hi, u_lo = sem("u_src"), sem("u_hi"), sem("u_lo")
        prod_done, sum_done = sem("prod_done"), sem("sum_done")
        csil_done, mod_mm, mod_done, masks_done = sem("csil_done"), sem("mod_mm"), sem("mod_done"), sem("masks_done")
        chunk_ready, sq_done, sq_added, nsum, nstd, nrstd = (
            sem(n) for n in ("chunk_ready", "sq_done", "sq_added", "nsum", "nstd", "nrstd"))
        dve_chain, act_chain, pool_chain = sem("dve_chain"), sem("act_chain"), sem("pool_chain")
        s_scores, s_biased, s_negmax, s_exp, s_pt, s_ptsb, s_out, s_norm, s_esk = (
            sem(n) for n in ("s_scores", "s_biased", "s_negmax", "s_exp", "s_pt", "s_ptsb", "s_out", "s_norm", "s_esk"))
        r_s, r_st, r_qx, r_state, r_o, r_y, r_sq, r_var, ret_done = (
            sem(n) for n in ("r_s", "r_st", "r_qx", "r_state", "r_o", "r_y", "r_sq", "r_var", "ret_done"))
        k_z, k_abs, k_log, k_sp, k_sum, k_r, k_a, k_mask, k_o, k_y = (
            sem(n) for n in ("k_z", "k_abs", "k_log", "k_sp", "k_sum", "k_r", "k_a", "k_mask", "k_o", "k_y"))
        c_pos, c_h, c_hs, c_kv, c_kvs, c_s, c_sb, c_e, c_p, c_t, c_tb, c_o, c_y = (
            sem("c_%s" % n) for n in ("pos", "h", "hs", "kv", "kvs", "s", "sb", "e", "p", "t", "tb", "o", "y"))
        f_x, f_abs, f_log, f_c, f_ct, f_ci, f_bc, f_cb = (
            sem("f_%s" % n) for n in ("x", "abs", "log", "c", "ct", "ci", "bc", "cb"))
        conf_done, m_mean, m_cent, m_sq, m_var, m_std, m_hat, m_silu, m_pw, m_pool, m_pool_in, sc_done, pl_in, pl_done = (
            sem(n) for n in ("conf_done", "m_mean", "m_cent", "m_sq", "m_var", "m_std", "m_hat", "m_silu", "m_pw",
                             "m_pool", "m_pool_in", "sc_done", "pl_in", "pl_done"))
        pe_order = sem("pe_order")
        res_added, t_ready, napplied, mix_src, m_pw_in = (
            sem(n) for n in ("res_added", "t_ready", "napplied", "mix_src", "m_pw_in"))

        nblocks = len(BLOCKS)

        def wait_evacuated(eng, name, extra=0):
            g = TILE[name] + extra
            eng.wait_ge(slot_free[g % 2], g // 2 + 1)

        def wait_tile(eng, g):
            eng.wait_ge(tile_done, g + 1)

        LAST_USE = {1: last_tile(INDEX["Am7"]), 2: last_tile(INDEX["o7"]), 3: last_tile(INDEX["Ep1"]),
                    4: last_tile(INDEX["x7"]), 5: last_tile(INDEX["u%d_%d" % (NEIGHTH - 1, UPS - 1)])}

        def operand_version(name):
            if name[0] in "DBCA":
                return 0
            return {"o": 1, "E": 2, "x": 3, "u": 4, "g": 5}[name[0]]

        def flat(t):
            a = t[:]
            return a.rearrange("p a b -> p (a b)") if len(a.shape) == 3 else a

        dtab = rtab[:, 0:4 * P]
        xi = rtab[:, 4 * P:6 * P].rearrange("p (t q) -> p t q", t=2)
        zt = rtab[:, 6 * P:8 * P].rearrange("p (t q) -> p t q", t=2)
        block = ctx.enter_context(nc.Block())

        @block.sync
        def _(sp):
            sp.dma_start(vec[:], vecs).then_inc(small_in, 16)
            sp.dma_start(tab[:], tables).then_inc(small_in, 16)
            sp.dma_start(ada1[:], wada[1]).then_inc(ada_in[1], 16)
            sp.dma_start(mm[:], xT).then_inc(x_in, 16)
            sp.dma_start(ada0[:], wada[0]).then_inc(ada_in[0], 16)
            sp.dma_start(ada2[:], wada[2]).then_inc(ada_in[2], 16)
            sp.dma_start(rtab[:], rtables).then_inc(rtab_in, 16)

            def load_weights(b):
                if b >= 1:
                    sp.wait_ge(w_lo, b)
                n = BLOCK_LEN[b]
                src = wstream[BLOCK_OFF[b]:BLOCK_OFF[b] + P * n].rearrange("(p n) -> p n", p=P)
                sp.dma_start(raw[:, 0:n], src).then_inc(raw_in, 16)

            load_weights(0)
            for ev in TIMELINE:
                if ev[0] == "dense" and ev[2] == 1 and ev[1] + 1 < nblocks:
                    load_weights(ev[1] + 1)
                elif ev == ("cmp", 0):
                    sp.wait_ge(k_y, H)
                    sp.dma_start(cw1s[:], cw1).then_inc(cmp_in, 16)
                    sp.dma_start(cw2s[:], cw2).then_inc(cmp_in, 16)
                elif ev[0] == "split_merged":
                    for n in range(NC):
                        sp.wait_ge(x_lo, 8 + n + 1)
                        sp.dma_start(mm[:, n, :], xT[:, n, :]).then_inc(xres_in, 16)
                elif ev[0] == "norm2":
                    for n in range(NC):
                        sp.wait_ge(chunk_ready, n + 1)
                        sp.dma_start(res_dram[:, n, :], mm[:, n, :]).then_inc(res_out, 16)
                elif ev[0] == "mix":
                    sp.wait_ge(pl_done, 2)
                    sp.dma_start(wpws[:], wpw).then_inc(pw_in, 16)
                    sp.dma_start(wpls[:], wpool).then_inc(pw_in, 16)
                elif ev[0] == "dense" and ev[2] == 0 and BLOCKS[ev[1]][1] == "x1":
                    sp.wait_ge(res_out, 16 * NC)
                    wait_tile(sp, TILE["yE1"])
                    sp.wait_ge(x_lo, 32)
                    for n in range(NC):
                        sp.dma_start(res[:, n, :], res_dram[:, n, :]).then_inc(res_in, 16)
                elif ev[0] == "norm4":
                    wait_tile(sp, last_tile(INDEX["d%d_%d" % (NEIGHTH - 1, NC // 2 - 1)]))
                    for n in range(2):
                        sp.dma_start(zs2[n][:], pT[:, n, :]).then_inc(p_in, 16)
                elif ev[0] == "norm5":
                    for n in range(NC):
                        sp.wait_ge(res_added, 2 * NC + n + 1)
                        sp.dma_start(out[:, n, :], res[:, n, :]).then_inc(out_done, 16)
            sp.wait_ge(out_done, 16 * NC)

        @block.tensor
        def _(pe):
            mm_ = nc.tensor.matmul
            order = [0]

            def ordered(ins):
                order[0] += 1
                ins.then_inc(pe_order, 1)
                pe.wait_ge(pe_order, order[0])

            def wait_slot(g):
                if g >= 2:
                    pe.wait_ge(slot_free[g % 2], g // 2)

            def three(outs, k_w, k_x, b, hi, lo, first, last):
                for j, (w, x) in enumerate(((whi, hi), (whi, lo), (wlo, hi))):
                    for half in range(2):
                        o = mm_(outs[:, half * HALF:(half + 1) * HALF], w[b % 2][:, k_w, :],
                                x[:, k_x, half * HALF:(half + 1) * HALF],
                                start=first and j == 0, stop=last and j == 2)
                return o

            def dense(b, part):
                kind, name, n = BLOCKS[b]
                g = TILE[name]
                if part == 0:
                    pe.wait_ge(w_lo, b + 1)
                    wait_slot(g)
                v = None if kind == "D" else operand_version(name)
                first_of_version = name in ("Dq0", "o0", "Eq0", "x0", "u0_0", "g0")
                out_ = slot[g % 2]
                if kind in "FM":
                    for kc in (2 * part, 2 * part + 1):
                        if first_of_version:
                            pe.wait_ge(x_lo, 8 * v + (8 if v == 3 else kc + 1))
                        o = three(out_, kc, kc, b, xhi, xlo, kc == 0, kc == 7)
                    if part == 3:
                        o.then_inc(tile_done, 1)
                        if kind == "M":
                            wait_slot(g + 1)
                            r = BRANCHES.index(name[0]) if name[0] in BRANCHES else 4
                            pe.wait_ge(y_lo, 2 * r + 2)
                            for kc in range(2):
                                o = three(slot[(g + 1) % 2], 8 + kc, kc, b, yhi, ylo, kc == 0, kc == 1)
                            o.then_inc(tile_done, 1)
                elif kind == "T":
                    w_h = whi[b % 2][:].rearrange("p a b -> p (a b)")[:, 0:8 * n].rearrange("p (k n) -> p k n", k=8)
                    w_l = wlo[b % 2][:].rearrange("p a b -> p (a b)")[:, 0:8 * n].rearrange("p (k n) -> p k n", k=8)
                    for tb in (2 * part, 2 * part + 1):
                        for kc in range(8):
                            for j, (x, w) in enumerate(((xhi, w_h), (xhi, w_l), (xlo, w_h))):
                                o = mm_(out_[:, tb * n:(tb + 1) * n], x[:, kc, tb * P:(tb + 1) * P], w[:, kc, :],
                                        start=kc == 0 and j == 0, stop=kc == 7 and j == 2)
                    if part == 3:
                        o.then_inc(tile_done, 1)
                else:
                    e = int(name[1:].split("_")[0])
                    t = part // 2
                    if part == 2:
                        wait_slot(g + 1)
                    if part == 0:
                        pe.wait_ge(u_lo, UPS * (e + 1))
                    w_h = whi[b % 2][:, 0:8, :].rearrange("p (k t) n -> p k t n", k=4)
                    w_l = wlo[b % 2][:, 0:8, :].rearrange("p (k t) n -> p k t n", k=4)
                    for kc in (2 * (part % 2), 2 * (part % 2) + 1):
                        for j, (w, x) in enumerate(((w_h, uhi), (w_h, ulo), (w_l, uhi))):
                            for half in range(2):
                                o = mm_(slot[(g + t) % 2][:, half * HALF:(half + 1) * HALF], w[:, kc, t, :],
                                        x[:, kc, half * HALF:(half + 1) * HALF],
                                        start=kc == 0 and j == 0, stop=kc == 3 and j == 2)
                    if part % 2 == 1:
                        o.then_inc(tile_done, 1)

            def ytrans(g, n):
                wait_slot(g)
                for tb in range(NB):
                    o = nc.tensor.transpose(slot[g % 2][:, tb * P:(tb + 1) * P], ytok[:, tb, n * P:(n + 1) * P],
                                            t_("ident"))
                o.then_inc(tile_done, 1)

            def column_sum(k):
                pe.wait_ge(sq_added, 7 * (k + 1))
                if k:
                    pe.wait_ge(nstd, k)
                for half in range(2):
                    o = mm_(psb[half], t_("ones"), pbuf[0][:, half * HALF:(half + 1) * HALF], start=True, stop=True)
                o.then_inc(nsum, 1)

            def retention(n):
                if n < NB:
                    if n == 0:
                        wait_evacuated(pe, "Dt1")
                        wait_evacuated(pe, "Dt0")
                    if n >= 2:
                        pe.wait_ge(r_st, n - 1)
                    for h in (0, 2, 1, 3):
                        if h == 1:
                            ordered(o)
                        r0 = DH * (h % 2)
                        o = mm_(psb[n % 2][:, h * P:(h + 1) * P], dk[r0:r0 + DH, h // 2, n * P:(n + 1) * P],
                                dq[r0:r0 + DH, h // 2, n * P:(n + 1) * P], start=True, stop=True)
                    if n >= 1:
                        pe.wait_ge(r_state, min(n, NB - 1))
                    if n < NB - 1:
                        for h in range(H):
                            r0 = DH * (h % 2)
                            o = mm_(ps6[r0:r0 + DH, (h // 2) * DH:(h // 2 + 1) * DH],
                                    dt_[:, h // 2, n, r0:r0 + DH], dv[:, h // 2, n, r0:r0 + DH],
                                    start=True, stop=True)
                    o.then_inc(r_s, 1)
                if n >= 1:
                    m = n - 1
                    pe.wait_ge(r_st, m + 1)
                    if m >= 1:
                        pe.wait_ge(r_qx, m)
                        pe.wait_ge(r_state, m)
                    if m >= 1:
                        pe.wait_ge(r_y, m)
                    for h in (0, 2, 1, 3):
                        if h == 1:
                            ordered(o)
                        r0 = DH * (h % 2)
                        oo = ps7[:, h * DH:(h + 1) * DH]
                        o = mm_(oo, sbuf[m % 2][:, h * P:(h + 1) * P], dv[:, h // 2, m, r0:r0 + DH],
                                start=True, stop=m == 0)
                        if m >= 1:
                            o = mm_(oo, pbuf[m % 2][r0:r0 + DH, (h // 2) * P:(h // 2 + 1) * P],
                                    rst[r0:r0 + DH, m, h // 2, :], start=False, stop=True)
                    o.then_inc(r_o, 1)

            def soft(u, first, count):
                if u < first + count:
                    ph, h, i, lo, nb = unit(u)
                    if u == first:
                        if ph == "SWA":
                            wait_evacuated(pe, "Bv0")
                            wait_evacuated(pe, "Bk1")
                            pe.wait_ge(masks_done, 1)
                            pe.wait_ge(ret_done, 1)
                        elif ph == "SEL":
                            pe.wait_ge(c_y, 4)
                        elif ph == "FGT":
                            wait_evacuated(pe, "Ef")
                            wait_evacuated(pe, "Ev1")
                    if u >= 1:
                        pe.wait_ge(s_biased, u)
                    r0 = DH * (h % 2)
                    kt = {"SWA": h // 2, "SEL": 0, "WIN": 1, "FGT": h // 2}[ph]
                    w = nb * P
                    low = (ph == "SWA" and i >= 1) or (ph == "WIN" and i >= 4)
                    for c0 in range(0, w, HALF):
                        c1 = min(w, c0 + HALF)
                        o = mm_(ps4[:, c0:c1], brq[r0:r0 + DH, h // 2, i * P:(i + 1) * P],
                                brk[r0:r0 + DH, kt, lo * P + c0:lo * P + c1], start=True, stop=True)
                        if low and c0 == 0:
                            o = mm_(ps4[:, 0:P], identb[:], lowb[:], start=False, stop=True, skip_group_check=True)
                        if ph == "FGT" and c1 == w:
                            o = mm_(ps4[:, w - P:w], identb[:], upb[:], start=False, stop=True,
                                    skip_group_check=True)
                    o.then_inc(s_scores, 1)
                m = u - 1
                if first <= m < first + count:
                    nb = unit(m)[4]
                    pe.wait_ge(s_exp, m + 1)
                    for bi in range(batches(m)):
                        done = BATCH_END[m] - batches(m) + bi
                        if done >= 1:
                            pe.wait_ge(s_ptsb, done)
                        for c in range(4 * bi, min(nb, 4 * bi + 4)):
                            o = nc.tensor.transpose(ps6[:, (c - 4 * bi) * P:(c - 4 * bi + 1) * P],
                                                    sbuf[m % 2][:, c * P:(c + 1) * P], t_("ident"))
                        o.then_inc(s_pt, 1)
                m = u - 2
                if first <= m < first + count:
                    ph, h, i, lo, nb = unit(m)
                    pe.wait_ge(s_ptsb, BATCH_END[m])
                    if m >= 1:
                        pe.wait_ge(s_norm, m)
                    for c in range(nb):
                        if ph == "SWA":
                            v = brv[:, 0, lo + c, DH * (h // 2):DH * (h // 2) + DH]
                        elif ph == "SEL":
                            v = brv[:, 0, lo + c, 0:DH]
                        elif ph == "WIN":
                            v = brv[:, 0, lo + c, DH:2 * DH]
                        else:
                            v = brv[:, h // 2, lo + c, DH * (h % 2):DH * (h % 2) + DH]
                        o = mm_(ps7[:, 0:DH], pbuf[m % 2][:, c * P:(c + 1) * P], v,
                                start=c == 0, stop=c == nb - 1)
                    o.then_inc(s_out, 1)

            def stick(s):
                if s < NSTICK:
                    h, half, j = STICK[s]
                    c0 = stick_q0(s)
                    r0 = DH * (h % 2)
                    if s == 0:
                        wait_evacuated(pe, "Cv1")
                        wait_evacuated(pe, "Cv0")
                        pe.wait_ge(s_norm, NSWA)
                    if s >= 2:
                        pe.wait_ge(k_a, s - 1)
                    mm_(psb[s % 2][:, c0:HALF], brk[r0:r0 + DH, h // 2, j * P:(j + 1) * P],
                        brq[r0:r0 + DH, h // 2, half * HALF + c0:(half + 1) * HALF],
                        start=True, stop=True).then_inc(k_z, 1)
                if 1 <= s <= NSTICK:
                    m = s - 1
                    h, half, j = STICK[m]
                    c0 = stick_q0(m)
                    first = j == 4 * half + 3
                    pe.wait_ge(k_sp, m + 1)
                    o = mm_(psb[m % 2][:, c0:HALF], t_("tri"), skt[m % 2][:, c0:HALF], start=False, stop=first,
                            skip_group_check=True)
                    if not first:
                        pe.wait_ge(k_sum, m)
                        o = mm_(psb[m % 2][:, c0:HALF], t_("negones"), skl[m % 2][:, c0:HALF], start=False,
                                stop=True, skip_group_check=True)
                    o.then_inc(k_r, 1)
                if s >= 2:
                    m = s - 2
                    h, half, j = STICK[m]
                    c0 = stick_q0(m)
                    pe.wait_ge(k_a, m + 1)
                    pe.wait_ge(k_mask, DIAG_COUNT[m])
                    if half == 0 and j == 3 and h >= 2:
                        pe.wait_ge(k_y, h - 1)
                    for i in range(c0 // P, 4):
                        qb = 4 * half + i
                        o = mm_(pso[h % 2][:, qb * DH:(qb + 1) * DH], ska[m % 2][:, i * P:(i + 1) * P],
                                brv[:, h // 2, j, DH * (h % 2):DH * (h % 2) + DH],
                                start=(half == 0 and j == 3 and i == 3), stop=(half == 1 and j == 0 and i == 3),
                                skip_group_check=True)
                    o.then_inc(k_o, 1)

            def compress(s):
                if s == 0:
                    pe.wait_ge(cmp_in, 32)
                    pe.wait_ge(c_pos, 1)
                    for j in range(2):
                        zt = acmp[j * DH:(j + 1) * DH, :].rearrange("d (c l) -> d l c", l=32)
                        for l in range(32):
                            o = mm_(psb[j][0:DH, 0:NCMP], cw1s[j * DH:(j + 1) * DH, l, :], zt[:, l, :],
                                    start=l == 0, stop=l == 31)
                    o.then_inc(c_h, 1)
                elif s == 1:
                    pe.wait_ge(c_hs, 2)
                    mm_(ps6[:, 0:NCMP], cw2s[:, 0:2 * DH], hsil[:, 0:NCMP], start=True, stop=True)
                    mm_(ps7[:, 0:DH], hsil[:, NCMP:5 * NCMP], cw2s[:, 2 * DH:3 * DH],
                        start=True, stop=True).then_inc(c_kv, 1)
                elif s == 2:
                    pe.wait_ge(c_kvs, 2)
                    wait_evacuated(pe, "Aq0")
                    wait_evacuated(pe, "Aq1")
                    for h in (0, 2, 1, 3):
                        if h == 1:
                            ordered(o)
                        r0 = DH * (h % 2)
                        for i in range(NB):
                            c = h * NB * NCMP + i * NCMP
                            o = mm_(ps4[:, c:c + NCMP], brq[r0:r0 + DH, h // 2, i * P:(i + 1) * P],
                                    kct[r0:r0 + DH, :], start=True, stop=True)
                    o.then_inc(c_s, 1)
                elif s == 3:
                    pe.wait_ge(c_p, 1)
                    for half in range(2):
                        if half:
                            pe.wait_ge(c_tb, 1)
                        for c in range(4):
                            o = nc.tensor.transpose(ps6[:, c * P:(c + 1) * P],
                                                    sbuf[0][:, half * HALF + c * P:half * HALF + (c + 1) * P],
                                                    t_("ident"))
                        o.then_inc(c_t, 1)
                elif s == 4:
                    pe.wait_ge(c_tb, 2)
                    for h in range(H):
                        if h:
                            pe.wait_ge(c_y, h)
                        for i in (0, 4, 1, 5, 2, 6, 3, 7):
                            if 0 < i < 4:
                                ordered(o)
                            r0 = 32 * (i % 4)
                            c = (h * 2 + i // 4) * P
                            o = mm_(ps7[:, i * DH:(i + 1) * DH], pbuf[1][r0:r0 + 32, c:c + P],
                                    vc4[r0:r0 + 32, :], start=True, stop=True, tile_position=(r0, 0))
                        o.then_inc(c_o, 1)

            def forget_prep(s):
                if s == 0:
                    pe.wait_ge(f_c, 1)
                    for tb in range(NB):
                        o = nc.tensor.transpose(ps7[:, tb * 4:tb * 4 + 4], ct[0:4, tb * P:(tb + 1) * P],
                                                t_("ident")[0:4, 0:4])
                    o.then_inc(f_ct, 1)

            pe.wait_ge(small_in, 32)
            pe.wait_ge(csil_done, 1)
            for t, a in ((1, ada1), (0, ada0), (2, ada2)):
                pe.wait_ge(ada_in[t], 16)
                for n in range(NC):
                    for kc in range(8):
                        o = mm_(ps6[:, 8 * t + n:8 * t + n + 1], a[:, kc, n * P:(n + 1) * P], csil[:, kc:kc + 1],
                                start=kc == 0, stop=kc == 7)
                if t == 1:
                    column_sum(0)
            o.then_inc(mod_mm, 1)

            for ev in TIMELINE:
                if ev[0] == "dense":
                    dense(ev[1], ev[2])
                elif ev[0] == "ytrans":
                    if ev[2] == 0:
                        if ev[1] == "D":
                            pe.wait_ge(ret_done, 1)
                        elif ev[1] == "B":
                            pe.wait_ge(s_norm, NSWA)
                        elif ev[1] == "C":
                            pe.wait_ge(k_y, H)
                        else:
                            pe.wait_ge(s_norm, NSWA + NSEL + NWIN)
                    ytrans(TILE["y%s%d" % (ev[1], ev[2])], ev[2])
                elif ev[0] == "ret":
                    retention(ev[1])
                elif ev[0] == "soft":
                    if ev[2] == U_FGT and ev[1] < U_FGT + NFGT and unit(ev[1])[2] == 0:
                        h = unit(ev[1])[1]
                        if h == 0:
                            pe.wait_ge(f_ci, 1)
                            wait_evacuated(pe, "Ef")
                        pe.wait_ge(s_biased, ev[1])
                        for half in range(2):
                            o = mm_(psb[half], t_("ident")[0:4, h:h + 1].to_broadcast([4, P]), ct[0:4, half * HALF:(half + 1) * HALF],
                                    start=True, stop=True)
                        o.then_inc(f_bc, 1)
                        pe.wait_ge(f_cb, h + 1)
                    soft(ev[1], ev[2], ev[3])
                elif ev[0] == "stick":
                    stick(ev[1])
                elif ev[0] == "cmp":
                    compress(ev[1])
                elif ev[0] == "fprep":
                    forget_prep(ev[1])
                elif ev[0] == "norm2":
                    column_sum(1)
                    column_sum(2)
                elif ev[0] == "norm3":
                    column_sum(3)
                    column_sum(4)
                elif ev[0] == "norm4":
                    column_sum(5)
                    column_sum(6)
                elif ev[0] == "norm5":
                    column_sum(7)
                elif ev[0] == "mix":
                    pe.wait_ge(s_norm, 128)
                    for n in range(2):
                        ytrans(TILE["yE%d" % n], n)
                    pe.wait_ge(pw_in, 32)
                    pe.wait_ge(pl_done, 2)
                    for t in range(2):
                        if t:
                            pe.wait_ge(m_pool_in, 1)
                        for half in range(2):
                            o = mm_(psb[half], wpls[:, t, :], ply[:, t, half * HALF:(half + 1) * HALF],
                                    start=True, stop=True)
                        o.then_inc(m_pool, 1)
                    pe.wait_ge(m_pool_in, 2)
                    for t in range(2):
                        pe.wait_ge(conf_done, 2)
                        for half in range(2):
                            o = mm_(psb[half], t_("ones"), cacc[:, t, half * HALF:(half + 1) * HALF],
                                    start=t == 0, stop=t == 1)
                    o.then_inc(m_mean, 1)
                    pe.wait_ge(m_sq, 2)
                    for t in range(2):
                        for half in range(2):
                            o = mm_(psb[half], t_("ones"), sbuf[t][:, half * HALF:(half + 1) * HALF],
                                    start=t == 0, stop=t == 1)
                    o.then_inc(m_var, 1)
                    pe.wait_ge(m_silu, 2)
                    for n in range(2):
                        if n:
                            pe.wait_ge(m_pw_in, 1)
                        for t in range(2):
                            for half in range(2):
                                o = mm_(psb[half], wpws[:, t, n * P:(n + 1) * P],
                                        cacc[:, t, half * HALF:(half + 1) * HALF], start=t == 0, stop=t == 1)
                        o.then_inc(m_pw, 1)

        @block.scalar
        def _(act):
            def split_weights(b):
                act.wait_ge(raw_in, 16 * (b + 1))
                if b >= 2:
                    wait_tile(act, last_tile(b - 2))
                n = BLOCK_LEN[b]
                nc.scalar.activation(flat(whi[b % 2])[:, 0:n], raw[:, 0:n], ACT.Copy).then_inc(w_hi, 1)

            def split_wide(k, src):
                nc.scalar.activation(xhi[:, k, :], src, ACT.Copy).then_inc(x_hi, 1)

            def square(k, n, src):
                if n == 0 and k:
                    act.wait_ge(nsum, k)
                if n >= 3:
                    act.wait_ge(sq_added, 7 * k + n - 2)
                dst = pbuf[0] if n == 0 else sbuf[n % 2]
                nc.scalar.activation(dst[:], src, ACT.Square).then_inc(sq_done, 1)

            def std(k):
                act.wait_ge(nsum, k + 1)
                if k:
                    act.wait_ge(napplied, k)
                nc.scalar.activation(pbuf[1][:], ps4[:], ACT.Sqrt, bias=t_("eps6"), scale=1.0 / D).then_inc(nstd, 1)

            def evacuate(b):
                kind, name, n = BLOCKS[b]
                g = TILE[name]
                if name[0] in "DBCAE" and name[1] in "qk" and name[2:] in ("0", "1"):
                    wait_tile(act, g)
                    t = int(name[2])
                    q = name[1] == "q"
                    dst = ((dq if q else dk) if name[0] == "D" else (brq if q else brk))[:, t, :]
                    nc.scalar.activation(dst, slot[g % 2][:], ACT.Copy,
                                         scale=QSCALE if q else 1.0).then_inc(slot_free[g % 2], 1)
                elif name == "Acmp":
                    wait_tile(act, g)
                    nc.scalar.activation(acmp[:], slot[g % 2][:], ACT.Copy).then_inc(slot_free[g % 2], 1)
                elif name == "Agates":
                    wait_tile(act, g)
                    nc.scalar.activation(flat(gates), slot[g % 2][:, 0:NB * 12], ACT.Sigmoid
                                         ).then_inc(slot_free[g % 2], 1)
                elif name[0] in "DBCA" and name[1] == "z":
                    r, t = BRANCHES.index(name[0]), int(name[2])
                    wait_tile(act, g)
                    if r == 1:
                        wait_evacuated(act, "Dm%d" % (6 + t), 1)
                    elif r >= 2:
                        act.wait_ge(sum_done, 8 * (r - 2) + 6 + t + 1)
                    nc.scalar.activation(zs[t][:], slot[g % 2][:], ACT.Silu).then_inc(slot_free[g % 2], 1)
                elif name[0] in "DBCA" and name[1] == "m":
                    r, n = BRANCHES.index(name[0]), int(name[2])
                    wait_tile(act, g)
                    if n < 2:
                        act.wait_ge(y_lo, 2 * r + n + 1)
                    elif r == 0:
                        wait_evacuated(act, "Dm%d" % (n - 2), 1)
                    else:
                        act.wait_ge(sum_done, 8 * (r - 1) + n - 1)
                    nc.scalar.activation(zs[n % 2][:], slot[g % 2][:], ACT.Sigmoid).then_inc(slot_free[g % 2], 1)
                elif name[0] == "o":
                    wait_evacuated(act, name)
                    n = int(name[1])
                    square(1, n, mm[:, n, :])
                elif name == "Ef":
                    wait_tile(act, g)
                    nc.scalar.activation(ct[0:4, :], slot[g % 2][0:4, :], ACT.Identity, bias=v_("bf")[0:4, :]
                                         ).then_inc(slot_free[g % 2], 1)
                    act.wait_ge(f_abs, 1)
                    nc.scalar.activation(cb[0:4, :], cb[0:4, :], ACT.Exp, scale=-1.0).then_inc(act_chain, 1)
                    act.wait_ge(act_chain, NSTICK + 1)
                    nc.scalar.activation(cb[0:4, :], cb[0:4, :], ACT.Ln, bias=1.0).then_inc(f_log, 1)
                elif name in ("Ecb0", "Ecb1", "Esh0", "Esh1"):
                    wait_tile(act, g)
                    if name == "Ecb1":
                        wait_evacuated(act, "Eca0")
                    if name == "Esh1":
                        wait_evacuated(act, "Esc0")
                    z, f = (zs[0], ACT.Sigmoid) if name[1] == "c" else (zs[1], ACT.Copy)
                    nc.scalar.activation(z[:], slot[g % 2][:], f).then_inc(slot_free[g % 2], 1)
                elif name in ("Ep0", "Ep1"):
                    wait_tile(act, g)
                    if name == "Ep1":
                        wait_evacuated(act, "Esb1")
                    nc.scalar.activation((sx if name == "Ep0" else su)[:], slot[g % 2][:], ACT.Copy
                                         ).then_inc(slot_free[g % 2], 1)
                elif name[0] == "x":
                    n = int(name[1])
                    wait_tile(act, g)
                    if n == 0:
                        act.wait_ge(x_lo, 32)
                    nc.scalar.activation(mm[:, n, :], slot[g % 2][:], ACT.Copy).then_inc(slot_free[g % 2], 1)
                    wait_evacuated(act, name)
                    square(3, n, mm[:, n, :])
                elif name[0] == "u":
                    e, n = (int(v) for v in name[1:].split("_"))
                    if e and n == 0:
                        wait_tile(act, last_tile(INDEX["d%d_%d" % (e - 1, NC // 2 - 1)]))
                    act.wait_ge(u_src, UPS * e + n + 1)
                    nc.scalar.activation(uhi[:, n, :], tbuf[n % 2][:], ACT.Copy).then_inc(u_hi, 1)
                elif name[0] == "d":
                    e, m = (int(v) for v in name[1:].split("_"))
                    for t in range(2):
                        n, gg = 2 * m + t, g + t
                        if e == 0:
                            wait_tile(act, gg)
                            nc.scalar.activation(mm[:, n, :], slot[gg % 2][:], ACT.Copy
                                                 ).then_inc(slot_free[gg % 2], 1)
                elif name[0] == "g":
                    n = int(name[1])
                    wait_tile(act, g)
                    if n < 2:
                        act.wait_ge(y_lo, 10)
                    else:
                        wait_evacuated(act, "g%d" % (n - 2), 1)
                    nc.scalar.activation(zs2[n % 2][:], slot[g % 2][:], ACT.Sigmoid).then_inc(slot_free[g % 2], 1)
                    wait_evacuated(act, name, 1)
                    square(7, n, mm[:, n, :])

            def soft(u, first, count):
                m = u - 1
                if first <= m < first + count:
                    nb = unit(m)[4]
                    if m >= 2:
                        act.wait_ge(s_out, m - 1)
                    for bi in range(batches(m)):
                        act.wait_ge(s_pt, BATCH_END[m] - batches(m) + bi + 1)
                        w = P * (min(nb, 4 * bi + 4) - 4 * bi)
                        nc.scalar.activation(pbuf[m % 2][:, bi * HALF:bi * HALF + w], ps6[:, 0:w], ACT.Copy
                                             ).then_inc(s_ptsb, 1)
                if u < first + count:
                    ph, h, i, lo, nb = unit(u)
                    act.wait_ge(s_negmax, u + 1)
                    if ph == "SWA":
                        nc.scalar.activation(esk[:, u % 4:u % 4 + 1], v_("sink", h, 1), ACT.Exp,
                                             bias=nmx[:, u % 4:u % 4 + 1]).then_inc(s_esk, 1)
                    w = nb * P
                    nc.scalar.activation(sbuf[u % 2][:, 0:w], sbuf[u % 2][:, 0:w], ACT.Exp,
                                         bias=nmx[:, u % 4:u % 4 + 1],
                                         accum_out=den[:, u % 4:u % 4 + 1]).then_inc(s_exp, 1)

            def stick(s):
                if s < NSTICK:
                    c0 = stick_q0(s)
                    t = skt[s % 2][:, c0:HALF]
                    act.wait_ge(k_abs, s + 1)
                    nc.scalar.activation(t, t, ACT.Exp, scale=-1.0).then_inc(act_chain, 1)
                    act.wait_ge(act_chain, s + 1)
                    nc.scalar.activation(t, t, ACT.Ln, bias=1.0).then_inc(k_log, 1)
                if 1 <= s <= NSTICK:
                    m = s - 1
                    c0 = stick_q0(m)
                    act.wait_ge(k_r, m + 1)
                    if m >= 2:
                        act.wait_ge(k_o, m - 1)
                    nc.scalar.activation(ska[m % 2][:, c0:HALF], psb[m % 2][:, c0:HALF], ACT.Exp).then_inc(k_a, 1)

            act.wait_ge(small_in, 32)
            nc.scalar.activation(csil[:], v_("c"), ACT.Silu).then_inc(csil_done, 1)
            act.wait_ge(x_in, 16)
            for n in range(NC):
                square(0, n, mm[:, n, :])
            split_weights(0)
            for ev in TIMELINE:
                if ev[0] == "dense":
                    if ev[2] == 0 and ev[1] + 1 < nblocks:
                        split_weights(ev[1] + 1)
                    if ev[2] == 3:
                        evacuate(ev[1])
                elif ev[0] == "ytrans":
                    br, n = ev[1], ev[2]
                    r = BRANCHES.index(br)
                    wait_evacuated(act, "y%s%d" % (br, n))
                    if r:
                        wait_tile(act, last_tile(INDEX[BRANCHES[r - 1] + "m7"]))
                    nc.scalar.activation(yhi[:, n, :], zs[n][:], ACT.Copy).then_inc(y_hi, 1)
                elif ev[0] == "retnorm":
                    act.wait_ge(r_var, 1)
                    nc.scalar.activation(st32[:, 2, :], st32[:, 1, :], ACT.Sqrt, bias=t_("eps5"),
                                         scale=1.0 / DH).then_inc(r_sq, 1)
                elif ev[0] == "soft":
                    if ev[2] == U_FGT and ev[1] < U_FGT + NFGT and unit(ev[1])[2] == 0:
                        h = unit(ev[1])[1]
                        act.wait_ge(f_bc, h + 1)
                        nc.scalar.activation(cb[:], ps4[:], ACT.Copy).then_inc(f_cb, 1)
                    soft(ev[1], ev[2], ev[3])
                elif ev[0] == "stick":
                    stick(ev[1])
                elif ev[0] == "cmp":
                    if ev[1] == 1:
                        act.wait_ge(c_h, 1)
                        nc.scalar.activation(hsil[:, 0:NCMP], psb[0][0:DH, 0:NCMP], ACT.Silu).then_inc(c_hs, 1)
                        nc.scalar.activation(hsil[:, NCMP:].rearrange("p (a c) -> p a c", a=4),
                                             psb[1][0:DH, 0:NCMP].unsqueeze(1).to_broadcast([DH, 4, NCMP]), ACT.Silu
                                             ).then_inc(c_hs, 1)
                        act.wait_ge(c_kv, 1)
                        nc.scalar.activation(kct[:], ps6[:, 0:NCMP], ACT.Copy).then_inc(c_kvs, 1)
                        nc.scalar.activation(vc4[:], ps7[:, 0:DH], ACT.Copy).then_inc(c_kvs, 1)
                    elif ev[1] == 2:
                        act.wait_ge(c_sb, 1)
                        nc.scalar.activation(sbuf[0][:], sbuf[0][:], ACT.Exp).then_inc(c_e, 1)
                    elif ev[1] == 3:
                        for half in range(2):
                            act.wait_ge(c_t, half + 1)
                            nc.scalar.activation(pbuf[1][:, half * HALF:(half + 1) * HALF], ps6[:], ACT.Copy
                                                 ).then_inc(c_tb, 1)
                elif ev[0] == "fprep":
                    act.wait_ge(f_ct, 1)
                    nc.scalar.activation(flat(ci), ps7[:, 0:4 * NB], ACT.Copy).then_inc(f_ci, 1)
                elif ev[0] == "norm1":
                    std(0)
                    act.wait_ge(mod_mm, 1)
                    for n in range(NC):
                        act.wait_ge(x_src, n + 1)
                        split_wide(n, mm[:, n, :])
                elif ev[0] == "split_merged":
                    wait_tile(act, LAST_USE[1])
                    for n in range(NC):
                        act.wait_ge(sum_done, 16 + n + 1)
                        split_wide(n, mm[:, n, :])
                elif ev[0] == "norm2":
                    std(1)
                    for n in range(NC):
                        act.wait_ge(chunk_ready, n + 1)
                        square(2, n, mm[:, n, :])
                    std(2)
                    wait_tile(act, LAST_USE[2])
                    for n in range(NC):
                        act.wait_ge(x_src, 8 + n + 1)
                        split_wide(n, res[:, n, :])
                elif ev[0] in ("norm3", "norm4"):
                    k = 3 if ev[0] == "norm3" else 5
                    if k == 5:
                        for n in range(2):
                            wait_evacuated(act, "d%d_%d" % (NEIGHTH - 1, NC // 2 - 1), n)
                        for n in range(NC):
                            square(5, n, mm[:, n, :])
                    std(k)
                    for n in range(NC):
                        act.wait_ge(res_added, 8 * (k == 5) + n + 1)
                        square(k + 1, n, res[:, n, :])
                    std(k + 1)
                    wait_tile(act, LAST_USE[4 if k == 3 else 5])
                    for n in range(NC):
                        act.wait_ge(x_src, 16 + 8 * (k == 5) + n + 1)
                        split_wide(n, mm[:, n, :])
                    if k == 5:
                        act.wait_ge(p_in, 32)
                        for n in range(2):
                            nc.scalar.activation(yhi[:, n, :], zs2[n][:], ACT.Copy).then_inc(y_hi, 1)
                elif ev[0] == "norm5":
                    std(7)
                elif ev[0] == "mix":
                    wait_tile(act, LAST_USE[3])
                    act.wait_ge(sc_done, 2)
                    for t in range(2):
                        split_wide(4 + t, scy[:, t, :])
                    for t in range(2):
                        act.wait_ge(mix_src, 1 + t)
                        split_wide(2 + t, pbuf[t][:])
                    for t in range(2):
                        act.wait_ge(mix_src, 3 + t)
                        split_wide(6 + t, ply[:, t, :])
                    for t in range(2):
                        act.wait_ge(m_cent, t + 1)
                        nc.scalar.activation(sbuf[t][:], cacc[:, t, :], ACT.Square).then_inc(m_sq, 1)
                    act.wait_ge(m_var, 1)
                    act.wait_ge(pl_done, 2)
                    nc.scalar.activation(sx[:], ps4[:], ACT.Sqrt, bias=t_("eps6"), scale=1.0 / BW).then_inc(m_std, 1)
                    for t in range(2):
                        act.wait_ge(m_hat, t + 1)
                        nc.scalar.activation(cacc[:, t, :], cacc[:, t, :], ACT.Silu, bias=v_("ln_b", t, 1),
                                             scale=v_("ln_g", t, 1)).then_inc(m_silu, 1)
                    for t in range(2):
                        act.wait_ge(mix_src, 5 + t)
                        split_wide(t, cu[:, t, :])

        @block.gpsimd
        def _(pool):
            tt = nc.gpsimd.tensor_tensor

            def split_weights(b):
                n = BLOCK_LEN[b]
                pool.wait_ge(w_hi, b + 1)
                tt(flat(wlo[b % 2])[:, 0:n], raw[:, 0:n], flat(whi[b % 2])[:, 0:n].bitcast(F32),
                   ALU.subtract).then_inc(w_lo, 1)

            wide = [0]

            def split_wide(k, src):
                wide[0] += 1
                pool.wait_ge(x_hi, wide[0])
                tt(xlo[:, k, :], src, xhi[:, k, :].bitcast(F32), ALU.subtract).then_inc(x_lo, 1)

            def add_square(k, n):
                if n:
                    pool.wait_ge(sq_done, 8 * k + n + 1)
                    if n > 1:
                        pool.wait_ge(sq_added, 7 * k + n - 1)
                    tt(pbuf[0][:], pbuf[0][:], sbuf[n % 2][:], ALU.add).then_inc(sq_added, 1)

            def split_narrow(n, src):
                pool.wait_ge(y_hi, n + 1)
                tt(ylo[:, n % 2, :], src, yhi[:, n % 2, :].bitcast(F32), ALU.subtract).then_inc(y_lo, 1)

            def add_residual(k):
                for n in range(NC):
                    pool.wait_ge(t_ready, 8 * k + n + 1)
                    if k == 0:
                        pool.wait_ge(res_in, 16 * NC)
                    tt(res[:, n, :], res[:, n, :], mm[:, n, :], ALU.add).then_inc(res_added, 1)

            chain = [0]

            def link(ins):
                chain[0] += 1
                ins.then_inc(pool_chain, 1)
                pool.wait_ge(pool_chain, chain[0])

            def window_sums(t):
                v = (sx, su)[t]
                wait_evacuated(pool, "Ep%d" % t)
                if t == 0:
                    wait_evacuated(pool, "Esc1")
                    wait_evacuated(pool, "Eca1")
                else:
                    pool.wait_ge(pl_done, 1)
                src = v
                for step in range(1 + 2 * t + 1):
                    last = step == 2 * t + 1
                    sh = 1 << step
                    dst = zs[step % 2]
                    link(nc.gpsimd.tensor_copy(dst[:, 0:sh], src[:, 0:sh]))
                    ins = tt(dst[:, sh:S], src[:, sh:S], src[:, 0:S - sh], ALU.add)
                    if last:
                        ins.then_inc(pl_in, 1)
                    else:
                        link(ins)
                    src = dst

            for n in range(NC):
                add_square(0, n)
            split_weights(0)
            for ev in TIMELINE:
                if ev[0] == "dense":
                    kind, name, _ = BLOCKS[ev[1]]
                    if ev[2] == 0 and ev[1] + 1 < nblocks:
                        split_weights(ev[1] + 1)
                    if ev[2] == 3:
                        if name[0] in "BCA" and name[1] == "m":
                            r, n = BRANCHES.index(name[0]), int(name[2])
                            wait_evacuated(pool, name, 1)
                            tt(mm[:, n, :], mm[:, n, :], zs[n % 2][:], ALU.add).then_inc(sum_done, 1)
                        elif name[0] == "o":
                            add_square(1, int(name[1]))
                        elif name[0] == "x":
                            add_square(3, int(name[1]))
                        elif name[0] == "u":
                            e, n = (int(v) for v in name[1:].split("_"))
                            pool.wait_ge(u_hi, UPS * e + n + 1)
                            tt(ulo[:, n, :], tbuf[n % 2][:], uhi[:, n, :].bitcast(F32), ALU.subtract
                               ).then_inc(u_lo, 1)
                        elif name[0] == "g":
                            add_square(7, int(name[1]))
                        elif name in ("Ep0", "Ep1"):
                            window_sums(int(name[2]))
                elif ev[0] == "ytrans":
                    r = BRANCHES.index(ev[1])
                    split_narrow(2 * r + ev[2], zs[ev[2]][:])
                elif ev[0] == "ret" and 1 <= ev[1] < NB:
                    n = ev[1]
                    if n == 1:
                        pool.wait_ge(rtab_in, 16)
                        wait_evacuated(pool, "Dq0")
                        wait_evacuated(pool, "Dq1")
                        pool.wait_ge(napplied, 1)
                    if n >= 2:
                        pool.wait_ge(r_o, n - 1)
                    tt(pbuf[n % 2][:, 0:2 * P].rearrange("p (t q) -> p t q", t=2), dq[:, :, n * P:(n + 1) * P],
                       xi, ALU.mult).then_inc(r_qx, 1)
                elif ev[0] == "stick":
                    m = ev[1] - 1
                    if 0 <= m < NSTICK:
                        h, half, j = STICK[m]
                        c0 = stick_q0(m)
                        pool.wait_ge(k_sp, m + 1)
                        if j == 4 * half + 3:
                            if m:
                                pool.wait_ge(k_r, m)
                            else:
                                pool.wait_ge(s_norm, NSWA)
                            link(nc.gpsimd.memset(skl[0][:], 0.0))
                            link(nc.gpsimd.memset(skl[1][:], 0.0))
                        elif m:
                            pool.wait_ge(k_r, m)
                            pool.wait_ge(k_sum, m)
                        tt(skl[(m + 1) % 2][:, c0:HALF], skl[m % 2][:, c0:HALF], skt[m % 2][:, c0:HALF],
                           ALU.add).then_inc(k_sum, 1)
                        if STICK_DIAG[m]:
                            pool.wait_ge(k_a, m + 1)
                            blk = ska[m % 2][:, c0:c0 + P]
                            nc.gpsimd.affine_select(out=blk, in_=blk, compare_op=ALU.is_gt, fill=0.0, base=0,
                                                    pattern=[[1, P]], channel_multiplier=-1).then_inc(k_mask, 1)
                elif ev[0] == "norm1":
                    for n in range(NC):
                        split_wide(n, mm[:, n, :])
                elif ev[0] == "split_merged":
                    for n in range(NC):
                        split_wide(n, mm[:, n, :])
                elif ev[0] == "norm2":
                    for n in range(NC):
                        add_square(2, n)
                    for n in range(NC):
                        split_wide(n, res[:, n, :])
                elif ev[0] in ("norm3", "norm4"):
                    k = 3 if ev[0] == "norm3" else 5
                    if k == 5:
                        for n in range(NC):
                            add_square(5, n)
                    add_residual((k - 3) // 2)
                    for n in range(NC):
                        add_square(k + 1, n)
                    for n in range(NC):
                        split_wide(n, mm[:, n, :])
                    if k == 5:
                        for n in range(2):
                            split_narrow(8 + n, zs2[n][:])
                elif ev[0] == "norm5":
                    add_residual(2)
                elif ev[0] == "mix":
                    for k, src in ((4, scy[:, 0, :]), (5, scy[:, 1, :]), (2, pbuf[0][:]), (3, pbuf[1][:]),
                                   (6, ply[:, 0, :]), (7, ply[:, 1, :]), (0, cu[:, 0, :]), (1, cu[:, 1, :])):
                        split_wide(k, src)

        @block.vector
        def _(dve):
            v = nc.vector
            chain = [0]

            def link(ins):
                chain[0] += 1
                ins.then_inc(dve_chain, 1)
                dve.wait_ge(dve_chain, chain[0])

            def rstd(k):
                dve.wait_ge(nstd, k + 1)
                link(v.reciprocal(pbuf[1][:], pbuf[1][:]))

            def scaled(dst, src, g, s_, last, k):
                ins = v.scalar_tensor_tensor(out=dst, in0=src, scalar=g, in1=pbuf[1][:], op0=ALU.mult, op1=ALU.mult)
                ins.then_inc(s_, 1)

            def applied(k, s_, n):
                dve.wait_ge(s_, n)
                v.tensor_copy(fac[:, 0:1], fac[:, 1:2]).then_inc(napplied, 1)

            def copy_out(name, dst, extra=0):
                g = TILE[name] + extra
                wait_tile(dve, g)
                v.tensor_copy(dst, slot[g % 2][:]).then_inc(slot_free[g % 2], 1)

            def evacuate(b):
                kind, name, n = BLOCKS[b]
                g = TILE[name]
                if name[0] in "DBCAE" and name[1] == "v":
                    t = int(name[2])
                    dst = (dv if name[0] == "D" else brv)[:, t, :, :].rearrange("p b n -> p (b n)")
                    copy_out(name, dst)
                elif name[0] == "D" and name[1] == "t":
                    t = int(name[2])
                    wait_tile(dve, g)
                    dve.wait_ge(rtab_in, 16)
                    v.tensor_tensor(dt_[:, t, :, :], slot[g % 2][:].rearrange("p (b n) -> p b n", b=NB),
                                    zt[:, t, :].unsqueeze(1).to_broadcast([P, NB, P]), ALU.mult
                                    ).then_inc(slot_free[g % 2], 1)
                elif name[0] in "DBCA" and name[1] == "m":
                    r, n = BRANCHES.index(name[0]), int(name[2])
                    wait_tile(dve, g + 1)
                    wait_evacuated(dve, name)
                    dst = mm[:, n, :] if r == 0 else zs[n % 2][:]
                    v.tensor_tensor(dst, slot[(g + 1) % 2][:], zs[n % 2][:], ALU.mult
                                    ).then_inc(slot_free[(g + 1) % 2], 1)
                elif name[0] == "o":
                    n = int(name[1])
                    wait_tile(dve, g)
                    dve.wait_ge(xres_in, 16 * NC)
                    v.scalar_tensor_tensor(out=mm[:, n, :], in0=slot[g % 2][:], scalar=mod[:, 16 + n:17 + n],
                                           in1=mm[:, n, :], op0=ALU.mult, op1=ALU.add).then_inc(slot_free[g % 2], 1)
                elif name == "Ef":
                    wait_evacuated(dve, "Ef")
                    v.tensor_scalar(cb[0:4, :].bitcast(I32), ct[0:4, :].bitcast(I32), 0x7FFFFFFF, None,
                                    ALU.bitwise_and).then_inc(f_abs, 1)
                    link(v.memset(pbuf[1][0:4, :], 1.0))
                    dve.wait_ge(f_log, 1)
                    link(v.scalar_tensor_tensor(out=pbuf[0][0:4, :], in0=ct[0:4, :], scalar=0.0, in1=cb[0:4, :],
                                                op0=ALU.min, op1=ALU.subtract))
                    v.tensor_tensor_scan(ct[0:4, :], pbuf[1][0:4, :], pbuf[0][0:4, :], 0.0, ALU.mult, ALU.add
                                         ).then_inc(f_c, 1)
                elif name in ("Eca0", "Eca1"):
                    t = int(name[3])
                    wait_tile(dve, g)
                    wait_evacuated(dve, "Ecb%d" % t)
                    v.tensor_tensor(cu[:, t, :], slot[g % 2][:], zs[0][:], ALU.mult).then_inc(slot_free[g % 2], 1)
                elif name in ("Esc0", "Esc1"):
                    t = int(name[3])
                    wait_tile(dve, g)
                    wait_evacuated(dve, "Esh%d" % t)
                    if t:
                        dve.wait_ge(sc_done, 1)
                    v.tensor_tensor(su[:], slot[g % 2][:], zs[1][:], ALU.mult).then_inc(slot_free[g % 2], 1)
                    wait_evacuated(dve, name)
                    link(v.tensor_scalar(scy[:, t, :], su[:], v_("sc", 3 * t + 2, 1), None, ALU.mult))
                    for k in (1, 0):
                        sh = 2 - k
                        link(v.scalar_tensor_tensor(out=scy[:, t, sh:S], in0=su[:, 0:S - sh],
                                                    scalar=v_("sc", 3 * t + k, 1), in1=scy[:, t, sh:S],
                                                    op0=ALU.mult, op1=ALU.add))
                elif name in ("Esb0", "Esb1"):
                    t = int(name[3])
                    wait_tile(dve, g)
                    v.tensor_tensor(scy[:, t, :], slot[g % 2][:], scy[:, t, :], ALU.mult
                                    ).then_inc(slot_free[g % 2], 1)
                    wait_evacuated(dve, name)
                    v.tensor_copy(fac[:, 0:1], fac[:, 1:2]).then_inc(sc_done, 1)
                elif name in ("Ep0", "Ep1"):
                    t = int(name[2])
                    vv = (sx, su)[t]
                    dve.wait_ge(pl_in, t + 1)
                    for r0, z in ((0, zs[0]), (DH, zs[1])):
                        rr = slice(r0, r0 + DH)
                        link(v.scalar_tensor_tensor(out=ply[rr, t, 16:S], in0=z[rr, 16:S],
                                                    scalar=t_("invw", t, 1)[rr, :], in1=vv[rr, 16:S],
                                                    op0=ALU.mult, op1=ALU.subtract))
                        link(v.tensor_tensor(ply[rr, t, 0:16], z[rr, 0:16], t_("invc", 16 * t, 16)[rr, :], ALU.mult))
                        ins = v.tensor_tensor(ply[rr, t, 0:16], ply[rr, t, 0:16], vv[rr, 0:16], ALU.subtract)
                        if r0:
                            ins.then_inc(pl_done, 1)
                        else:
                            link(ins)
                elif name[0] == "u":
                    e, n = (int(w) for w in name[1:].split("_"))
                    wait_tile(dve, g)
                    if UPS * e + n >= 2:
                        dve.wait_ge(u_lo, UPS * e + n - 1)
                    t = tbuf[n % 2]
                    v.tensor_scalar(t[:], slot[g % 2][:], 0.0, None, ALU.max).then_inc(slot_free[g % 2], 1)
                    wait_evacuated(dve, name)
                    v.tensor_tensor(t[:], t[:], t[:], ALU.mult).then_inc(u_src, 1)
                elif name[0] == "d":
                    e, m = (int(w) for w in name[1:].split("_"))
                    for t in range(2):
                        n, gg = 2 * m + t, g + t
                        if e:
                            wait_tile(dve, gg)
                            if e == 1:
                                wait_evacuated(dve, "d0_%d" % m, t)
                            v.tensor_tensor(mm[:, n, :], slot[gg % 2][:], mm[:, n, :], ALU.add
                                            ).then_inc(slot_free[gg % 2], 1)
                elif name[0] == "g":
                    n = int(name[1])
                    wait_tile(dve, g + 1)
                    wait_evacuated(dve, name)
                    if n == 0:
                        dve.wait_ge(x_lo, 48)
                    v.tensor_tensor(mm[:, n, :], slot[(g + 1) % 2][:], zs2[n % 2][:], ALU.mult
                                    ).then_inc(slot_free[(g + 1) % 2], 1)

            def soft(u, first, count):
                if u < first + count:
                    ph, h, i, lo, nb = unit(u)
                    w = nb * P
                    dve.wait_ge(s_scores, u + 1)
                    if u >= 2:
                        dve.wait_ge(s_pt, BATCH_END[u - 2])
                    if ph == "FGT":
                        dve.wait_ge(f_cb, h + 1)
                        v.scalar_tensor_tensor(out=sbuf[u % 2][:, 0:w], in0=ps4[:, 0:w], scalar=ci[:, i, h:h + 1],
                                               in1=cb[:, 0:w], op0=ALU.add, op1=ALU.subtract).then_inc(s_biased, 1)
                    else:
                        o = (NB - 1 - i + lo) * P
                        v.scalar_tensor_tensor(out=sbuf[u % 2][:, 0:w], in0=t_("dist", o, w), scalar=SLOPES[h],
                                               in1=ps4[:, 0:w], op0=ALU.mult, op1=ALU.add).then_inc(s_biased, 1)
                    dve.wait_ge(s_biased, u + 1)
                    nm = nmx[:, u % 4:u % 4 + 1]
                    ins = v.tensor_reduce(nm, sbuf[u % 2][:, 0:w], AX, ALU.max, negate=True)
                    if ph == "SWA":
                        link(ins)
                        ins = v.tensor_tensor(nm, nm, nsink[:, h:h + 1], ALU.min)
                    ins.then_inc(s_negmax, 1)
                m = u - 2
                if first <= m < first + count:
                    ph, h, i, lo, nb = unit(m)
                    dve.wait_ge(s_out, m + 1)
                    d, f = den[:, m % 4:m % 4 + 1], fac[:, m % 4:m % 4 + 1]
                    if ph == "SWA":
                        link(v.tensor_tensor(d, d, esk[:, m % 4:m % 4 + 1], ALU.add))
                    link(v.tensor_scalar(d, d, TINY, None, ALU.max))
                    link(v.reciprocal(f, d))
                    y = ytok[:, i, h * DH:(h + 1) * DH]
                    o = ps7[:, 0:DH]
                    if ph in ("SEL", "WIN"):
                        gi = 3 * h + (1 if ph == "SEL" else 2)
                        link(v.tensor_tensor(f, f, gates[:, i, gi:gi + 1], ALU.mult))
                        v.scalar_tensor_tensor(out=y, in0=o, scalar=f, in1=y, op0=ALU.mult, op1=ALU.add
                                               ).then_inc(s_norm, 1)
                    else:
                        if m == first:
                            wait_tile(dve, TILE["yD1" if ph == "SWA" else "yA1"])
                        v.tensor_scalar(y, o, f, None, ALU.mult).then_inc(s_norm, 1)

            def stick(s):
                if s < NSTICK:
                    c0 = stick_q0(s)
                    dve.wait_ge(k_z, s + 1)
                    if s >= 2:
                        dve.wait_ge(k_r, s - 1)
                        dve.wait_ge(k_sum, s - 1)
                    v.tensor_scalar(skt[s % 2][:, c0:HALF].bitcast(I32), psb[s % 2][:, c0:HALF].bitcast(I32),
                                    0x7FFFFFFF, None, ALU.bitwise_and).then_inc(k_abs, 1)
                if 1 <= s <= NSTICK:
                    m = s - 1
                    c0 = stick_q0(m)
                    t = skt[m % 2]
                    dve.wait_ge(k_log, m + 1)
                    ins = v.scalar_tensor_tensor(out=t[:, c0:HALF], in0=psb[m % 2][:, c0:HALF], scalar=0.0,
                                                 in1=t[:, c0:HALF], op0=ALU.max, op1=ALU.add)
                    if STICK_DIAG[m]:
                        link(ins)
                        ins = v.tensor_tensor(t[:, c0:c0 + P], t[:, c0:c0 + P], t_("strict"), ALU.mult)
                    ins.then_inc(k_sp, 1)
                if s >= 2 and STICK[s - 2][1:] == (1, 0):
                    h = STICK[s - 2][0]
                    dve.wait_ge(k_o, s - 1)
                    if h == 0:
                        wait_tile(dve, TILE["yB1"])
                    v.tensor_copy(ytok[:, :, h * DH:(h + 1) * DH],
                                  pso[h % 2][:].rearrange("p (b d) -> p b d", b=NB)).then_inc(k_y, 1)

            def retention(n):
                if n < NB:
                    dve.wait_ge(r_s, n + 1)
                    if n == 0:
                        dve.wait_ge(rtab_in, 16)
                    if n >= 2:
                        dve.wait_ge(r_o, n - 1)
                    v.tensor_tensor(sbuf[n % 2][:, 0:HALF], psb[n % 2], dtab, ALU.mult).then_inc(r_st, 1)
                    if n < NB - 1:
                        for t in range(2):
                            u = ps6[:, t * DH:(t + 1) * DH]
                            if n == 0:
                                ins = v.tensor_copy(rst[:, 1, t, :], u)
                            else:
                                if t == 0:
                                    dve.wait_ge(r_state, n)
                                ins = v.scalar_tensor_tensor(out=rst[:, n + 1, t, :], in0=rst[:, n, t, :],
                                                             scalar=t_("gc", t, 1), in1=u,
                                                             op0=ALU.mult, op1=ALU.add)
                            if t == 0:
                                link(ins)
                            else:
                                ins.then_inc(r_state, 1)
                if n >= 1:
                    m = n - 1
                    dve.wait_ge(r_o, m + 1)
                    v.tensor_copy(ytok[:, m, :], ps7[:, 0:BW]).then_inc(r_y, 1)

            def retention_norm():
                y = ytok[:].rearrange("p b (h d) -> p (b h) d", h=H)
                sq = sq8[:].rearrange("p b (h d) -> p (b h) d", h=H)

                def wide_(a):
                    return a.unsqueeze(2).to_broadcast([P, 32, DH])

                dve.wait_ge(r_y, NB)
                link(v.tensor_reduce(st32[:, 0, :], y, AX, ALU.add))
                link(v.tensor_scalar(st32[:, 0, :], st32[:, 0, :], -1.0 / DH, None, ALU.mult))
                link(v.tensor_tensor(y, y, wide_(st32[:, 0, :]), ALU.add))
                link(v.tensor_tensor(sq, y, y, ALU.mult))
                v.tensor_reduce(st32[:, 1, :], sq, AX, ALU.add).then_inc(r_var, 1)
                dve.wait_ge(r_sq, 1)
                link(v.reciprocal(st32[:, 3, :], st32[:, 2, :]))
                v.tensor_tensor(y, y, wide_(st32[:, 3, :]), ALU.mult).then_inc(ret_done, 1)

            def compress(s):
                if s == 0:
                    wait_evacuated(dve, "Acmp")
                    z = acmp[:].rearrange("p (c l) -> p c l", l=32)
                    v.tensor_tensor(z, z, v_("pos").unsqueeze(1).to_broadcast([P, NCMP, 32]), ALU.add
                                    ).then_inc(c_pos, 1)
                elif s == 2:
                    s3 = sbuf[0][:].rearrange("p (u c) -> p u c", c=NCMP)

                    def wide_(a):
                        return a.unsqueeze(2).to_broadcast([P, 32, NCMP])

                    dve.wait_ge(c_s, 1)
                    w = NB * NCMP
                    for h in range(H):
                        link(v.scalar_tensor_tensor(out=sbuf[0][:, h * w:(h + 1) * w], in0=t_("cdist"),
                                                    scalar=SLOPES[h], in1=ps4[:, h * w:(h + 1) * w],
                                                    op0=ALU.mult, op1=ALU.add))
                    link(v.tensor_reduce(st32[:, 0, :], s3, AX, ALU.max, negate=True))
                    v.tensor_tensor(s3, s3, wide_(st32[:, 0, :]), ALU.add).then_inc(c_sb, 1)
                    dve.wait_ge(c_e, 1)
                    s4 = sbuf[0][:].rearrange("p (h w) -> p h w", h=H)
                    link(v.tensor_tensor(s4, s4, t_("cmask").unsqueeze(1).to_broadcast([P, H, w]), ALU.mult))
                    link(v.tensor_reduce(st32[:, 1, :], s3, AX, ALU.add))
                    link(v.tensor_scalar(st32[:, 1, :], st32[:, 1, :], TINY, None, ALU.max))
                    link(v.reciprocal(st32[:, 2, :], st32[:, 1, :]))
                    v.tensor_tensor(s3, s3, wide_(st32[:, 2, :]), ALU.mult).then_inc(c_p, 1)
                elif s == 4:
                    wait_evacuated(dve, "Agates")
                    wait_tile(dve, TILE["yC1"])
                    for h in range(H):
                        dve.wait_ge(c_o, h + 1)
                        v.tensor_tensor(ytok[:, :, h * DH:(h + 1) * DH], ps7[:].rearrange("p (b d) -> p b d", b=NB),
                                        gates[:, :, 3 * h:3 * h + 1].to_broadcast([P, NB, DH]), ALU.mult
                                        ).then_inc(c_y, 1)

            dve.wait_ge(small_in, 32)
            link(v.tensor_copy(identb[:], t_("ident")))
            link(v.tensor_copy(upb[:], t_("up")))
            link(v.tensor_copy(lowb[:], t_("low")))
            link(v.memset(fac[:], 1.0))
            v.tensor_scalar(nsink[:], v_("sink"), -1.0, None, ALU.mult).then_inc(masks_done, 1)
            dve.wait_ge(mod_mm, 1)
            link(v.tensor_tensor(mod[:], ps6[:, 0:24], v_("b_ada"), ALU.add))
            link(v.tensor_scalar(gmul[:], mod[:, 8:16], 1.0, None, ALU.add))
            v.tensor_tensor(gmul[:], gmul[:], v_("norm_g"), ALU.mult).then_inc(mod_done, 1)

            for ev in TIMELINE:
                if ev[0] == "dense":
                    if ev[2] == 3:
                        evacuate(ev[1])
                elif ev[0] == "ytrans":
                    br, n = ev[1], ev[2]
                    g = TILE["y%s%d" % (br, n)]
                    wait_tile(dve, g)
                    wait_evacuated(dve, "%sz%d" % (br, n))
                    v.tensor_tensor(zs[n][:], slot[g % 2][:], zs[n][:], ALU.mult).then_inc(slot_free[g % 2], 1)
                elif ev[0] == "ret":
                    retention(ev[1])
                elif ev[0] == "retnorm":
                    retention_norm()
                elif ev[0] == "soft":
                    soft(ev[1], ev[2], ev[3])
                elif ev[0] == "stick":
                    stick(ev[1])
                elif ev[0] == "cmp":
                    compress(ev[1])
                elif ev[0] == "conv":
                    t, k = ev[1], ev[2]
                    w = v_("dw", 31 * t + k, 1)
                    sh = 30 - k
                    if k == 0:
                        wait_evacuated(dve, "Eca%d" % t)
                        link(v.tensor_scalar(cacc[:, t, :], cu[:, t, :], v_("dw", 31 * t + 30, 1), None, ALU.mult))
                    if k < 30:
                        ins = v.scalar_tensor_tensor(out=cacc[:, t, sh:S], in0=cu[:, t, 0:S - sh], scalar=w,
                                                     in1=cacc[:, t, sh:S], op0=ALU.mult, op1=ALU.add)
                        if k < 29:
                            link(ins)
                        else:
                            ins.then_inc(conf_done, 1)
                elif ev[0] == "norm1":
                    rstd(0)
                    dve.wait_ge(mod_done, 1)
                    for n in range(NC):
                        dve.wait_ge(sq_done, n + 1)
                        link(v.scalar_tensor_tensor(out=mm[:, n, :], in0=mm[:, n, :], scalar=gmul[:, n:n + 1],
                                                    in1=pbuf[1][:], op0=ALU.mult, op1=ALU.mult))
                        v.tensor_scalar(mm[:, n, :], mm[:, n, :], mod[:, n:n + 1], None, ALU.add).then_inc(x_src, 1)
                    applied(0, x_src, 8)
                elif ev[0] == "norm2":
                    rstd(1)
                    for n in range(NC):
                        dve.wait_ge(sq_done, 8 + n + 1)
                        scaled(mm[:, n, :], mm[:, n, :], v_("final_g", n, 1), chunk_ready, n == 7, 1)
                    applied(1, chunk_ready, 8)
                    rstd(2)
                    for n in range(NC):
                        scaled(res[:, n, :], mm[:, n, :], v_("g_mix_pre", n, 1), x_src, n == 7, 2)
                    applied(2, x_src, 16)
                elif ev[0] in ("norm3", "norm4"):
                    k = 3 if ev[0] == "norm3" else 5
                    post, pre = ("g_mix_post", "g_mlp_pre") if k == 3 else ("g_mlp_post", "g_ple_pre")
                    rstd(k)
                    for n in range(NC):
                        dve.wait_ge(sq_done, 8 * k + n + 1)
                        scaled(mm[:, n, :], mm[:, n, :], v_(post, n, 1), t_ready, n == 7, k)
                    applied(k, t_ready, 8 * (k - 1) // 2)
                    rstd(k + 1)
                    for n in range(NC):
                        dve.wait_ge(res_added, 4 * (k - 3) + n + 1)
                        scaled(mm[:, n, :], res[:, n, :], v_(pre, n, 1), x_src, n == 7, k + 1)
                    applied(k + 1, x_src, 24 + 4 * (k - 3))
                elif ev[0] == "norm5":
                    rstd(7)
                    for n in range(NC):
                        dve.wait_ge(sq_done, 56 + n + 1)
                        scaled(mm[:, n, :], mm[:, n, :], v_("g_ple_post", n, 1), t_ready, n == 7, 7)
                elif ev[0] == "mix":
                    dve.wait_ge(s_norm, 128)
                    for t in range(2):
                        g = TILE["yE%d" % t]
                        wait_tile(dve, g)
                        v.tensor_copy(pbuf[t][:], slot[g % 2][:]).then_inc(slot_free[g % 2], 1)
                        wait_evacuated(dve, "yE%d" % t)
                        v.tensor_copy(fac[:, 0:1], fac[:, 1:2]).then_inc(mix_src, 1)
                    for t in range(2):
                        dve.wait_ge(m_pool, t + 1)
                        v.tensor_scalar(ply[:, t, :], ps4[:], v_("pool_scale", t, 1), None, ALU.mult
                                        ).then_inc(m_pool_in, 1)
                        dve.wait_ge(m_pool_in, t + 1)
                        v.tensor_copy(fac[:, 0:1], fac[:, 1:2]).then_inc(mix_src, 1)
                    dve.wait_ge(m_mean, 1)
                    for t in range(2):
                        v.scalar_tensor_tensor(out=cacc[:, t, :], in0=ps4[:], scalar=-1.0 / BW, in1=cacc[:, t, :],
                                               op0=ALU.mult, op1=ALU.add).then_inc(m_cent, 1)
                    dve.wait_ge(m_std, 1)
                    link(v.reciprocal(sx[:], sx[:]))
                    for t in range(2):
                        v.tensor_tensor(cacc[:, t, :], cacc[:, t, :], sx[:], ALU.mult).then_inc(m_hat, 1)
                    for t in range(2):
                        dve.wait_ge(m_pw, t + 1)
                        v.tensor_copy(cu[:, t, :], ps4[:]).then_inc(m_pw_in, 1)
                        dve.wait_ge(m_pw_in, t + 1)
                        v.tensor_copy(fac[:, 0:1], fac[:, 1:2]).then_inc(mix_src, 1)


def tables():
    t = np.zeros((P, NTABLE), np.float32)
    p = np.arange(P)[:, None]

    def put(name, value):
        o, w = TABLES[name]
        t[:, o:o + w] = value

    j = np.arange(S)[None, :]
    rel = j - p - (S - P)
    put("dist", np.where(rel <= 0, rel, -1e32))
    c = np.arange(P)[None, :]
    put("ident", p == c)
    put("strict", p < c)
    put("tri", np.where(p >= c, -1.0, 0.0))
    put("negones", -1.0)
    put("ones", 1.0)
    put("up", np.where(c > p, NEG, 0.0))
    put("low", np.where(c > p, 0.0, NEG))
    i = np.arange(NB * NCMP)[None, :]
    dist = (i // NCMP) * P + p - 32 * (i % NCMP) - 31
    put("cdist", np.where(dist >= 0, -dist, -1e32))
    put("cmask", dist >= 0)
    lg = np.log(1.0 - 2.0 ** (-5.0 - np.arange(H)))
    head = np.arange(2)[None, :] * 2 + p // DH
    put("gc", np.exp(lg[head] * P))
    put("eps6", 1e-6)
    put("eps5", 1e-5)
    win = np.array([2.0, 4.0, 8.0, 16.0])[head]
    put("invw", 1.0 / win)
    tok = np.arange(16)[None, None, :]
    put("invc", (1.0 / np.minimum(tok + 1, win[:, :, None])).reshape(P, 32))
    r = np.zeros((P, RET_TABLE), np.float32)
    d = c - p
    r[:, 0:4 * P] = np.concatenate([np.where(d >= 0, np.exp(lg[h] * np.maximum(d, 0)), 0.0) for h in range(H)], 1)
    r[:, 4 * P:6 * P] = np.exp(lg[head][:, :, None] * (np.arange(P)[None, None, :] + 1)).reshape(P, 2 * P)
    f = np.arange(2 * P)[None, :]
    r[:, 6 * P:8 * P] = np.exp(lg[f // DH] * (P - 1 - p))
    return t, r


def pack_weights(inp):
    w1, w2 = inp["w_in"][0], inp["w_in_2"][0]
    wm, wb, wo = inp["w_merge"][0], inp["w_br"][0], inp["w_out"][0]
    bi = {"A": 0, "B": 1, "C": 2, "D": 3}
    start = {"Aq": 0, "Acmp": 256, "Az": 652, "Bq": 908, "Bv": 1292, "Bz": 1420,
             "Cq": 1676, "Ck": 1932, "Cv": 2188, "Cz": 2444, "Dq": 2700, "Dk": 2956, "Dt": 2956, "Dv": 3212,
             "Dz": 3468, "Eca": 0, "Ecb": 256, "Eq": 512, "Ek": 768, "Ev": 1024, "Ef": 1280, "Esh": 1284,
             "Esb": 1540, "Esc": 1796, "Ep": 2052}

    def chunks(w):
        return np.asarray(w).reshape(-1, P, w.shape[1]).transpose(1, 0, 2).reshape(P, -1)

    def twice(w):
        return np.concatenate([w, w], 1)

    out = []
    for kind, name, n in BLOCKS:
        if name == "Ak0":
            blk = chunks(twice(w1[:, 384:448]))
        elif name == "Ak1":
            blk = chunks(twice(w1[:, 512:576]))
        elif name == "Av0":
            blk = chunks(np.concatenate([w1[:, 448:512], w1[:, 576:640]], 1))
        elif name == "Agates":
            blk = chunks(w1[:, 640:652])
        elif name in ("Bk0", "Bk1"):
            o = 1164 + DH * int(name[2])
            blk = chunks(twice(w1[:, o:o + DH]))
        elif kind == "M":
            m = int(name[-1])
            cols = slice(m * P, (m + 1) * P)
            if name[0] == "g":
                blk = np.concatenate([chunks(inp["w_ple_gate_2"][0][:, cols]),
                                      chunks(inp["w_ple_proj_2"][0][:, cols])], 1)
            else:
                blk = np.concatenate([chunks(wm[bi[name[0]]][:, cols]), chunks(wb[bi[name[0]]][:, cols])], 1)
        elif name[0] in "ox":
            m = int(name[1])
            blk = chunks((wo if name[0] == "o" else inp["w_out_2"][0])[:, m * P:(m + 1) * P])
        elif name[0] == "u":
            e, m = (int(x) for x in name[1:].split("_"))
            o = (UPS * e + m) * P
            blk = chunks(inp["w_up_2"][0][:, o:o + P])
        elif name[0] == "d":
            e, m = (int(x) for x in name[1:].split("_"))
            blk = chunks(inp["w_down_2"][0][UPS * P * e:UPS * P * (e + 1), 2 * P * m:2 * P * (m + 1)])
        else:
            w = w2 if name[0] == "E" else w1
            key = name.rstrip("0123456789")
            o = start[key] + P * int(name[len(key):] or 0)
            blk = chunks(w[:, o:o + P])
        out.append(blk.ravel())
    return np.concatenate(out)


def pack_vectors(inp):
    v = np.zeros((P, NVEC), np.float32)

    def put(name, value):
        o, w = VECS[name]
        v[:, o:o + w] = value

    def cols(a):
        return np.asarray(a).reshape(-1, P).T

    put("c", cols(inp["c"][0]))
    put("b_ada", cols(inp["b_ada"][0]))
    put("norm_g", cols(inp["norm_g"][0]))
    put("final_g", cols(inp["final_g"]))
    for n in ("g_mix_pre", "g_mix_post", "g_mlp_pre", "g_mlp_post", "g_ple_pre", "g_ple_post"):
        put(n, cols(inp[n + "_2"][0]))
    dw, sc = np.asarray(inp["w_conf_dw_2"][0]), np.asarray(inp["w_sc_2"][0])
    put("dw", np.concatenate([dw[:, 0:P].T, dw[:, P:].T], 1))
    put("sc", np.concatenate([sc[:, 0:P].T, sc[:, P:].T], 1))
    put("ln_g", cols(inp["conf_ln_g_2"][0]))
    put("ln_b", cols(inp["conf_ln_b_2"][0]))
    put("pool_scale", cols(inp["pool_scale_2"][0]))
    put("sink", np.broadcast_to(inp["sink"][0], (P, H)))
    o, _ = VECS["bf"]
    v[0:H, o] = inp["b_forget_2"][0]
    pos = np.asarray(inp["cmp_pos"][0])
    put("pos", pos.transpose(0, 2, 1).reshape(P, 32))
    return v


def kernel(**inputs):
    import concourse.bacc as _bacc
    from concourse.bass_utils import run_bass_kernel_spmd as _run

    inp = {k: np.asarray(a) for k, a in inputs.items()}
    tab, rtab = tables()
    w1, w2 = inp["cmp_w1"][0], inp["cmp_w2"][0]
    wp = np.zeros((P, 2, P), np.float32)
    for g in range(4):
        r = DH * (g % 2)
        wp[r:r + DH, g // 2, r:r + DH] = inp["w_pool_2"][0, g]
    arrays = {
        "xT": inp["x"][0].T.reshape(NC, P, S).transpose(1, 0, 2),
        "pT": inp["p_2"][0, 0].T.reshape(2, P, S).transpose(1, 0, 2),
        "wstream": pack_weights(inp),
        "wada": inp["w_ada"][0].reshape(8, P, 3, D).transpose(2, 1, 0, 3),
        "vecs": pack_vectors(inp),
        "tables": tab,
        "rtables": rtab,
        "cw1": w1.reshape(2, 32, DH, DH).transpose(0, 2, 1, 3).reshape(P, 32, DH),
        "cw2": np.concatenate([w2[0], w2[0], w2[1]], 1),
        "wpw": inp["w_conf_pw_2"][0].reshape(2, P, BW).transpose(1, 0, 2),
        "wpool": wp,
    }
    arrays = {k: np.ascontiguousarray(a) for k, a in arrays.items()}
    nc = _bacc.Bacc("TRN2", target_bir_lowering=False, num_devices=1)
    args = [nc.dram_tensor(k, a.shape, F32, kind="ExternalInput").ap() for k, a in arrays.items()]
    args.append(nc.dram_tensor("outT", (P, NC, S), F32, kind="ExternalOutput").ap())
    build(nc, *args)
    r = _run(nc, [arrays], core_ids=[0])
    o = r.results[0]["outT"]
    return o.transpose(1, 0, 2).reshape(D, S).T.reshape(1, S, D)
```

```python
from contextlib import ExitStack

import numpy as np
import concourse.bass as bass
from concourse import mybir

ALU = mybir.AluOpType
ACT = mybir.ActivationFunctionType
F32 = mybir.dt.float32
F32R = mybir.dt.float32r
BF16 = mybir.dt.bfloat16
I32 = mybir.dt.int32
AX = mybir.AxisListType.X

P = 128
S = 1024
D = 1024
NC = D // P
NB = S // P
H = 4
DH = 64
BW = H * DH
HALF = 512
FF = 4 * D
NCMP = S // 32
TINY = 1e-30
NEG = -1e30
SLOPES = [2.0 ** (-8.0 * (h + 1) / H) for h in range(H)]
QSCALE = DH ** -0.5

BRANCHES = "DBCA"
NPROJ = {"D": ["v0", "v1", "t0", "t1", "q0", "q1", "k0", "k1"],
         "B": ["v0", "q0", "q1", "k0", "k1"],
         "C": ["v0", "v1", "q0", "q1", "k0", "k1"],
         "A": ["v0", "g1", "q0", "q1", "cmp", "k0", "k1"],
         "E": ["cb0", "ca0", "cb1", "ca1", "v0", "q0", "k0", "f", "v1", "q1", "k1"]}
NGATE = 3 * H
NEIGHTH = 8
UPS = FF // P // NEIGHTH


def list_blocks():
    blocks = []

    def proj(br):
        for name in NPROJ[br]:
            blocks.append(("F", br + name))

    def merge(br):
        for n in range(2):
            blocks.append(("F", br + "z%d" % n))
        for n in range(NC):
            blocks.append(("M", br + "m%d" % n))

    proj("D")
    proj("B")
    merge("D")
    proj("C")
    merge("B")
    proj("A")
    merge("C")
    merge("A")
    blocks.extend(("F", "o%d" % n) for n in range(NC))
    for name in NPROJ["E"] + ["sh0", "sc0", "sb0", "sh1", "sc1", "sb1", "p0", "p1"]:
        blocks.append(("F", "E" + name))
    blocks.extend(("F", "x%d" % n) for n in range(NC))
    for e in range(NEIGHTH):
        blocks.extend(("F", "u%d_%d" % (e, n)) for n in range(UPS))
        blocks.extend(("D", "d%d_%d" % (e, n)) for n in range(NC // 2))
    blocks.extend(("M", "g%d" % n) for n in range(NC))
    return blocks


BLOCKS = list_blocks()
INDEX = {name: b for b, (_, name) in enumerate(BLOCKS)}
BLOCK_LEN = [{"F": 8 * P, "M": 10 * P, "D": 8 * P}[kind] for kind, _ in BLOCKS]
BLOCK_OFF = [P * int(v) for v in np.cumsum([0] + BLOCK_LEN)]


PARTS = {"F": 8, "M": 10, "D": 8}


def dense_part_events(names):
    return [("dense", INDEX[n], part) for n in names for part in range(PARTS[BLOCKS[INDEX[n]][0]])]


def last_part(ev):
    return ev[2] == PARTS[BLOCKS[ev[1]][0]] - 1


def weight(ev):
    if ev[0] == "soft":
        u, first, n = ev[1:]
        return 1.5 + sum(0.5 * unit(v)[4] for v in (u, u - 2) if first <= v < first + n)
    if ev[0] == "stick" and ev[1] < NSTICK:
        return 1.0 + (HALF - stick_q0(ev[1])) / P
    return 2.0


NTAPS_EARLY = 40


def spread(dense, steps):
    total = sum(weight(ev) for ev in steps)
    out, done, passed = [], 0, 0.0
    for n, ev in enumerate(dense):
        out.append(ev)
        while done < len(steps) and passed + weight(steps[done]) / 2 <= (n + 1) * total / len(dense):
            passed += weight(steps[done])
            out.append(steps[done])
            done += 1
    return out + steps[done:]


def unit(u):
    ph, r = ("SWA", "SEL", "WIN", "FGT")[u // 32], u % 32
    if ph == "FGT":
        h, i = r // NB, r % NB
    else:
        h, i = 2 * (r // 16) + r % 2, r % 16 // 2
    lo = {"SWA": max(0, i - 1), "SEL": 0, "WIN": max(0, i - 4), "FGT": 0}[ph]
    return ph, h, i, lo, i + 1 - lo


KTILE = [{"SWA": unit(u)[1] // 2, "SEL": 0, "WIN": 1, "FGT": unit(u)[1] // 2}[unit(u)[0]] for u in range(128)]
KSPLITS = [u for u in range(128) if u == 0 or (unit(u)[0], KTILE[u]) != (unit(u - 1)[0], KTILE[u - 1])]
QKEY = [(unit(u)[0], unit(u)[1] // 2, unit(u)[2]) for u in range(128)]
QFIRST = [u for u in range(128) if u == 0 or QKEY[u] != QKEY[u - 1]]
QLAST = [u - 1 for u in QFIRST[1:]] + [127]
QID = [int(np.searchsorted(QFIRST, u, side="right")) - 1 for u in range(128)]


def batches(u):
    return -(-unit(u)[4] // 4)


BATCH_END = [int(v) for v in np.cumsum([batches(u) for u in range(128)])]


NRET, NSTICK, NSWA, NSEL, NWIN, NFGT = NB, H * 12, 32, 32, 32, 32
U_SWA, U_SEL, U_WIN, U_FGT = 0, 32, 64, 96


STICK = [(h, half, j) for h in range(H) for half in range(2) for j in range(4 * half + 3, -1, -1)]
STICK_DIAG = [j * P >= half * HALF for _, half, j in STICK]
DIAG_COUNT = [int(v) for v in np.cumsum(STICK_DIAG)]


def stick_q0(s):
    _, half, j = STICK[s]
    return max(0, j * P - half * HALF)


def soft_events(first, n):
    out = []
    for u in range(first, first + n + 3):
        if u < first + n and u in KSPLITS:
            out.append(("ksplit", u))
        out.append(("soft", u, first, n))
    return out


def proj_events(br):
    out, late = [], []
    for name in NPROJ[br]:
        out += dense_part_events([br + name]) + late
        late = [("turn", br + name)] if name[0] in "vtg" else []
    return out + late


def list_timeline():
    def merge_names(br):
        return [br + "m%d" % n for n in range(NC)]

    def z_events(br):
        ev = dense_part_events([br + "z0", br + "z1"])
        return ev + [("ytrans", br, 0), ("ytrans", br, 1)]

    tl = [("norm1",)]
    proj = proj_events("D")
    middle = proj.index(("dense", INDEX["Dk0"], 0))
    tl += proj[:middle] + [("gate_mod",)] + proj[middle:]
    ret = [("ret", n) for n in range(NB + 1)] + [("retnorm",)]
    tl += spread(proj_events("B"), ret)
    tl += z_events("D")
    tl += spread(dense_part_events(merge_names("D")), soft_events(U_SWA, NSWA))
    tl += proj_events("C")
    tl += z_events("B")
    tl += spread(dense_part_events(merge_names("B")), [("stick", s) for s in range(NSTICK + 3)])
    tl += proj_events("A")
    tl += z_events("C")
    tl += spread(dense_part_events(merge_names("C")),
                 [ev for s in range(5) for ev in (("cmp", s), ("pause",), ("pause",))]
                 + soft_events(U_SEL, NSEL + NWIN))
    tl += z_events("A")
    tl += dense_part_events(merge_names("A"))
    tl += [("split_merged",)]
    tl += dense_part_events("o%d" % n for n in range(NC))
    tl += [("norm2",)]
    proj = proj_events("E") + dense_part_events("E" + n for n in ("sh0", "sc0", "sb0", "sh1", "sc1", "sb1"))
    taps = proj.index(("dense", INDEX["Eca1"], PARTS["F"] - 1)) + 1
    soft = proj.index(("dense", INDEX["Ef"], PARTS["F"] - 1)) + 1
    conv = [("conv", t, k) for t in range(2) for k in range(31)]
    steps = [("fprep", 0)] + soft_events(U_FGT, NFGT)
    rest = spread(proj[soft:], steps)
    tl += proj[:taps] + spread(proj[taps:soft], conv[:NTAPS_EARLY]) + spread(rest, conv[NTAPS_EARLY:])
    tl += dense_part_events(["Ep0", "Ep1"])
    tl += [("mix",)]
    tl += dense_part_events("x%d" % n for n in range(NC))
    tl += [("norm3",)]
    for e in range(NEIGHTH):
        tl += dense_part_events("u%d_%d" % (e, n) for n in range(UPS))
        tl += dense_part_events("d%d_%d" % (e, n) for n in range(NC // 2))
    tl += [("norm4",)]
    tl += dense_part_events("g%d" % n for n in range(NC))
    tl += [("norm5",)]
    return tl


TIMELINE = list_timeline()


def number_tiles():
    g, tiles = 0, {}
    for ev in TIMELINE:
        if ev[0] == "dense" and ev[2] == 0:
            kind, name = BLOCKS[ev[1]]
            tiles[name] = g
            g += 2 if kind in "MD" else 1
        elif ev[0] == "turn":
            tiles["turned " + ev[1]] = g
            g += 1
        elif ev[0] == "ytrans":
            tiles["y%s%d" % (ev[1], ev[2])] = g
            g += 1
        elif ev[0] == "mix":
            tiles["yE0"] = g
            g += 2
    tiles["yE1"] = tiles["yE0"] + 1
    return tiles


TILE = number_tiles()


def last_tile(b):
    kind, name = BLOCKS[b]
    return TILE[name] + (1 if kind in "MD" else 0)


def table_layout():
    at, out = 0, {}
    for name, n in [("dist", S), ("ident", P), ("strict", P), ("tri", P), ("negones", P), ("ones", P),
                    ("up", P), ("low", P), ("cdist", NB * NCMP), ("cmask", NB * NCMP), ("gc", 2),
                    ("eps6", 1), ("eps5", 1), ("invw", 2), ("invc", 32)]:
        out[name] = (at, n)
        at += n
    return out, at


TABLES, NTABLE = table_layout()
VECS = {}
_at = 0
for _n, _w in [("c", 8), ("b_ada", 24), ("norm_g", 8), ("final_g", 8), ("g_mix_pre", 8), ("g_mix_post", 8),
               ("g_mlp_pre", 8), ("g_mlp_post", 8), ("g_ple_pre", 8), ("g_ple_post", 8),
               ("dw", 62), ("ln_g", 2), ("ln_b", 2), ("sc", 6), ("pool_scale", 2), ("sink", 4), ("bf", 1),
               ("pos", 32)]:
    VECS[_n] = (_at, _w)
    _at += _w
NVEC = _at
RET_TABLE = 4 * P + 2 * P + 2 * P
CMP_W2 = 3 * DH


def build(nc, xT, pT, wstream, wada, vecs, tables, rtables, cw1, cw2, wpw, wpool, out):
    with ExitStack() as ctx:
        base = 16512
        K = 256

        def at(name, kib, shape, dt=F32):
            return nc.alloc_sbuf_tensor_at(name, shape, dt, offset=base + int(kib * 1024))

        def psum(name, shape):
            return ctx.enter_context(nc.psum_tensor(name, shape, F32))

        def sem(name):
            return ctx.enter_context(nc.semaphore(name))

        xhi = at("xhi", 0, [P, NC, S], F32R)
        xlo = at("xlo", 32, [P, NC, S], F32R)
        ada0 = at("ada0", 0, [P, 8, D])
        ada1 = at("ada1", 32, [P, 8, D])
        mm = at("mm", 64, [P, NC, S])
        raw = at("raw", 96, [P, 10 * P])
        whi = [at("whi%d" % i, 101 + 5 * i, [P, 10, P], F32R) for i in range(2)]
        wlo = [at("wlo%d" % i, 111 + 5 * i, [P, 10, P], F32R) for i in range(2)]
        yhi = at("yhi", 121, [P, 2, S], F32R)
        ylo = at("ylo", 129, [P, 2, S], F32R)
        uhi = at("uhi", 121, [P, UPS, S], F32R)
        ulo = at("ulo", 137, [P, UPS, S], F32R)
        rtab = at("rtab", 121, [P, RET_TABLE])
        rst = at("rst", 125, [P, NB, 2, DH])
        cb = at("cb", 121, [P, S])
        ct = at("ct", 125, [P, S])
        cu = at("cu", 129, [P, 2, S])
        ytok = at("ytok", 137, [P, NB, BW])
        zs2 = [at("zs2%d" % i, 137 + 4 * i, [P, S]) for i in range(2)]
        sbuf = [at("sbuf%d" % i, 145 + 4 * i, [P, S]) for i in range(2)]
        pbuf = [at("pbuf%d" % i, 153 + 4 * i, [P, S]) for i in range(2)]
        sq8 = at("sq8", 145, [P, NB, BW])
        sring = [sbuf[0], sbuf[1], pbuf[0]]
        ptr = pbuf[1]
        skt = [at("skt%d" % i, 145 + 2 * i, [P, HALF]) for i in range(4)]
        ska = [at("ska%d" % i, 153 + 2 * i, [P, HALF]) for i in range(2)]
        skl = [at("skl%d" % i, 157 + 2 * i, [P, HALF]) for i in range(2)]
        cw1s = at("cw1s", 153, [P, 32, DH])
        tbuf = [at("tbuf0", 153, [P, S]), at("tbuf1", 157, [P, S])]
        brq = at("brq", 161, [P, 2, S])
        brk = at("brk", 169, [P, 2, S])
        brv = at("brv", 177, [P, 2, NB, P])
        dq = at("dq", 64, [P, 2, S])
        dk = at("dk", 72, [P, 2, S])
        dv = at("dv", 80, [P, 2, NB, P])
        dt_ = at("dt", 88, [P, 2, NB, P])
        brkl = at("brkl", 169, [P, 2, S], F32R)
        khi = at("khi", 190, [P, S], F32R)
        qp = at("qp", 181, [P, 2, 2, P], F32R)
        acmp = at("acmp", 181, [P, S])
        ada2 = [at("ada20", 129, [P, 8, HALF]), at("ada21", 161, [P, 8, HALF])]
        ada_sum = [at("ada_sum%d" % i, kib, [P, D]) for i, kib in enumerate((186, 190, 153))]
        acc2 = at("acc2", 161, [P, S])
        sqr2 = [at("sqr2%d" % i, 165 + 4 * i, [P, S]) for i in range(2)]
        res = at("res", 161, [P, NC, S])
        zs = [at("zs%d" % i, 186 + 4 * i, [P, S]) for i in range(2)]
        cacc = at("cacc", 64, [P, 2, S])
        scy = at("scy", 72, [P, 2, S])
        ply = at("ply", 80, [P, 2, S])
        khif = at("khif", 80, [P, S], F32R)
        qpf = at("qpf", 84, [P, 2, 2, P], F32R)
        su = at("su", 88, [P, S])
        sx = at("sx", 92, [P, S])
        tab = at("tab", 194, [P, NTABLE])
        top = 194 + (NTABLE * 4 + 31) // 32 * 32 / 1024

        small_at = [top]

        def small(name, shape, dt=F32):
            n = int(np.prod(shape[1:])) * (2 if dt == BF16 else 4)
            t = at(name, small_at[0], shape, dt)
            small_at[0] += (n + 31) // 32 * 32 / 1024
            return t

        vec = small("vec", [P, NVEC])
        identb = small("identb", [P, P], BF16)
        upb = small("upb", [P, P], BF16)
        lowb = small("lowb", [P, P], BF16)
        csil = small("csil", [P, 8])
        mod = small("mod", [P, 24])
        gmul = small("gmul", [P, 8])
        nsink = small("nsink", [P, 4])
        fgp = small("fgp", [P, 8])
        nmx = small("nmx", [P, 4])
        den = small("den", [P, 4])
        esk = small("esk", [P, 4])
        fac = small("fac", [P, 4])
        gates = small("gates", [P, NB, 12])
        st32 = small("st32", [P, 4, 32])
        ci = small("ci", [P, NB, 4])
        kct = small("kct", [P, NCMP])
        vc4 = small("vc4", [P, DH])
        hsil = small("hsil", [DH, 5 * NCMP])
        assert base + small_at[0] * 1024 <= 229344, small_at[0]
        cw2s = at("cw2s", 185, [DH, CMP_W2])
        wpws = at("wpws", 186, [P, 2, BW])
        wpls = at("wpls", 188, [P, 2, P])

        def t_(name, a=0, n=None):
            o, w = TABLES[name]
            return tab[:, o + a:o + (w if n is None else a + n)]

        def v_(name, a=0, n=None):
            o, w = VECS[name]
            return vec[:, o + a:o + (w if n is None else a + n)]

        slot = [psum("slot%d" % i, [P, S]) for i in range(2)]
        ps4 = psum("ps4", [P, S])
        ps6 = psum("ps6", [P, HALF])
        ps7 = psum("ps7", [P, HALF])
        psb = [ps4[:, 0:HALF], ps4[:, HALF:S]]
        skz = [psb[0], psb[1], ps6]

        res_dram = nc.dram_tensor("res_dram", [P, NC, S], F32, kind="Internal").ap()

        small_in, x_in, raw_in, rtab_in = (sem(n) for n in ("small_in", "x_in", "raw_in", "rtab_in"))
        ada_in = [[sem("ada_in%d%d" % (i, half)) for half in range(2)] for i in range(3)]
        cmp_in, xres_in, res_out, res_in, p_in, pw_in, out_done = (
            sem(n) for n in ("cmp_in", "xres_in", "res_out", "res_in", "p_in", "pw_in", "out_done"))
        x_lo2, pq_done, pq_used, tq_done, tq_added, n2_t, res_odd, turned = (
            sem(n) for n in ("x_lo2", "pq_done", "pq_used", "tq_done", "tq_added", "n2_t", "res_odd", "turned"))
        w_hi, w_lo, tile_done = sem("w_hi"), sem("w_lo"), sem("tile_done")
        slot_free = [sem("slot_free0"), sem("slot_free1")]
        x_hi, x_lo, x_src = sem("x_hi"), sem("x_lo"), sem("x_src")
        y_src, y_hi, y_lo = sem("y_src"), sem("y_hi"), sem("y_lo")
        u_src, u_hi, u_lo = sem("u_src"), sem("u_hi"), sem("u_lo")
        prod_done, sum_done = sem("prod_done"), sem("sum_done")
        csil_done, mod_mm, mod_done, masks_done = sem("csil_done"), sem("mod_mm"), sem("mod_done"), sem("masks_done")
        chunk_ready, sq_done, sq_added, nsum, nstd, nrstd = (
            sem(n) for n in ("chunk_ready", "sq_done", "sq_added", "nsum", "nstd", "nrstd"))
        dve_chain, act_chain, pool_chain = sem("dve_chain"), sem("act_chain"), sem("pool_chain")
        s_scores, s_biased, s_negmax, s_exp, s_pt, s_ptsb, s_out, s_norm, s_esk = (
            sem(n) for n in ("s_scores", "s_biased", "s_negmax", "s_exp", "s_pt", "s_ptsb", "s_out", "s_norm", "s_esk"))
        r_s, r_st, r_qx, r_state, r_o, r_y, r_sq, r_var, ret_done = (
            sem(n) for n in ("r_s", "r_st", "r_qx", "r_state", "r_o", "r_y", "r_sq", "r_var", "ret_done"))
        k_z, k_abs, k_log, k_sp, k_sum, k_r, k_a, k_mask, k_o, k_y = (
            sem(n) for n in ("k_z", "k_abs", "k_log", "k_sp", "k_sum", "k_r", "k_a", "k_mask", "k_o", "k_y"))
        c_pos, c_h, c_hs, c_kv, c_kvs, c_s, c_sb, c_e, c_p, c_t, c_tb, c_o, c_y = (
            sem("c_%s" % n) for n in ("pos", "h", "hs", "kv", "kvs", "s", "sb", "e", "p", "t", "tb", "o", "y"))
        f_x, f_abs, f_log, f_c, f_ct, f_ci, f_bc, f_cb = (
            sem("f_%s" % n) for n in ("x", "abs", "log", "c", "ct", "ci", "bc", "cb"))
        conf_done, m_mean, m_cent, m_sq, m_var, m_std, m_hat, m_silu, m_pw, m_pool, m_pool_in, sc_done, pl_in, pl_done = (
            sem(n) for n in ("conf_done", "m_mean", "m_cent", "m_sq", "m_var", "m_std", "m_hat", "m_silu", "m_pw",
                             "m_pool", "m_pool_in", "sc_done", "pl_in", "pl_done"))
        pe_order = sem("pe_order")
        kh_done, kl_done, qh_done, ql_done, ada_acc = (
            sem(n) for n in ("kh_done", "kl_done", "qh_done", "ql_done", "ada_acc"))
        res_added, t_ready, napplied, mix_src, m_pw_in = (
            sem(n) for n in ("res_added", "t_ready", "napplied", "mix_src", "m_pw_in"))

        nblocks = len(BLOCKS)

        def wait_evacuated(eng, name, extra=0):
            g = TILE[name] + extra
            eng.wait_ge(slot_free[g % 2], g // 2 + 1)

        def wait_tile(eng, g):
            eng.wait_ge(tile_done, g + 1)

        def wait_split(eng, v, k):
            eng.wait_ge(x_lo if k % 2 else x_lo2, 4 * v + k // 2 + 1)

        def wait_all_split(eng, v):
            wait_split(eng, v, 6)
            wait_split(eng, v, 7)

        def wait_residual(eng, k, n):
            eng.wait_ge(res_odd if n % 2 else res_added, 4 * k + n // 2 + 1)

        LAST_USE = {1: last_tile(INDEX["Am7"]), 2: last_tile(INDEX["o7"]), 3: last_tile(INDEX["Ep1"]),
                    4: last_tile(INDEX["x7"]), 5: last_tile(INDEX["u%d_%d" % (NEIGHTH - 1, UPS - 1)])}

        def operand_version(name):
            if name[0] in "DBCA":
                return 0
            return {"o": 1, "E": 2, "x": 3, "u": 4, "g": 5}[name[0]]

        def flat(t):
            a = t[:]
            return a.rearrange("p a b -> p (a b)") if len(a.shape) == 3 else a

        dtab = rtab[:, 0:4 * P]
        xi = rtab[:, 4 * P:6 * P].rearrange("p (t q) -> p t q", t=2)
        zt = rtab[:, 6 * P:8 * P].rearrange("p (t q) -> p t q", t=2)
        mix_sources = [(4, scy[:, 0, :]), (5, scy[:, 1, :]), (2, pbuf[0][:]), (3, pbuf[1][:]),
                       (6, ply[:, 0, :]), (7, ply[:, 1, :]), (0, cu[:, 0, :]), (1, cu[:, 1, :])]

        def query_ids(u, first, count):
            ids = [QID[v] for v in ((u, u + 1) if u == first else (u + 1,)) if v < first + count and v in QFIRST]
            return ids

        def q_parts(m):
            ring = qpf if QKEY[QFIRST[m]][0] == "FGT" else qp
            return ring[:, m % 2, 0, :], ring[:, m % 2, 1, :]

        block = ctx.enter_context(nc.Block())

        @block.sync
        def _(sp):
            sp.dma_start(vec[:], vecs).then_inc(small_in, 16)
            sp.dma_start(tab[:], tables).then_inc(small_in, 16)
            for half in range(2):
                sp.dma_start(ada1[:, 4 * half:4 * half + 4, :], wada[1][:, 4 * half:4 * half + 4, :]
                             ).then_inc(ada_in[1][half], 16)
            sp.dma_start(mm[:], xT).then_inc(x_in, 16)
            for half in range(2):
                sp.dma_start(ada0[:, 4 * half:4 * half + 4, :], wada[0][:, 4 * half:4 * half + 4, :]
                             ).then_inc(ada_in[0][half], 16)

            def load_weights(b):
                if b >= 1:
                    sp.wait_ge(w_lo, b)
                n = BLOCK_LEN[b]
                src = wstream[BLOCK_OFF[b]:BLOCK_OFF[b] + P * n].rearrange("(p n) -> p n", p=P)
                sp.dma_start(raw[:, 0:n], src).then_inc(raw_in, 16)

            load_weights(0)
            sp.dma_start(rtab[:], rtables).then_inc(rtab_in, 16)
            for half in range(2):
                sp.dma_start(ada2[half][:], wada[2][:, :, half * HALF:(half + 1) * HALF]).then_inc(ada_in[2][half], 16)
            for ev in TIMELINE:
                if ev[0] == "dense" and ev[2] == 2 and ev[1] + 1 < nblocks:
                    load_weights(ev[1] + 1)
                elif ev == ("cmp", 0):
                    sp.wait_ge(k_y, H)
                    sp.dma_start(cw1s[:], cw1).then_inc(cmp_in, 16)
                    sp.dma_start(cw2s[:], cw2).then_inc(cmp_in, 16)
                elif ev[0] == "split_merged":
                    for n in range(NC):
                        wait_split(sp, 1, n)
                        sp.dma_start(mm[:, n, :], xT[:, n, :]).then_inc(xres_in, 16)
                elif ev[0] == "norm2":
                    for n in range(NC):
                        sp.wait_ge(chunk_ready, n + 1)
                        sp.dma_start(res_dram[:, n, :], mm[:, n, :]).then_inc(res_out, 16)
                elif ev[0] == "mix":
                    sp.wait_ge(pl_done, 2)
                    sp.dma_start(wpws[:], wpw).then_inc(pw_in, 16)
                    sp.dma_start(wpls[:], wpool).then_inc(pw_in, 16)
                elif ev[0] == "dense" and ev[2] == 0 and BLOCKS[ev[1]][1] == "x1":
                    sp.wait_ge(res_out, 16 * NC)
                    wait_tile(sp, TILE["yE1"])
                    wait_all_split(sp, 3)
                    for n in range(NC):
                        sp.dma_start(res[:, n, :], res_dram[:, n, :]).then_inc(res_in, 16)
                elif ev[0] == "norm4":
                    wait_tile(sp, last_tile(INDEX["d%d_%d" % (NEIGHTH - 1, NC // 2 - 1)]))
                    for n in range(2):
                        sp.dma_start(zs2[n][:], pT[:, n, :]).then_inc(p_in, 16)
                elif ev[0] == "norm5":
                    for n in range(NC):
                        wait_residual(sp, 2, n)
                        sp.dma_start(out[:, n, :], res[:, n, :]).then_inc(out_done, 16)
            sp.wait_ge(out_done, 16 * NC)

        @block.tensor
        def _(pe):
            mm_ = nc.tensor.matmul
            order = [0]

            def ordered(ins):
                order[0] += 1
                ins.then_inc(pe_order, 1)
                pe.wait_ge(pe_order, order[0])

            def wait_slot(g):
                if g >= 2:
                    pe.wait_ge(slot_free[g % 2], g // 2)

            def three(outs, k_w, k_x, b, hi, lo, first, last):
                for j, (w, x) in enumerate(((whi, hi), (whi, lo), (wlo, hi))):
                    for half in range(2):
                        o = mm_(outs[:, half * HALF:(half + 1) * HALF], w[b % 2][:, k_w, :],
                                x[:, k_x, half * HALF:(half + 1) * HALF],
                                start=first and j == 0, stop=last and j == 2)
                return o

            def dense(b, part):
                kind, name = BLOCKS[b]
                g = TILE[name]
                if part == 0:
                    pe.wait_ge(w_lo, b + 1)
                    wait_slot(g)
                v = None if kind == "D" else operand_version(name)
                first_of_version = name in ("Dv0", "o0", "Ecb0", "x0", "u0_0", "g0")
                out_ = slot[g % 2]
                if kind in "FM" and part < 8:
                    if first_of_version:
                        if v == 3:
                            wait_all_split(pe, v)
                        else:
                            wait_split(pe, v, part)
                    o = three(out_, part, part, b, xhi, xlo, part == 0, part == 7)
                    if part == 7:
                        o.then_inc(tile_done, 1)
                elif kind == "M":
                    kc = part - 8
                    if kc == 0:
                        wait_slot(g + 1)
                        r = BRANCHES.index(name[0]) if name[0] in BRANCHES else 4
                        pe.wait_ge(y_lo, 2 * r + 2)
                    o = three(slot[(g + 1) % 2], 8 + kc, kc, b, yhi, ylo, kc == 0, kc == 1)
                    if kc == 1:
                        o.then_inc(tile_done, 1)
                else:
                    e = int(name[1:].split("_")[0])
                    t, kc = part // 4, part % 4
                    if part == 4:
                        wait_slot(g + 1)
                    w_h = whi[b % 2][:, 0:8, :].rearrange("p (k t) n -> p k t n", k=4)
                    w_l = wlo[b % 2][:, 0:8, :].rearrange("p (k t) n -> p k t n", k=4)
                    if t == 0:
                        pe.wait_ge(u_lo, UPS * e + kc + 1)
                    for j, (w, x) in enumerate(((w_h, uhi), (w_h, ulo), (w_l, uhi))):
                        for half in range(2):
                            o = mm_(slot[(g + t) % 2][:, half * HALF:(half + 1) * HALF], w[:, kc, t, :],
                                    x[:, kc, half * HALF:(half + 1) * HALF],
                                    start=kc == 0 and j == 0, stop=kc == 3 and j == 2)
                    if kc == 3:
                        o.then_inc(tile_done, 1)

            def turn(name):
                g = TILE["turned " + name]
                rows = NGATE if name[1] == "g" else P
                z = zs[int(name[2])]
                wait_evacuated(pe, name)
                wait_slot(g)
                for tb in range(NB):
                    o = nc.tensor.transpose(slot[g % 2][:, tb * rows:(tb + 1) * rows], z[0:rows, tb * P:(tb + 1) * P],
                                            t_("ident")[0:rows, 0:rows])
                o.then_inc(tile_done, 1)

            def ytrans(g, n):
                wait_slot(g)
                for tb in range(NB):
                    o = nc.tensor.transpose(slot[g % 2][:, tb * P:(tb + 1) * P], ytok[:, tb, n * P:(n + 1) * P],
                                            t_("ident"))
                o.then_inc(tile_done, 1)

            def column_sum(k, acc, added, n):
                pe.wait_ge(added, n)
                pe.wait_ge(nstd, k)
                for half in range(2):
                    o = mm_(psb[half], t_("ones"), acc[:, half * HALF:(half + 1) * HALF], start=True, stop=True)
                o.then_inc(nsum, 1)

            def chunk_sums(k, j):
                if k:
                    pe.wait_ge(nstd, k)
                for n in range(NC):
                    pe.wait_ge(pq_done, 8 * j + n + 1)
                    for half in range(2):
                        o = mm_(psb[half], t_("ones"), sbuf[n % 2][:, half * HALF:(half + 1) * HALF],
                                start=n == 0, stop=n == 7)
                    if n < 7:
                        o.then_inc(pq_used, 1)
                o.then_inc(nsum, 1)

            def retention(n):
                if n < NB:
                    if n == 0:
                        wait_evacuated(pe, "turned Dt1")
                        wait_evacuated(pe, "Dk1")
                        wait_evacuated(pe, "Dk0")
                        pe.wait_ge(mod_done, 2)
                    if n >= 2:
                        pe.wait_ge(r_st, n - 1)
                    for h in (0, 2, 1, 3):
                        if h == 1:
                            ordered(o)
                        r0 = DH * (h % 2)
                        o = mm_(psb[n % 2][:, h * P:(h + 1) * P], dk[r0:r0 + DH, h // 2, n * P:(n + 1) * P],
                                dq[r0:r0 + DH, h // 2, n * P:(n + 1) * P], start=True, stop=True)
                    if n >= 1:
                        pe.wait_ge(r_state, min(n, NB - 1))
                    if n < NB - 1:
                        for h in range(H):
                            r0 = DH * (h % 2)
                            o = mm_(ps6[r0:r0 + DH, (h // 2) * DH:(h // 2 + 1) * DH],
                                    dt_[:, h // 2, n, r0:r0 + DH], dv[:, h // 2, n, r0:r0 + DH],
                                    start=True, stop=True)
                    o.then_inc(r_s, 1)
                if n >= 1:
                    m = n - 1
                    pe.wait_ge(r_st, m + 1)
                    if m >= 1:
                        pe.wait_ge(r_qx, m)
                        pe.wait_ge(r_state, m)
                    if m >= 1:
                        pe.wait_ge(r_y, m)
                    for h in (0, 2, 1, 3):
                        if h == 1:
                            ordered(o)
                        r0 = DH * (h % 2)
                        oo = ps7[:, h * DH:(h + 1) * DH]
                        o = mm_(oo, sbuf[m % 2][:, h * P:(h + 1) * P], dv[:, h // 2, m, r0:r0 + DH],
                                start=True, stop=m == 0)
                        if m >= 1:
                            o = mm_(oo, pbuf[m % 2][r0:r0 + DH, (h // 2) * P:(h // 2 + 1) * P],
                                    rst[r0:r0 + DH, m, h // 2, :], start=False, stop=True)
                    o.then_inc(r_o, 1)

            def transposes(m, bi):
                nb = unit(m)[4]
                done = BATCH_END[m] - batches(m) + bi
                if done >= 1:
                    pe.wait_ge(s_ptsb, done)
                for c in range(4 * bi, min(nb, 4 * bi + 4)):
                    o = nc.tensor.transpose(ps6[:, (c - 4 * bi) * P:(c - 4 * bi + 1) * P],
                                            sring[m % 3][:, c * P:(c + 1) * P], t_("ident"))
                o.then_inc(s_pt, 1)

            def soft(u, first, count):
                m = u - 3
                if first <= m < first + count:
                    ph, h, i, lo, nb = unit(m)
                    pe.wait_ge(s_ptsb, BATCH_END[m])
                    if m in (U_FGT, U_FGT + NFGT // 2):
                        wait_evacuated(pe, "turned Ev%d" % (h // 2))
                    if m >= 1:
                        pe.wait_ge(s_norm, m)
                    for c in range(nb):
                        if ph == "SWA":
                            v = brv[:, 0, lo + c, DH * (h // 2):DH * (h // 2) + DH]
                        elif ph == "SEL":
                            v = brv[:, 0, lo + c, 0:DH]
                        elif ph == "WIN":
                            v = brv[:, 0, lo + c, DH:2 * DH]
                        else:
                            v = brv[:, h // 2, lo + c, DH * (h % 2):DH * (h % 2) + DH]
                        o = mm_(ps7[:, 0:DH], ptr[:, c * P:(c + 1) * P], v, start=c == 0, stop=c == nb - 1)
                    o.then_inc(s_out, 1)
                m = u - 2
                if first <= m < first + count:
                    pe.wait_ge(s_exp, m + 1)
                    transposes(m, 0)
                if u < first + count:
                    ph, h, i, lo, nb = unit(u)
                    if u == first:
                        if ph == "SWA":
                            wait_evacuated(pe, "turned Bv0")
                            wait_evacuated(pe, "Bk1")
                            pe.wait_ge(masks_done, 1)
                            pe.wait_ge(ret_done, 1)
                        elif ph == "SEL":
                            pe.wait_ge(c_y, 4)
                        elif ph == "FGT":
                            wait_evacuated(pe, "Ef")
                    if u >= 1:
                        pe.wait_ge(s_biased, u)
                    r0 = DH * (h % 2)
                    pe.wait_ge(kl_done, sum(k <= u for k in KSPLITS))
                    pe.wait_ge(ql_done, QID[u] + 1)
                    q_h, q_l = q_parts(QID[u])
                    k_h, k_l = khif if ph == "FGT" else khi, brkl[:, KTILE[u], :]
                    w = nb * P
                    low = (ph == "SWA" and i >= 1) or (ph == "WIN" and i >= 4)
                    for c0 in range(0, w, HALF):
                        c1 = min(w, c0 + HALF)
                        for j, (q_, k_) in enumerate(((q_h, k_h), (q_h, k_l), (q_l, k_h))):
                            o = mm_(ps4[:, c0:c1], q_[r0:r0 + DH, :], k_[r0:r0 + DH, lo * P + c0:lo * P + c1],
                                    start=j == 0, stop=j == 2)
                        if low and c0 == 0:
                            o = mm_(ps4[:, 0:P], identb[:], lowb[:], start=False, stop=True, skip_group_check=True)
                        if ph == "FGT" and c1 == w:
                            o = mm_(ps4[:, w - P:w], identb[:], upb[:], start=False, stop=True,
                                    skip_group_check=True)
                    o.then_inc(s_scores, 1)
                m = u - 2
                if first <= m < first + count and batches(m) > 1:
                    transposes(m, 1)

            def stick(s):
                if s < NSTICK:
                    h, half, j = STICK[s]
                    c0 = stick_q0(s)
                    r0 = DH * (h % 2)
                    if s == 0:
                        wait_evacuated(pe, "Ck1")
                        wait_evacuated(pe, "Ck0")
                        wait_evacuated(pe, "turned Cv1")
                        pe.wait_ge(s_norm, NSWA)
                    if s >= 3:
                        pe.wait_ge(k_a, s - 2)
                    mm_(skz[s % 3][:, c0:HALF], brk[r0:r0 + DH, h // 2, j * P:(j + 1) * P],
                        brq[r0:r0 + DH, h // 2, half * HALF + c0:(half + 1) * HALF],
                        start=True, stop=True).then_inc(k_z, 1)
                if 2 <= s < NSTICK + 2:
                    m = s - 2
                    h, half, j = STICK[m]
                    c0 = stick_q0(m)
                    first = j == 4 * half + 3
                    pe.wait_ge(k_sp, m + 1)
                    o = mm_(skz[m % 3][:, c0:HALF], t_("tri"), skt[m % 4][:, c0:HALF], start=False, stop=first,
                            skip_group_check=True)
                    if not first:
                        pe.wait_ge(k_sum, m)
                        o = mm_(skz[m % 3][:, c0:HALF], t_("negones"), skl[m % 2][:, c0:HALF], start=False,
                                stop=True, skip_group_check=True)
                    o.then_inc(k_r, 1)
                if s >= 3:
                    m = s - 3
                    h, half, j = STICK[m]
                    c0 = stick_q0(m)
                    pe.wait_ge(k_a, m + 1)
                    pe.wait_ge(k_mask, DIAG_COUNT[m])
                    if half == 0 and j == 3 and h >= 1:
                        pe.wait_ge(k_y, h)
                    for i in range(c0 // P, 4):
                        qb = 4 * half + i
                        o = mm_(ps7[:, qb * DH:(qb + 1) * DH], ska[m % 2][:, i * P:(i + 1) * P],
                                brv[:, h // 2, j, DH * (h % 2):DH * (h % 2) + DH],
                                start=(half == 0 and j == 3 and i == 3), stop=(half == 1 and j == 0 and i == 3),
                                skip_group_check=True)
                    o.then_inc(k_o, 1)

            def compress(s):
                if s == 0:
                    pe.wait_ge(cmp_in, 32)
                    pe.wait_ge(c_pos, 1)
                    for j in range(2):
                        zt = acmp[j * DH:(j + 1) * DH, :].rearrange("d (c l) -> d l c", l=32)
                        for l in range(32):
                            o = mm_(psb[j][0:DH, 0:NCMP], cw1s[j * DH:(j + 1) * DH, l, :], zt[:, l, :],
                                    start=l == 0, stop=l == 31)
                    o.then_inc(c_h, 1)
                elif s == 1:
                    pe.wait_ge(c_hs, 2)
                    mm_(ps6[:, 0:NCMP], cw2s[:, 0:2 * DH], hsil[:, 0:NCMP], start=True, stop=True)
                    mm_(ps7[:, 0:DH], hsil[:, NCMP:5 * NCMP], cw2s[:, 2 * DH:3 * DH],
                        start=True, stop=True).then_inc(c_kv, 1)
                elif s == 2:
                    pe.wait_ge(c_kvs, 2)
                    wait_evacuated(pe, "Aq0")
                    wait_evacuated(pe, "Aq1")
                    for h in (0, 2, 1, 3):
                        if h == 1:
                            ordered(o)
                        r0 = DH * (h % 2)
                        for i in range(NB):
                            c = h * NB * NCMP + i * NCMP
                            o = mm_(ps4[:, c:c + NCMP], brq[r0:r0 + DH, h // 2, i * P:(i + 1) * P],
                                    kct[r0:r0 + DH, :], start=True, stop=True)
                    o.then_inc(c_s, 1)
                elif s == 3:
                    pe.wait_ge(c_p, 1)
                    for half in range(2):
                        if half:
                            pe.wait_ge(c_tb, 1)
                        for c in range(4):
                            o = nc.tensor.transpose(ps6[:, c * P:(c + 1) * P],
                                                    sbuf[0][:, half * HALF + c * P:half * HALF + (c + 1) * P],
                                                    t_("ident"))
                        o.then_inc(c_t, 1)
                elif s == 4:
                    pe.wait_ge(c_tb, 2)
                    for h in range(H):
                        if h:
                            pe.wait_ge(c_y, h)
                        for i in (0, 4, 1, 5, 2, 6, 3, 7):
                            if 0 < i < 4:
                                ordered(o)
                            r0 = 32 * (i % 4)
                            c = (h * 2 + i // 4) * P
                            o = mm_(ps7[:, i * DH:(i + 1) * DH], pbuf[1][r0:r0 + 32, c:c + P],
                                    vc4[r0:r0 + 32, :], start=True, stop=True, tile_position=(r0, 0))
                        o.then_inc(c_o, 1)

            def forget_prep(s):
                if s == 0:
                    pe.wait_ge(f_c, 1)
                    for tb in range(NB):
                        o = nc.tensor.transpose(ps7[:, tb * 4:tb * 4 + 4], ct[0:4, tb * P:(tb + 1) * P],
                                                t_("ident")[0:4, 0:4])
                    o.then_inc(f_ct, 1)

            pe.wait_ge(small_in, 32)

            def modulation(t):
                pe.wait_ge(ada_acc, {1: 1, 0: 2, 2: 3}[t])
                for n in range(NC):
                    o = mm_(ps6[:, 8 * t + n:8 * t + n + 1], ada_sum[t][:, n * P:(n + 1) * P], t_("ones", 0, 1),
                            start=True, stop=True)
                return o

            modulation(1)
            chunk_sums(0, 0)
            modulation(0).then_inc(mod_mm, 1)

            for ev in TIMELINE:
                if ev[0] == "dense":
                    dense(ev[1], ev[2])
                elif ev[0] == "turn":
                    turn(ev[1])
                elif ev[0] == "gate_mod":
                    pe.wait_ge(mod_done, 1)
                    modulation(2).then_inc(mod_mm, 1)
                elif ev[0] == "ytrans":
                    if ev[2] == 0:
                        if ev[1] == "D":
                            pe.wait_ge(ret_done, 1)
                        elif ev[1] == "B":
                            pe.wait_ge(s_norm, NSWA)
                        elif ev[1] == "C":
                            pe.wait_ge(k_y, H)
                        else:
                            pe.wait_ge(s_norm, NSWA + NSEL + NWIN)
                    ytrans(TILE["y%s%d" % (ev[1], ev[2])], ev[2])
                elif ev[0] == "ret":
                    retention(ev[1])
                elif ev[0] == "soft":
                    if ev[2] == U_FGT and ev[1] < U_FGT + NFGT and unit(ev[1])[2] == 0:
                        h = unit(ev[1])[1]
                        if h == 0:
                            pe.wait_ge(f_ci, 1)
                            wait_evacuated(pe, "Ef")
                        pe.wait_ge(s_biased, ev[1])
                        for half in range(2):
                            o = mm_(psb[half], t_("ident")[0:4, h:h + 1].to_broadcast([4, P]), ct[0:4, half * HALF:(half + 1) * HALF],
                                    start=True, stop=True)
                        o.then_inc(f_bc, 1)
                        pe.wait_ge(f_cb, h + 1)
                    soft(ev[1], ev[2], ev[3])
                elif ev[0] == "stick":
                    stick(ev[1])
                elif ev[0] == "cmp":
                    compress(ev[1])
                elif ev[0] == "fprep":
                    forget_prep(ev[1])
                elif ev[0] == "norm2":
                    column_sum(1, pbuf[0], sq_added, 7)
                    column_sum(2, acc2, tq_added, 7)
                elif ev[0] == "norm3":
                    column_sum(3, pbuf[0], sq_added, 14)
                    chunk_sums(4, 1)
                elif ev[0] == "norm4":
                    chunk_sums(5, 2)
                    chunk_sums(6, 3)
                elif ev[0] == "norm5":
                    column_sum(7, pbuf[0], sq_added, 21)
                elif ev[0] == "mix":
                    pe.wait_ge(s_norm, 128)
                    for n in range(2):
                        ytrans(TILE["yE%d" % n], n)
                    pe.wait_ge(pw_in, 32)
                    pe.wait_ge(pl_done, 2)
                    for t in range(2):
                        if t:
                            pe.wait_ge(m_pool_in, 1)
                        for half in range(2):
                            o = mm_(psb[half], wpls[:, t, :], ply[:, t, half * HALF:(half + 1) * HALF],
                                    start=True, stop=True)
                        o.then_inc(m_pool, 1)
                    pe.wait_ge(m_pool_in, 2)
                    for t in range(2):
                        pe.wait_ge(conf_done, 2)
                        for half in range(2):
                            o = mm_(psb[half], t_("ones"), cacc[:, t, half * HALF:(half + 1) * HALF],
                                    start=t == 0, stop=t == 1)
                    o.then_inc(m_mean, 1)
                    pe.wait_ge(m_sq, 2)
                    for t in range(2):
                        for half in range(2):
                            o = mm_(psb[half], t_("ones"), sbuf[t][:, half * HALF:(half + 1) * HALF],
                                    start=t == 0, stop=t == 1)
                    o.then_inc(m_var, 1)
                    pe.wait_ge(m_silu, 2)
                    for n in range(2):
                        if n:
                            pe.wait_ge(m_pw_in, 1)
                        for t in range(2):
                            for half in range(2):
                                o = mm_(psb[half], wpws[:, t, n * P:(n + 1) * P],
                                        cacc[:, t, half * HALF:(half + 1) * HALF], start=t == 0, stop=t == 1)
                        o.then_inc(m_pw, 1)

        @block.scalar
        def _(act):
            def split_weights(b):
                act.wait_ge(raw_in, 16 * (b + 1))
                if b >= 2:
                    wait_tile(act, last_tile(b - 2))
                n = BLOCK_LEN[b]
                nc.scalar.activation(flat(whi[b % 2])[:, 0:n], raw[:, 0:n], ACT.Copy).then_inc(w_hi, 1)

            def split_wide(k, src):
                nc.scalar.activation(xhi[:, k, :], src, ACT.Copy).then_inc(x_hi, 1)

            def square(k, j, n, src):
                if n == 0:
                    act.wait_ge(nsum, k)
                if n >= 3:
                    act.wait_ge(sq_added, 7 * j + n - 2)
                dst = pbuf[0] if n == 0 else sbuf[n % 2]
                nc.scalar.activation(dst[:], src, ACT.Square).then_inc(sq_done, 1)

            def chunk_square(j, n, src):
                if n < 2 and j:
                    act.wait_ge(nsum, (0, 4, 5, 6)[j])
                if n >= 2:
                    act.wait_ge(pq_used, 7 * j + n - 1)
                nc.scalar.activation(sbuf[n % 2][:], src, ACT.Square).then_inc(pq_done, 1)

            def std(k):
                act.wait_ge(nsum, k + 1)
                if k:
                    act.wait_ge(napplied, k)
                nc.scalar.activation(pbuf[1][:], ps4[:], ACT.Sqrt, bias=t_("eps6"), scale=1.0 / D).then_inc(nstd, 1)

            def evacuate(b):
                kind, name = BLOCKS[b]
                g = TILE[name]
                if name[0] in "DBCAE" and name[1] in "qk" and name[2:] in ("0", "1"):
                    wait_tile(act, g)
                    t = int(name[2])
                    q = name[1] == "q"
                    dst = ((dq if q else dk) if name[0] == "D" else (brq if q else brk))[:, t, :]
                    nc.scalar.activation(dst, slot[g % 2][:], ACT.Copy,
                                         scale=QSCALE if q else 1.0).then_inc(slot_free[g % 2], 1)
                elif name == "Acmp":
                    wait_tile(act, g)
                    nc.scalar.activation(acmp[:], slot[g % 2][:], ACT.Copy).then_inc(slot_free[g % 2], 1)
                elif name[0] in "DBCAE" and name[1] in "vtg":
                    br, t = name[0], int(name[2])
                    rows = NGATE if name[1] == "g" else P
                    wait_tile(act, g)
                    if name[1] == "t":
                        wait_tile(act, TILE["turned Dv%d" % t])
                    elif br == "B":
                        wait_tile(act, TILE["turned Dt%d" % t])
                    elif br == "C" and t == 0:
                        wait_evacuated(act, "Dm7", 1)
                    elif br == "C":
                        act.wait_ge(s_scores, NSWA)
                    elif br == "A" and t == 0:
                        act.wait_ge(sum_done, 8)
                    elif br == "A":
                        act.wait_ge(y_lo, 4)
                    elif br == "E" and t == 0:
                        wait_evacuated(act, "Eca1")
                    elif br == "E":
                        wait_all_split(act, 2)
                    nc.scalar.activation(zs[t][0:rows, :], slot[g % 2][0:rows, :],
                                         ACT.Sigmoid if name[1] == "g" else ACT.Copy).then_inc(slot_free[g % 2], 1)
                elif name[0] in "DBCA" and name[1] == "z":
                    r, t = BRANCHES.index(name[0]), int(name[2])
                    wait_tile(act, g)
                    if r < 3:
                        wait_tile(act, TILE["turned " + ("Bv0", "Cv%d" % t, "Av0" if t == 0 else "Ag1")[r]])
                    elif t == 0:
                        act.wait_ge(sum_done, 8 * (r - 1))
                    else:
                        act.wait_ge(s_scores, U_FGT)
                    nc.scalar.activation(zs[t][:], slot[g % 2][:], ACT.Silu).then_inc(slot_free[g % 2], 1)
                elif name[0] in "DBCA" and name[1] == "m":
                    r, n = BRANCHES.index(name[0]), int(name[2])
                    wait_tile(act, g)
                    if n == 0:
                        act.wait_ge(y_lo, 2 * r + 1)
                    elif r == 0:
                        wait_evacuated(act, "Dm%d" % (n - 1), 1)
                    else:
                        act.wait_ge(sum_done, 8 * (r - 1) + n)
                    nc.scalar.activation(zs[0][:], slot[g % 2][:], ACT.Sigmoid).then_inc(slot_free[g % 2], 1)
                elif name[0] == "o":
                    wait_evacuated(act, name)
                    n = int(name[1])
                    square(1, 0, n, mm[:, n, :])
                    if n >= 3:
                        act.wait_ge(tq_added, n - 2)
                    nc.scalar.activation((acc2 if n == 0 else sqr2[n % 2])[:], mm[:, n, :], ACT.Square,
                                         scale=v_("final_g", n, 1)).then_inc(tq_done, 1)
                elif name == "Ef":
                    wait_tile(act, g)
                    nc.scalar.activation(ct[0:4, :], slot[g % 2][0:4, :], ACT.Identity, bias=v_("bf")[0:4, :]
                                         ).then_inc(slot_free[g % 2], 1)
                    act.wait_ge(f_abs, 1)
                    nc.scalar.activation(cb[0:4, :], cb[0:4, :], ACT.Exp, scale=-1.0).then_inc(act_chain, 1)
                    act.wait_ge(act_chain, NSTICK + 1)
                    nc.scalar.activation(cb[0:4, :], cb[0:4, :], ACT.Ln, bias=1.0).then_inc(f_log, 1)
                elif name in ("Ecb0", "Ecb1", "Esh0", "Esh1"):
                    wait_tile(act, g)
                    if name == "Ecb0":
                        wait_all_split(act, 2)
                    if name == "Ecb1":
                        wait_evacuated(act, "Eca0")
                    if name == "Esh0":
                        wait_tile(act, TILE["turned Ev1"])
                    if name == "Esh1":
                        wait_evacuated(act, "Esc0")
                    z, f = (zs[0], ACT.Sigmoid) if name[1] == "c" else (zs[1], ACT.Copy)
                    nc.scalar.activation(z[:], slot[g % 2][:], f).then_inc(slot_free[g % 2], 1)
                elif name in ("Ep0", "Ep1"):
                    wait_tile(act, g)
                    if name == "Ep1":
                        wait_evacuated(act, "Esb1")
                    nc.scalar.activation((sx if name == "Ep0" else su)[:], slot[g % 2][:], ACT.Copy
                                         ).then_inc(slot_free[g % 2], 1)
                elif name[0] == "x":
                    n = int(name[1])
                    wait_tile(act, g)
                    if n == 0:
                        wait_all_split(act, 3)
                    nc.scalar.activation(mm[:, n, :], slot[g % 2][:], ACT.Copy).then_inc(slot_free[g % 2], 1)
                    wait_evacuated(act, name)
                    square(3, 1, n, mm[:, n, :])
                elif name[0] == "u":
                    e, n = (int(v) for v in name[1:].split("_"))
                    if e and n == 0:
                        wait_tile(act, last_tile(INDEX["d%d_%d" % (e - 1, NC // 2 - 1)]))
                    act.wait_ge(u_src, UPS * e + n + 1)
                    nc.scalar.activation(uhi[:, n, :], tbuf[n % 2][:], ACT.Copy).then_inc(u_hi, 1)
                elif name[0] == "d":
                    e, m = (int(v) for v in name[1:].split("_"))
                    for t in range(2):
                        n, gg = 2 * m + t, g + t
                        if e == 0:
                            wait_tile(act, gg)
                            nc.scalar.activation(mm[:, n, :], slot[gg % 2][:], ACT.Copy
                                                 ).then_inc(slot_free[gg % 2], 1)
                elif name[0] == "g":
                    n = int(name[1])
                    wait_tile(act, g)
                    if n < 2:
                        act.wait_ge(y_lo, 10)
                    else:
                        wait_evacuated(act, "g%d" % (n - 2), 1)
                    nc.scalar.activation(zs2[n % 2][:], slot[g % 2][:], ACT.Sigmoid).then_inc(slot_free[g % 2], 1)
                    wait_evacuated(act, name, 1)
                    square(7, 2, n, mm[:, n, :])

            def soft(u, first, count):
                m = u - 2
                if first <= m < first + count:
                    nb = unit(m)[4]
                    if m >= 1:
                        act.wait_ge(s_out, m)
                    for bi in range(batches(m)):
                        act.wait_ge(s_pt, BATCH_END[m] - batches(m) + bi + 1)
                        w = P * (min(nb, 4 * bi + 4) - 4 * bi)
                        nc.scalar.activation(ptr[:, bi * HALF:bi * HALF + w], ps6[:, 0:w], ACT.Copy
                                             ).then_inc(s_ptsb, 1)
                if u < first + count:
                    ph, h, i, lo, nb = unit(u)
                    act.wait_ge(s_negmax, u + 1)
                    if ph == "SWA":
                        nc.scalar.activation(esk[:, u % 4:u % 4 + 1], v_("sink", h, 1), ACT.Exp,
                                             bias=nmx[:, u % 4:u % 4 + 1]).then_inc(s_esk, 1)
                    w = nb * P
                    nc.scalar.activation(sring[u % 3][:, 0:w], sring[u % 3][:, 0:w], ACT.Exp,
                                         bias=nmx[:, u % 4:u % 4 + 1],
                                         accum_out=den[:, u % 4:u % 4 + 1]).then_inc(s_exp, 1)

            def stick(s):
                if 2 <= s < NSTICK + 2:
                    m = s - 2
                    c0 = stick_q0(m)
                    act.wait_ge(k_r, m + 1)
                    if m >= 2:
                        act.wait_ge(k_o, m - 1)
                    nc.scalar.activation(ska[m % 2][:, c0:HALF], skz[m % 3][:, c0:HALF], ACT.Exp).then_inc(k_a, 1)
                if s < NSTICK:
                    c0 = stick_q0(s)
                    t = skt[s % 4][:, c0:HALF]
                    act.wait_ge(k_abs, s + 1)
                    nc.scalar.activation(t, t, ACT.Exp, scale=-1.0).then_inc(act_chain, 1)
                    act.wait_ge(act_chain, s + 1)
                    nc.scalar.activation(t, t, ACT.Ln, bias=1.0).then_inc(k_log, 1)

            act.wait_ge(small_in, 32)
            nc.scalar.activation(csil[:], v_("c"), ACT.Silu).then_inc(csil_done, 1)
            act.wait_ge(x_in, 16)
            for n in range(NC):
                chunk_square(0, n, mm[:, n, :])
            split_weights(0)
            for ev in TIMELINE:
                if ev[0] == "dense":
                    if ev[2] == 0 and ev[1] + 1 < nblocks:
                        split_weights(ev[1] + 1)
                    if last_part(ev):
                        evacuate(ev[1])
                elif ev[0] == "ytrans":
                    br, n = ev[1], ev[2]
                    r = BRANCHES.index(br)
                    wait_evacuated(act, "y%s%d" % (br, n))
                    if r:
                        wait_tile(act, last_tile(INDEX[BRANCHES[r - 1] + "m7"]))
                    nc.scalar.activation(yhi[:, n, :], zs[n][:], ACT.Copy).then_inc(y_hi, 1)
                elif ev[0] == "retnorm":
                    act.wait_ge(r_var, 1)
                    nc.scalar.activation(st32[:, 2, :], st32[:, 1, :], ACT.Sqrt, bias=t_("eps5"),
                                         scale=1.0 / DH).then_inc(r_sq, 1)
                elif ev[0] == "soft":
                    if ev[2] == U_FGT and ev[1] < U_FGT + NFGT and unit(ev[1])[2] == 0:
                        h = unit(ev[1])[1]
                        act.wait_ge(f_bc, h + 1)
                        nc.scalar.activation(cb[:], ps4[:], ACT.Copy).then_inc(f_cb, 1)
                    for m in query_ids(*ev[1:]):
                        ph, t, i = QKEY[QFIRST[m]]
                        wait_evacuated(act, {"SWA": "B", "FGT": "E"}.get(ph, "A") + "q%d" % t)
                        if m >= 2:
                            act.wait_ge(s_scores, QLAST[m - 2] + 1)
                        nc.scalar.activation(q_parts(m)[0], brq[:, t, i * P:(i + 1) * P], ACT.Copy
                                             ).then_inc(qh_done, 1)
                    soft(ev[1], ev[2], ev[3])
                elif ev[0] == "ksplit":
                    u = ev[1]
                    ph, t = unit(u)[0], KTILE[u]
                    wait_evacuated(act, {"SWA": "B", "FGT": "E"}.get(ph, "A") + "k%d" % t)
                    if ph == "FGT":
                        act.wait_ge(res_out, 16 * NC)
                    else:
                        act.wait_ge(y_lo, 2 if ph == "SWA" else 6)
                    if u:
                        act.wait_ge(s_scores, u)
                    nc.scalar.activation((khif if ph == "FGT" else khi)[:], brk[:, t, :], ACT.Copy
                                         ).then_inc(kh_done, 1)
                elif ev[0] == "stick":
                    stick(ev[1])
                elif ev[0] == "cmp":
                    if ev[1] == 1:
                        act.wait_ge(c_h, 1)
                        nc.scalar.activation(hsil[:, 0:NCMP], psb[0][0:DH, 0:NCMP], ACT.Silu).then_inc(c_hs, 1)
                        nc.scalar.activation(hsil[:, NCMP:].rearrange("p (a c) -> p a c", a=4),
                                             psb[1][0:DH, 0:NCMP].unsqueeze(1).to_broadcast([DH, 4, NCMP]), ACT.Silu
                                             ).then_inc(c_hs, 1)
                        act.wait_ge(c_kv, 1)
                        nc.scalar.activation(kct[:], ps6[:, 0:NCMP], ACT.Copy).then_inc(c_kvs, 1)
                        nc.scalar.activation(vc4[:], ps7[:, 0:DH], ACT.Copy).then_inc(c_kvs, 1)
                    elif ev[1] == 2:
                        act.wait_ge(c_sb, 1)
                        nc.scalar.activation(sbuf[0][:], sbuf[0][:], ACT.Exp).then_inc(c_e, 1)
                    elif ev[1] == 3:
                        for half in range(2):
                            act.wait_ge(c_t, half + 1)
                            nc.scalar.activation(pbuf[1][:, half * HALF:(half + 1) * HALF], ps6[:], ACT.Copy
                                                 ).then_inc(c_tb, 1)
                elif ev[0] == "fprep":
                    act.wait_ge(f_ct, 1)
                    nc.scalar.activation(flat(ci), ps7[:, 0:4 * NB], ACT.Copy).then_inc(f_ci, 1)
                elif ev[0] == "norm1":
                    std(0)
                    act.wait_ge(mod_mm, 1)
                    for n in range(NC):
                        act.wait_ge(x_src, n + 1)
                        split_wide(n, mm[:, n, :])
                elif ev[0] == "split_merged":
                    wait_tile(act, LAST_USE[1])
                    for n in range(NC):
                        act.wait_ge(sum_done, 16 + n + 1)
                        split_wide(n, mm[:, n, :])
                elif ev[0] == "norm2":
                    std(1)
                    act.wait_ge(n2_t, 1)
                    nc.scalar.activation(pbuf[0][:], pbuf[0][:], ACT.Sqrt, bias=t_("eps6"),
                                         scale=1.0 / D).then_inc(nstd, 1)
                    wait_tile(act, LAST_USE[2])
                    for n in range(NC):
                        act.wait_ge(x_src, 8 + n + 1)
                        split_wide(n, res[:, n, :])
                elif ev[0] in ("norm3", "norm4"):
                    k = 3 if ev[0] == "norm3" else 5
                    if k == 5:
                        for n in range(2):
                            wait_evacuated(act, "d%d_%d" % (NEIGHTH - 1, NC // 2 - 1), n)
                        for n in range(NC):
                            chunk_square(2, n, mm[:, n, :])
                    std(k)
                    for n in range(NC):
                        wait_residual(act, int(k == 5), n)
                        chunk_square(1 if k == 3 else 3, n, res[:, n, :])
                    std(k + 1)
                    wait_tile(act, LAST_USE[4 if k == 3 else 5])
                    for n in range(NC):
                        act.wait_ge(x_src, 16 + 8 * (k == 5) + n + 1)
                        split_wide(n, mm[:, n, :])
                    if k == 5:
                        act.wait_ge(p_in, 32)
                        for n in range(2):
                            nc.scalar.activation(yhi[:, n, :], zs2[n][:], ACT.Copy).then_inc(y_hi, 1)
                elif ev[0] == "norm5":
                    std(7)
                elif ev[0] == "mix":
                    wait_tile(act, LAST_USE[3])
                    act.wait_ge(sc_done, 2)
                    for t in range(2):
                        split_wide(4 + t, scy[:, t, :])
                    for t in range(2):
                        act.wait_ge(mix_src, 1 + t)
                        split_wide(2 + t, pbuf[t][:])
                    for t in range(2):
                        act.wait_ge(mix_src, 3 + t)
                        split_wide(6 + t, ply[:, t, :])
                    for t in range(2):
                        act.wait_ge(m_cent, t + 1)
                        nc.scalar.activation(sbuf[t][:], cacc[:, t, :], ACT.Square).then_inc(m_sq, 1)
                    act.wait_ge(m_var, 1)
                    act.wait_ge(pl_done, 2)
                    nc.scalar.activation(sx[:], ps4[:], ACT.Sqrt, bias=t_("eps6"), scale=1.0 / BW).then_inc(m_std, 1)
                    for t in range(2):
                        act.wait_ge(m_hat, t + 1)
                        nc.scalar.activation(cacc[:, t, :], cacc[:, t, :], ACT.Silu, bias=v_("ln_b", t, 1),
                                             scale=v_("ln_g", t, 1)).then_inc(m_silu, 1)
                    for t in range(2):
                        act.wait_ge(mix_src, 5 + t)
                        split_wide(t, cu[:, t, :])

        @block.gpsimd
        def _(pool):
            tt = nc.gpsimd.tensor_tensor

            def split_weights(b):
                n = BLOCK_LEN[b]
                pool.wait_ge(w_hi, b + 1)
                tt(flat(wlo[b % 2])[:, 0:n], raw[:, 0:n], flat(whi[b % 2])[:, 0:n].bitcast(F32),
                   ALU.subtract).then_inc(w_lo, 1)

            def split_wide(v, pos, k, src):
                if pos % 2:
                    pool.wait_ge(x_hi, 8 * v + pos + 1)
                    tt(xlo[:, k, :], src, xhi[:, k, :].bitcast(F32), ALU.subtract).then_inc(x_lo, 1)

            def add_square(j, n):
                if n:
                    pool.wait_ge(sq_done, 8 * j + n + 1)
                    if n > 1:
                        pool.wait_ge(sq_added, 7 * j + n - 1)
                    tt(pbuf[0][:], pbuf[0][:], sbuf[n % 2][:], ALU.add).then_inc(sq_added, 1)

            def split_narrow(n, src):
                pool.wait_ge(y_hi, n + 1)
                tt(ylo[:, n % 2, :], src, yhi[:, n % 2, :].bitcast(F32), ALU.subtract).then_inc(y_lo, 1)

            def add_residual(k):
                for n in range(1, NC, 2):
                    pool.wait_ge(t_ready, 8 * k + n + 1)
                    if k == 0:
                        pool.wait_ge(res_in, 16 * NC)
                    tt(res[:, n, :], res[:, n, :], mm[:, n, :], ALU.add).then_inc(res_odd, 1)

            chain = [0]

            def link(ins):
                chain[0] += 1
                ins.then_inc(pool_chain, 1)
                pool.wait_ge(pool_chain, chain[0])

            def window_sums(t):
                v = (sx, su)[t]
                wait_evacuated(pool, "Ep%d" % t)
                if t == 0:
                    wait_evacuated(pool, "Esc1")
                    wait_evacuated(pool, "Eca1")
                else:
                    pool.wait_ge(pl_done, 1)
                src = v
                for step in range(1 + 2 * t + 1):
                    last = step == 2 * t + 1
                    sh = 1 << step
                    dst = zs[step % 2]
                    link(nc.gpsimd.tensor_copy(dst[:, 0:sh], src[:, 0:sh]))
                    ins = tt(dst[:, sh:S], src[:, sh:S], src[:, 0:S - sh], ALU.add)
                    if last:
                        ins.then_inc(pl_in, 1)
                    else:
                        link(ins)
                    src = dst

            split_weights(0)
            for ev in TIMELINE:
                if ev[0] == "dense":
                    kind, name = BLOCKS[ev[1]]
                    if ev[2] == 0 and ev[1] + 1 < nblocks:
                        split_weights(ev[1] + 1)
                    if last_part(ev):
                        if name[0] in "BCA" and name[1] == "m":
                            r, n = BRANCHES.index(name[0]), int(name[2])
                            wait_evacuated(pool, name, 1)
                            tt(mm[:, n, :], mm[:, n, :], zs[0][:], ALU.add).then_inc(sum_done, 1)
                        elif name[0] == "o":
                            n = int(name[1])
                            add_square(0, n)
                            if n:
                                pool.wait_ge(tq_done, n + 1)
                                if n > 1:
                                    pool.wait_ge(tq_added, n - 1)
                                tt(acc2[:], acc2[:], sqr2[n % 2][:], ALU.add).then_inc(tq_added, 1)
                        elif name[0] == "x":
                            add_square(1, int(name[1]))
                        elif name[0] == "u":
                            e, n = (int(v) for v in name[1:].split("_"))
                            pool.wait_ge(u_hi, UPS * e + n + 1)
                            tt(ulo[:, n, :], tbuf[n % 2][:], uhi[:, n, :].bitcast(F32), ALU.subtract
                               ).then_inc(u_lo, 1)
                        elif name[0] == "g":
                            add_square(2, int(name[1]))
                        elif name in ("Ep0", "Ep1"):
                            window_sums(int(name[2]))
                elif ev[0] == "ytrans":
                    r = BRANCHES.index(ev[1])
                    split_narrow(2 * r + ev[2], zs[ev[2]][:])
                elif ev[0] == "soft":
                    for m in query_ids(*ev[1:]):
                        _, t, i = QKEY[QFIRST[m]]
                        q_h, q_l = q_parts(m)
                        pool.wait_ge(qh_done, m + 1)
                        tt(q_l, brq[:, t, i * P:(i + 1) * P], q_h.bitcast(F32), ALU.subtract).then_inc(ql_done, 1)
                elif ev[0] == "ret" and 1 <= ev[1] < NB:
                    n = ev[1]
                    if n == 1:
                        pool.wait_ge(rtab_in, 16)
                        wait_evacuated(pool, "Dq0")
                        wait_evacuated(pool, "Dq1")
                        pool.wait_ge(napplied, 1)
                    if n >= 2:
                        pool.wait_ge(r_o, n - 1)
                    tt(pbuf[n % 2][:, 0:2 * P].rearrange("p (t q) -> p t q", t=2), dq[:, :, n * P:(n + 1) * P],
                       xi, ALU.mult).then_inc(r_qx, 1)
                elif ev[0] == "stick":
                    m = ev[1] - 2
                    if 0 <= m < NSTICK and STICK_DIAG[m]:
                        c0 = stick_q0(m)
                        pool.wait_ge(k_a, m + 1)
                        blk = ska[m % 2][:, c0:c0 + P]
                        nc.gpsimd.affine_select(out=blk, in_=blk, compare_op=ALU.is_gt, fill=0.0, base=0,
                                                pattern=[[1, P]], channel_multiplier=-1).then_inc(k_mask, 1)
                    m = ev[1] - 1
                    if 0 <= m < NSTICK:
                        h, half, j = STICK[m]
                        c0 = stick_q0(m)
                        pool.wait_ge(k_sp, m + 1)
                        if j == 4 * half + 3:
                            if m:
                                pool.wait_ge(k_r, m)
                                pool.wait_ge(k_sum, m)
                            else:
                                pool.wait_ge(s_norm, NSWA)
                            link(nc.gpsimd.memset(skl[0][:], 0.0))
                            link(nc.gpsimd.memset(skl[1][:], 0.0))
                        elif m:
                            pool.wait_ge(k_r, m)
                            pool.wait_ge(k_sum, m)
                        tt(skl[(m + 1) % 2][:, c0:HALF], skl[m % 2][:, c0:HALF], skt[m % 4][:, c0:HALF],
                           ALU.add).then_inc(k_sum, 1)
                elif ev[0] in ("norm1", "split_merged"):
                    for n in range(NC):
                        split_wide(int(ev[0] != "norm1"), n, n, mm[:, n, :])
                elif ev[0] == "norm2":
                    for n in range(NC):
                        split_wide(2, n, n, res[:, n, :])
                elif ev[0] in ("norm3", "norm4"):
                    k = 3 if ev[0] == "norm3" else 5
                    add_residual((k - 3) // 2)
                    for n in range(NC):
                        split_wide(4 if k == 3 else 5, n, n, mm[:, n, :])
                    if k == 5:
                        for n in range(2):
                            split_narrow(8 + n, zs2[n][:])
                elif ev[0] == "norm5":
                    add_residual(2)
                elif ev[0] == "mix":
                    for pos, (k, src) in enumerate(mix_sources):
                        split_wide(3, pos, k, src)

        @block.vector
        def _(dve):
            v = nc.vector
            chain = [0]

            def link(ins):
                chain[0] += 1
                ins.then_inc(dve_chain, 1)
                dve.wait_ge(dve_chain, chain[0])

            def rstd(k):
                dve.wait_ge(nstd, k + 1)
                link(v.reciprocal(pbuf[1][:], pbuf[1][:]))

            def scaled(dst, src, g, s_):
                v.scalar_tensor_tensor(out=dst, in0=src, scalar=g, in1=pbuf[1][:], op0=ALU.mult, op1=ALU.mult
                                       ).then_inc(s_, 1)

            def add_residual(k, j, post):
                rstd(k)
                if j == 0:
                    dve.wait_ge(res_in, 16 * NC)
                for n in range(NC):
                    scaled(mm[:, n, :], mm[:, n, :], v_(post, n, 1), t_ready)
                    if n % 2 == 0:
                        dve.wait_ge(t_ready, 8 * j + n + 1)
                        v.tensor_tensor(res[:, n, :], res[:, n, :], mm[:, n, :], ALU.add).then_inc(res_added, 1)

            def applied(k, s_, n):
                dve.wait_ge(s_, n)
                if k:
                    dve.wait_ge(napplied, k)
                v.tensor_copy(fac[:, 0:1], fac[:, 1:2]).then_inc(napplied, 1)

            def copy_out(name, dst, extra=0):
                g = TILE[name] + extra
                wait_tile(dve, g)
                v.tensor_copy(dst, slot[g % 2][:]).then_inc(slot_free[g % 2], 1)

            def evacuate(b):
                kind, name = BLOCKS[b]
                g = TILE[name]
                if name[0] in "DBCA" and name[1] == "m":
                    r, n = BRANCHES.index(name[0]), int(name[2])
                    wait_tile(dve, g + 1)
                    wait_evacuated(dve, name)
                    dst = mm[:, n, :] if r == 0 else zs[0][:]
                    v.tensor_tensor(dst, slot[(g + 1) % 2][:], zs[0][:], ALU.mult
                                    ).then_inc(slot_free[(g + 1) % 2], 1)
                elif name[0] == "o":
                    n = int(name[1])
                    wait_tile(dve, g)
                    dve.wait_ge(xres_in, 16 * NC)
                    v.scalar_tensor_tensor(out=mm[:, n, :], in0=slot[g % 2][:], scalar=mod[:, 16 + n:17 + n],
                                           in1=mm[:, n, :], op0=ALU.mult, op1=ALU.add).then_inc(slot_free[g % 2], 1)
                elif name == "Ef":
                    wait_evacuated(dve, "Ef")
                    v.tensor_scalar(cb[0:4, :].bitcast(I32), ct[0:4, :].bitcast(I32), 0x7FFFFFFF, None,
                                    ALU.bitwise_and).then_inc(f_abs, 1)
                    link(v.memset(pbuf[1][0:4, :], 1.0))
                    dve.wait_ge(f_log, 1)
                    link(v.scalar_tensor_tensor(out=pbuf[0][0:4, :], in0=ct[0:4, :], scalar=0.0, in1=cb[0:4, :],
                                                op0=ALU.min, op1=ALU.subtract))
                    v.tensor_tensor_scan(ct[0:4, :], pbuf[1][0:4, :], pbuf[0][0:4, :], 0.0, ALU.mult, ALU.add
                                         ).then_inc(f_c, 1)
                elif name in ("Eca0", "Eca1"):
                    t = int(name[3])
                    wait_tile(dve, g)
                    wait_evacuated(dve, "Ecb%d" % t)
                    v.tensor_tensor(cu[:, t, :], slot[g % 2][:], zs[0][:], ALU.mult).then_inc(slot_free[g % 2], 1)
                elif name in ("Esc0", "Esc1"):
                    t = int(name[3])
                    wait_tile(dve, g)
                    wait_evacuated(dve, "Esh%d" % t)
                    if t:
                        dve.wait_ge(sc_done, 1)
                    v.tensor_tensor(su[:], slot[g % 2][:], zs[1][:], ALU.mult).then_inc(slot_free[g % 2], 1)
                    wait_evacuated(dve, name)
                    link(v.tensor_scalar(scy[:, t, :], su[:], v_("sc", 3 * t + 2, 1), None, ALU.mult))
                    for k in (1, 0):
                        sh = 2 - k
                        link(v.scalar_tensor_tensor(out=scy[:, t, sh:S], in0=su[:, 0:S - sh],
                                                    scalar=v_("sc", 3 * t + k, 1), in1=scy[:, t, sh:S],
                                                    op0=ALU.mult, op1=ALU.add))
                elif name in ("Esb0", "Esb1"):
                    t = int(name[3])
                    wait_tile(dve, g)
                    v.tensor_tensor(scy[:, t, :], slot[g % 2][:], scy[:, t, :], ALU.mult
                                    ).then_inc(slot_free[g % 2], 1)
                    wait_evacuated(dve, name)
                    v.tensor_copy(fac[:, 0:1], fac[:, 1:2]).then_inc(sc_done, 1)
                elif name in ("Ep0", "Ep1"):
                    t = int(name[2])
                    vv = (sx, su)[t]
                    dve.wait_ge(pl_in, t + 1)
                    for r0, z in ((0, zs[0]), (DH, zs[1])):
                        rr = slice(r0, r0 + DH)
                        link(v.scalar_tensor_tensor(out=ply[rr, t, 16:S], in0=z[rr, 16:S],
                                                    scalar=t_("invw", t, 1)[rr, :], in1=vv[rr, 16:S],
                                                    op0=ALU.mult, op1=ALU.subtract))
                        link(v.tensor_tensor(ply[rr, t, 0:16], z[rr, 0:16], t_("invc", 16 * t, 16)[rr, :], ALU.mult))
                        ins = v.tensor_tensor(ply[rr, t, 0:16], ply[rr, t, 0:16], vv[rr, 0:16], ALU.subtract)
                        if r0:
                            ins.then_inc(pl_done, 1)
                        else:
                            link(ins)
                elif name[0] == "u":
                    e, n = (int(w) for w in name[1:].split("_"))
                    wait_tile(dve, g)
                    if UPS * e + n >= 2:
                        dve.wait_ge(u_lo, UPS * e + n - 1)
                    t = tbuf[n % 2]
                    v.tensor_scalar(t[:], slot[g % 2][:], 0.0, None, ALU.max).then_inc(slot_free[g % 2], 1)
                    wait_evacuated(dve, name)
                    v.tensor_tensor(t[:], t[:], t[:], ALU.mult).then_inc(u_src, 1)
                elif name[0] == "d":
                    e, m = (int(w) for w in name[1:].split("_"))
                    for t in range(2):
                        n, gg = 2 * m + t, g + t
                        if e:
                            wait_tile(dve, gg)
                            if e == 1:
                                wait_evacuated(dve, "d0_%d" % m, t)
                            v.tensor_tensor(mm[:, n, :], slot[gg % 2][:], mm[:, n, :], ALU.add
                                            ).then_inc(slot_free[gg % 2], 1)
                elif name[0] == "g":
                    n = int(name[1])
                    wait_tile(dve, g + 1)
                    wait_evacuated(dve, name)
                    if n == 0:
                        wait_all_split(dve, 5)
                    v.tensor_tensor(mm[:, n, :], slot[(g + 1) % 2][:], zs2[n % 2][:], ALU.mult
                                    ).then_inc(slot_free[(g + 1) % 2], 1)

            def turn(name):
                g, t = TILE["turned " + name], int(name[2])
                wait_tile(dve, g)
                if name[1] == "v":
                    dst = (dv if name[0] == "D" else brv)[:, t, :, :].rearrange("p b n -> p (b n)")
                    ins = v.tensor_copy(dst, slot[g % 2][:])
                elif name[1] == "t":
                    dve.wait_ge(rtab_in, 16)
                    ins = v.tensor_tensor(dt_[:, t, :, :], slot[g % 2][:].rearrange("p (b n) -> p b n", b=NB),
                                          zt[:, t, :].unsqueeze(1).to_broadcast([P, NB, P]), ALU.mult)
                else:
                    ins = v.tensor_copy(flat(gates), slot[g % 2][:, 0:NB * NGATE])
                ins.then_inc(slot_free[g % 2], 1)

            def split_wide(v_, pos, k, src):
                if pos % 2 == 0:
                    dve.wait_ge(x_hi, 8 * v_ + pos + 1)
                    v.tensor_tensor(xlo[:, k, :], src, xhi[:, k, :].bitcast(F32), ALU.subtract).then_inc(x_lo2, 1)

            def soft(u, first, count):
                if u < first + count:
                    ph, h, i, lo, nb = unit(u)
                    w = nb * P
                    dve.wait_ge(s_scores, u + 1)
                    if u >= 3:
                        dve.wait_ge(s_pt, BATCH_END[u - 3])
                    if ph == "FGT":
                        dve.wait_ge(f_cb, h + 1)
                        v.scalar_tensor_tensor(out=sring[u % 3][:, 0:w], in0=ps4[:, 0:w], scalar=ci[:, i, h:h + 1],
                                               in1=cb[:, 0:w], op0=ALU.add, op1=ALU.subtract).then_inc(s_biased, 1)
                    else:
                        o = (NB - 1 - i + lo) * P
                        v.scalar_tensor_tensor(out=sring[u % 3][:, 0:w], in0=t_("dist", o, w), scalar=SLOPES[h],
                                               in1=ps4[:, 0:w], op0=ALU.mult, op1=ALU.add).then_inc(s_biased, 1)
                    dve.wait_ge(s_biased, u + 1)
                    nm = nmx[:, u % 4:u % 4 + 1]
                    ins = v.tensor_reduce(nm, sring[u % 3][:, 0:w], AX, ALU.max, negate=True)
                    if ph == "SWA":
                        link(ins)
                        ins = v.tensor_tensor(nm, nm, nsink[:, h:h + 1], ALU.min)
                    ins.then_inc(s_negmax, 1)
                m = u - 3
                if first <= m < first + count:
                    ph, h, i, lo, nb = unit(m)
                    dve.wait_ge(s_out, m + 1)
                    d, f = den[:, m % 4:m % 4 + 1], fac[:, m % 4:m % 4 + 1]
                    if ph == "SWA":
                        link(v.tensor_tensor(d, d, esk[:, m % 4:m % 4 + 1], ALU.add))
                    link(v.tensor_scalar(d, d, TINY, None, ALU.max))
                    link(v.reciprocal(f, d))
                    y = ytok[:, i, h * DH:(h + 1) * DH]
                    o = ps7[:, 0:DH]
                    if ph in ("SEL", "WIN"):
                        gi = 3 * h + (1 if ph == "SEL" else 2)
                        link(v.tensor_tensor(f, f, gates[:, i, gi:gi + 1], ALU.mult))
                        v.scalar_tensor_tensor(out=y, in0=o, scalar=f, in1=y, op0=ALU.mult, op1=ALU.add
                                               ).then_inc(s_norm, 1)
                    else:
                        if m == first:
                            wait_tile(dve, TILE["yD1" if ph == "SWA" else "yA1"])
                        v.tensor_scalar(y, o, f, None, ALU.mult).then_inc(s_norm, 1)

            def stick(s):
                if s < NSTICK:
                    c0 = stick_q0(s)
                    dve.wait_ge(k_z, s + 1)
                    if s >= 4:
                        dve.wait_ge(k_r, s - 3)
                        dve.wait_ge(k_sum, s - 3)
                    v.tensor_scalar(skt[s % 4][:, c0:HALF].bitcast(I32), skz[s % 3][:, c0:HALF].bitcast(I32),
                                    0x7FFFFFFF, None, ALU.bitwise_and).then_inc(k_abs, 1)
                if 1 <= s <= NSTICK:
                    m = s - 1
                    c0 = stick_q0(m)
                    t = skt[m % 4]
                    dve.wait_ge(k_log, m + 1)
                    ins = v.scalar_tensor_tensor(out=t[:, c0:HALF], in0=skz[m % 3][:, c0:HALF], scalar=0.0,
                                                 in1=t[:, c0:HALF], op0=ALU.max, op1=ALU.add)
                    if STICK_DIAG[m]:
                        link(ins)
                        ins = v.tensor_tensor(t[:, c0:c0 + P], t[:, c0:c0 + P], t_("strict"), ALU.mult)
                    ins.then_inc(k_sp, 1)
                if s >= 3 and STICK[s - 3][1:] == (1, 0):
                    h = STICK[s - 3][0]
                    dve.wait_ge(k_o, s - 2)
                    if h == 0:
                        wait_tile(dve, TILE["yB1"])
                    v.tensor_copy(ytok[:, :, h * DH:(h + 1) * DH],
                                  ps7[:].rearrange("p (b d) -> p b d", b=NB)).then_inc(k_y, 1)

            def retention(n):
                if n < NB:
                    dve.wait_ge(r_s, n + 1)
                    if n == 0:
                        dve.wait_ge(rtab_in, 16)
                    if n >= 2:
                        dve.wait_ge(r_o, n - 1)
                    v.tensor_tensor(sbuf[n % 2][:, 0:HALF], psb[n % 2], dtab, ALU.mult).then_inc(r_st, 1)
                    if n < NB - 1:
                        for t in range(2):
                            u = ps6[:, t * DH:(t + 1) * DH]
                            if n == 0:
                                ins = v.tensor_copy(rst[:, 1, t, :], u)
                            else:
                                if t == 0:
                                    dve.wait_ge(r_state, n)
                                ins = v.scalar_tensor_tensor(out=rst[:, n + 1, t, :], in0=rst[:, n, t, :],
                                                             scalar=t_("gc", t, 1), in1=u,
                                                             op0=ALU.mult, op1=ALU.add)
                            if t == 0:
                                link(ins)
                            else:
                                ins.then_inc(r_state, 1)
                if n >= 1:
                    m = n - 1
                    dve.wait_ge(r_o, m + 1)
                    v.tensor_copy(ytok[:, m, :], ps7[:, 0:BW]).then_inc(r_y, 1)

            def retention_norm():
                y = ytok[:].rearrange("p b (h d) -> p (b h) d", h=H)
                sq = sq8[:].rearrange("p b (h d) -> p (b h) d", h=H)

                def wide_(a):
                    return a.unsqueeze(2).to_broadcast([P, 32, DH])

                dve.wait_ge(r_y, NB)
                link(v.tensor_reduce(st32[:, 0, :], y, AX, ALU.add))
                link(v.tensor_scalar(st32[:, 0, :], st32[:, 0, :], -1.0 / DH, None, ALU.mult))
                link(v.tensor_tensor(y, y, wide_(st32[:, 0, :]), ALU.add))
                link(v.tensor_tensor(sq, y, y, ALU.mult))
                v.tensor_reduce(st32[:, 1, :], sq, AX, ALU.add).then_inc(r_var, 1)
                dve.wait_ge(r_sq, 1)
                link(v.reciprocal(st32[:, 3, :], st32[:, 2, :]))
                v.tensor_tensor(y, y, wide_(st32[:, 3, :]), ALU.mult).then_inc(ret_done, 1)

            def compress(s):
                if s == 0:
                    wait_evacuated(dve, "Acmp")
                    z = acmp[:].rearrange("p (c l) -> p c l", l=32)
                    v.tensor_tensor(z, z, v_("pos").unsqueeze(1).to_broadcast([P, NCMP, 32]), ALU.add
                                    ).then_inc(c_pos, 1)
                elif s == 2:
                    s3 = sbuf[0][:].rearrange("p (u c) -> p u c", c=NCMP)

                    def wide_(a):
                        return a.unsqueeze(2).to_broadcast([P, 32, NCMP])

                    dve.wait_ge(c_s, 1)
                    w = NB * NCMP
                    for h in range(H):
                        link(v.scalar_tensor_tensor(out=sbuf[0][:, h * w:(h + 1) * w], in0=t_("cdist"),
                                                    scalar=SLOPES[h], in1=ps4[:, h * w:(h + 1) * w],
                                                    op0=ALU.mult, op1=ALU.add))
                    link(v.tensor_reduce(st32[:, 0, :], s3, AX, ALU.max, negate=True))
                    v.tensor_tensor(s3, s3, wide_(st32[:, 0, :]), ALU.add).then_inc(c_sb, 1)
                    dve.wait_ge(c_e, 1)
                    s4 = sbuf[0][:].rearrange("p (h w) -> p h w", h=H)
                    link(v.tensor_tensor(s4, s4, t_("cmask").unsqueeze(1).to_broadcast([P, H, w]), ALU.mult))
                    link(v.tensor_reduce(st32[:, 1, :], s3, AX, ALU.add))
                    link(v.tensor_scalar(st32[:, 1, :], st32[:, 1, :], TINY, None, ALU.max))
                    link(v.reciprocal(st32[:, 2, :], st32[:, 1, :]))
                    v.tensor_tensor(s3, s3, wide_(st32[:, 2, :]), ALU.mult).then_inc(c_p, 1)
                elif s == 4:
                    wait_evacuated(dve, "turned Ag1")
                    wait_tile(dve, TILE["yC1"])
                    for h in range(H):
                        dve.wait_ge(c_o, h + 1)
                        v.tensor_tensor(ytok[:, :, h * DH:(h + 1) * DH], ps7[:].rearrange("p (b d) -> p b d", b=NB),
                                        gates[:, :, 3 * h:3 * h + 1].to_broadcast([P, NB, DH]), ALU.mult
                                        ).then_inc(c_y, 1)

            dve.wait_ge(small_in, 32)
            link(v.tensor_copy(identb[:], t_("ident")))
            link(v.tensor_copy(upb[:], t_("up")))
            link(v.tensor_copy(lowb[:], t_("low")))
            link(v.memset(fac[:], 1.0))
            v.tensor_scalar(nsink[:], v_("sink"), -1.0, None, ALU.mult).then_inc(masks_done, 1)

            def ada_products(t, tiles):
                for kc, parts in enumerate(tiles):
                    for cols, src, loaded in parts:
                        dve.wait_ge(ada_in[t][loaded], 16)
                        dst = ada_sum[t][:, cols]
                        if kc == 0:
                            ins = v.tensor_scalar(dst, src, csil[:, 0:1], None, ALU.mult)
                        else:
                            ins = v.scalar_tensor_tensor(out=dst, in0=src, scalar=csil[:, kc:kc + 1], in1=dst,
                                                         op0=ALU.mult, op1=ALU.add)
                        if kc == 7 and (cols.stop == D):
                            ins.then_inc(ada_acc, 1)
                        else:
                            link(ins)

            dve.wait_ge(csil_done, 1)
            for t, a in ((1, ada1), (0, ada0)):
                ada_products(t, [[(slice(0, D), a[:, kc, :], kc // 4)] for kc in range(8)])
            dve.wait_ge(mod_mm, 1)
            link(v.tensor_tensor(fgp[:], v_("final_g"), v_("g_mix_pre"), ALU.mult))
            link(v.tensor_tensor(mod[:, 0:16], ps6[:, 0:16], v_("b_ada", 0, 16), ALU.add))
            link(v.tensor_scalar(gmul[:], mod[:, 8:16], 1.0, None, ALU.add))
            v.tensor_tensor(gmul[:], gmul[:], v_("norm_g"), ALU.mult).then_inc(mod_done, 1)

            for ev in TIMELINE:
                if ev[0] == "dense":
                    if last_part(ev):
                        evacuate(ev[1])
                elif ev[0] == "ytrans":
                    br, n = ev[1], ev[2]
                    g = TILE["y%s%d" % (br, n)]
                    wait_tile(dve, g)
                    wait_evacuated(dve, "%sz%d" % (br, n))
                    v.tensor_tensor(zs[n][:], slot[g % 2][:], zs[n][:], ALU.mult).then_inc(slot_free[g % 2], 1)
                elif ev[0] == "turn":
                    turn(ev[1])
                elif ev[0] == "gate_mod":
                    ada_products(2, [[(slice(half * HALF, (half + 1) * HALF), ada2[half][:, kc, :], half)
                                      for half in range(2)] for kc in range(8)])
                    dve.wait_ge(mod_mm, 2)
                    v.tensor_tensor(mod[:, 16:24], ps6[:, 16:24], v_("b_ada", 16, 8), ALU.add).then_inc(mod_done, 1)
                elif ev[0] == "ret":
                    retention(ev[1])
                elif ev[0] == "retnorm":
                    retention_norm()
                elif ev[0] == "ksplit":
                    u = ev[1]
                    dve.wait_ge(kh_done, KSPLITS.index(u) + 1)
                    v.tensor_tensor(brkl[:, KTILE[u], :], brk[:, KTILE[u], :],
                                    (khif if u >= U_FGT else khi)[:].bitcast(F32), ALU.subtract
                                    ).then_inc(kl_done, 1)
                elif ev[0] == "soft":
                    soft(ev[1], ev[2], ev[3])
                elif ev[0] == "stick":
                    stick(ev[1])
                elif ev[0] == "cmp":
                    compress(ev[1])
                elif ev[0] == "conv":
                    t, k = ev[1], ev[2]
                    w = v_("dw", 31 * t + k, 1)
                    sh = 30 - k
                    if k == 0:
                        wait_evacuated(dve, "Eca%d" % t)
                        link(v.tensor_scalar(cacc[:, t, :], cu[:, t, :], v_("dw", 31 * t + 30, 1), None, ALU.mult))
                    if k < 30:
                        ins = v.scalar_tensor_tensor(out=cacc[:, t, sh:S], in0=cu[:, t, 0:S - sh], scalar=w,
                                                     in1=cacc[:, t, sh:S], op0=ALU.mult, op1=ALU.add)
                        if k < 29:
                            link(ins)
                        else:
                            ins.then_inc(conf_done, 1)
                elif ev[0] == "norm1":
                    rstd(0)
                    dve.wait_ge(mod_done, 1)
                    for n in range(NC + 1):
                        if n < NC:
                            link(v.scalar_tensor_tensor(out=mm[:, n, :], in0=mm[:, n, :], scalar=gmul[:, n:n + 1],
                                                        in1=pbuf[1][:], op0=ALU.mult, op1=ALU.mult))
                            v.tensor_scalar(mm[:, n, :], mm[:, n, :], mod[:, n:n + 1], None, ALU.add
                                            ).then_inc(x_src, 1)
                        if n:
                            split_wide(0, n - 1, n - 1, mm[:, n - 1, :])
                    applied(0, x_src, 8)
                elif ev[0] == "split_merged":
                    for n in range(NC):
                        split_wide(1, n, n, mm[:, n, :])
                elif ev[0] == "norm2":
                    rstd(1)
                    dve.wait_ge(nsum, 3)
                    link(v.tensor_tensor(pbuf[0][:], ps4[:], pbuf[1][:], ALU.mult))
                    v.tensor_tensor(pbuf[0][:], pbuf[0][:], pbuf[1][:], ALU.mult).then_inc(n2_t, 1)
                    dve.wait_ge(nstd, 3)
                    link(v.reciprocal(pbuf[0][:], pbuf[0][:]))
                    link(v.tensor_tensor(pbuf[0][:], pbuf[0][:], pbuf[1][:], ALU.mult))
                    for n in range(NC + 1):
                        if n < NC:
                            v.scalar_tensor_tensor(out=res[:, n, :], in0=mm[:, n, :], scalar=fgp[:, n:n + 1],
                                                   in1=pbuf[0][:], op0=ALU.mult, op1=ALU.mult).then_inc(x_src, 1)
                        if n:
                            split_wide(2, n - 1, n - 1, res[:, n - 1, :])
                    for n in range(NC):
                        scaled(mm[:, n, :], mm[:, n, :], v_("final_g", n, 1), chunk_ready)
                    applied(1, chunk_ready, 8)
                    applied(2, x_src, 16)
                    dve.wait_ge(res_out, 16 * NC)
                elif ev[0] in ("norm3", "norm4"):
                    k = 3 if ev[0] == "norm3" else 5
                    post, pre = ("g_mix_post", "g_mlp_pre") if k == 3 else ("g_mlp_post", "g_ple_pre")
                    add_residual(k, (k - 3) // 2, post)
                    applied(k, t_ready, 8 * (k - 1) // 2)
                    rstd(k + 1)
                    for n in range(NC + 1):
                        if n < NC:
                            wait_residual(dve, (k - 3) // 2, n)
                            scaled(mm[:, n, :], res[:, n, :], v_(pre, n, 1), x_src)
                        if n:
                            split_wide(4 if k == 3 else 5, n - 1, n - 1, mm[:, n - 1, :])
                    applied(k + 1, x_src, 24 + 4 * (k - 3))
                elif ev[0] == "norm5":
                    add_residual(7, 2, "g_ple_post")
                elif ev[0] == "mix":
                    split_wide(3, 0, 4, scy[:, 0, :])
                    dve.wait_ge(s_norm, 128)
                    for t in range(2):
                        g = TILE["yE%d" % t]
                        wait_tile(dve, g)
                        v.tensor_copy(pbuf[t][:], slot[g % 2][:]).then_inc(slot_free[g % 2], 1)
                        wait_evacuated(dve, "yE%d" % t)
                        v.tensor_copy(fac[:, 0:1], fac[:, 1:2]).then_inc(mix_src, 1)
                    split_wide(3, 2, 2, pbuf[0][:])
                    for t in range(2):
                        dve.wait_ge(m_pool, t + 1)
                        v.tensor_scalar(ply[:, t, :], ps4[:], v_("pool_scale", t, 1), None, ALU.mult
                                        ).then_inc(m_pool_in, 1)
                        dve.wait_ge(m_pool_in, t + 1)
                        v.tensor_copy(fac[:, 0:1], fac[:, 1:2]).then_inc(mix_src, 1)
                    split_wide(3, 4, 6, ply[:, 0, :])
                    dve.wait_ge(m_mean, 1)
                    for t in range(2):
                        v.scalar_tensor_tensor(out=cacc[:, t, :], in0=ps4[:], scalar=-1.0 / BW, in1=cacc[:, t, :],
                                               op0=ALU.mult, op1=ALU.add).then_inc(m_cent, 1)
                    dve.wait_ge(m_std, 1)
                    link(v.reciprocal(sx[:], sx[:]))
                    for t in range(2):
                        v.tensor_tensor(cacc[:, t, :], cacc[:, t, :], sx[:], ALU.mult).then_inc(m_hat, 1)
                    for t in range(2):
                        dve.wait_ge(m_pw, t + 1)
                        v.tensor_copy(cu[:, t, :], ps4[:]).then_inc(m_pw_in, 1)
                        dve.wait_ge(m_pw_in, t + 1)
                        v.tensor_copy(fac[:, 0:1], fac[:, 1:2]).then_inc(mix_src, 1)
                    split_wide(3, 6, 0, cu[:, 0, :])


def tables():
    t = np.zeros((P, NTABLE), np.float32)
    p = np.arange(P)[:, None]

    def put(name, value):
        o, w = TABLES[name]
        t[:, o:o + w] = value

    j = np.arange(S)[None, :]
    rel = j - p - (S - P)
    put("dist", np.where(rel <= 0, rel, -1e32))
    c = np.arange(P)[None, :]
    put("ident", p == c)
    put("strict", p < c)
    put("tri", np.where(p >= c, -1.0, 0.0))
    put("negones", -1.0)
    put("ones", 1.0)
    put("up", np.where(c > p, NEG, 0.0))
    put("low", np.where(c > p, 0.0, NEG))
    i = np.arange(NB * NCMP)[None, :]
    dist = (i // NCMP) * P + p - 32 * (i % NCMP) - 31
    put("cdist", np.where(dist >= 0, -dist, -1e32))
    put("cmask", dist >= 0)
    lg = np.log(1.0 - 2.0 ** (-5.0 - np.arange(H)))
    head = np.arange(2)[None, :] * 2 + p // DH
    put("gc", np.exp(lg[head] * P))
    put("eps6", 1e-6)
    put("eps5", 1e-5)
    win = np.array([2.0, 4.0, 8.0, 16.0])[head]
    put("invw", 1.0 / win)
    tok = np.arange(16)[None, None, :]
    put("invc", (1.0 / np.minimum(tok + 1, win[:, :, None])).reshape(P, 32))
    r = np.zeros((P, RET_TABLE), np.float32)
    d = c - p
    r[:, 0:4 * P] = np.concatenate([np.where(d >= 0, np.exp(lg[h] * np.maximum(d, 0)), 0.0) for h in range(H)], 1)
    r[:, 4 * P:6 * P] = np.exp(lg[head][:, :, None] * (np.arange(P)[None, None, :] + 1)).reshape(P, 2 * P)
    f = np.arange(2 * P)[None, :]
    r[:, 6 * P:8 * P] = np.exp(lg[f // DH] * (P - 1 - p))
    return t, r


def pack_weights(inp):
    w1, w2 = inp["w_in"][0], inp["w_in_2"][0]
    wm, wb, wo = inp["w_merge"][0], inp["w_br"][0], inp["w_out"][0]
    bi = {"A": 0, "B": 1, "C": 2, "D": 3}
    start = {"Aq": 0, "Acmp": 256, "Az": 652, "Bq": 908, "Bv": 1292, "Bz": 1420,
             "Cq": 1676, "Ck": 1932, "Cv": 2188, "Cz": 2444, "Dq": 2700, "Dk": 2956, "Dt": 2956, "Dv": 3212,
             "Dz": 3468, "Eca": 0, "Ecb": 256, "Eq": 512, "Ek": 768, "Ev": 1024, "Ef": 1280, "Esh": 1284,
             "Esb": 1540, "Esc": 1796, "Ep": 2052}

    def chunks(w):
        return np.asarray(w).reshape(-1, P, w.shape[1]).transpose(1, 0, 2).reshape(P, -1)

    def twice(w):
        return np.concatenate([w, w], 1)

    out = []
    for kind, name in BLOCKS:
        if name == "Ak0":
            blk = chunks(twice(w1[:, 384:448]))
        elif name == "Ak1":
            blk = chunks(twice(w1[:, 512:576]))
        elif name == "Av0":
            blk = chunks(np.concatenate([w1[:, 448:512], w1[:, 576:640]], 1))
        elif name == "Ag1":
            blk = chunks(w1[:, 640:640 + P])
        elif name in ("Bk0", "Bk1"):
            o = 1164 + DH * int(name[2])
            blk = chunks(twice(w1[:, o:o + DH]))
        elif kind == "M":
            m = int(name[-1])
            cols = slice(m * P, (m + 1) * P)
            if name[0] == "g":
                blk = np.concatenate([chunks(inp["w_ple_gate_2"][0][:, cols]),
                                      chunks(inp["w_ple_proj_2"][0][:, cols])], 1)
            else:
                blk = np.concatenate([chunks(wm[bi[name[0]]][:, cols]), chunks(wb[bi[name[0]]][:, cols])], 1)
        elif name[0] in "ox":
            m = int(name[1])
            blk = chunks((wo if name[0] == "o" else inp["w_out_2"][0])[:, m * P:(m + 1) * P])
        elif name[0] == "u":
            e, m = (int(x) for x in name[1:].split("_"))
            o = (UPS * e + m) * P
            blk = chunks(inp["w_up_2"][0][:, o:o + P])
        elif name[0] == "d":
            e, m = (int(x) for x in name[1:].split("_"))
            blk = chunks(inp["w_down_2"][0][UPS * P * e:UPS * P * (e + 1), 2 * P * m:2 * P * (m + 1)])
        else:
            w = w2 if name[0] == "E" else w1
            key = name.rstrip("0123456789")
            o = start[key] + P * int(name[len(key):] or 0)
            blk = chunks(w[:, o:o + P])
        out.append(blk.ravel())
    return np.concatenate(out)


def pack_vectors(inp):
    v = np.zeros((P, NVEC), np.float32)

    def put(name, value):
        o, w = VECS[name]
        v[:, o:o + w] = value

    def cols(a):
        return np.asarray(a).reshape(-1, P).T

    put("c", cols(inp["c"][0]))
    put("b_ada", cols(inp["b_ada"][0]))
    put("norm_g", cols(inp["norm_g"][0]))
    put("final_g", cols(inp["final_g"]))
    for n in ("g_mix_pre", "g_mix_post", "g_mlp_pre", "g_mlp_post", "g_ple_pre", "g_ple_post"):
        put(n, cols(inp[n + "_2"][0]))
    dw, sc = np.asarray(inp["w_conf_dw_2"][0]), np.asarray(inp["w_sc_2"][0])
    put("dw", np.concatenate([dw[:, 0:P].T, dw[:, P:].T], 1))
    put("sc", np.concatenate([sc[:, 0:P].T, sc[:, P:].T], 1))
    put("ln_g", cols(inp["conf_ln_g_2"][0]))
    put("ln_b", cols(inp["conf_ln_b_2"][0]))
    put("pool_scale", cols(inp["pool_scale_2"][0]))
    put("sink", np.broadcast_to(inp["sink"][0], (P, H)))
    o, _ = VECS["bf"]
    v[0:H, o] = inp["b_forget_2"][0]
    pos = np.asarray(inp["cmp_pos"][0])
    put("pos", pos.transpose(0, 2, 1).reshape(P, 32))
    return v


def kernel(**inputs):
    import concourse.bacc as _bacc
    from concourse.bass_utils import run_bass_kernel_spmd as _run

    inp = {k: np.asarray(a) for k, a in inputs.items()}
    tab, rtab = tables()
    w1, w2 = inp["cmp_w1"][0], inp["cmp_w2"][0]
    wp = np.zeros((P, 2, P), np.float32)
    for g in range(4):
        r = DH * (g % 2)
        wp[r:r + DH, g // 2, r:r + DH] = inp["w_pool_2"][0, g]
    arrays = {
        "xT": inp["x"][0].T.reshape(NC, P, S).transpose(1, 0, 2),
        "pT": inp["p_2"][0, 0].T.reshape(2, P, S).transpose(1, 0, 2),
        "wstream": pack_weights(inp),
        "wada": inp["w_ada"][0].reshape(8, P, 3, D).transpose(2, 1, 0, 3),
        "vecs": pack_vectors(inp),
        "tables": tab,
        "rtables": rtab,
        "cw1": w1.reshape(2, 32, DH, DH).transpose(0, 2, 1, 3).reshape(P, 32, DH),
        "cw2": np.concatenate([w2[0], w2[0], w2[1]], 1),
        "wpw": inp["w_conf_pw_2"][0].reshape(2, P, BW).transpose(1, 0, 2),
        "wpool": wp,
    }
    arrays = {k: np.ascontiguousarray(a) for k, a in arrays.items()}
    nc = _bacc.Bacc("TRN2", target_bir_lowering=False, num_devices=1)
    args = [nc.dram_tensor(k, a.shape, F32, kind="ExternalInput").ap() for k, a in arrays.items()]
    args.append(nc.dram_tensor("outT", (P, NC, S), F32, kind="ExternalOutput").ap())
    build(nc, *args)
    r = _run(nc, [arrays], core_ids=[0])
    o = r.results[0]["outT"]
    return o.transpose(1, 0, 2).reshape(D, S).T.reshape(1, S, D)
```
